# Optimizing a Trainium2 kernel written in Bass

```python
import math
import numpy as np
import jax
import jax.numpy as jnp
from jax import lax
import jax, jax.numpy as jnp

D_MODEL = 1024
BATCH = 1
SEQ = 512
DEPTH = 1

HEAD_DIM = 64
N_HEADS_NSA = 8
N_KV_NSA = 2
GROUP_NSA = N_HEADS_NSA // N_KV_NSA
N_HEADS_FOX = 8
MIX_WIDTH = (N_HEADS_NSA + N_HEADS_FOX) * HEAD_DIM
NSA_Q_W = N_HEADS_NSA * HEAD_DIM
NSA_KV_W = N_KV_NSA * HEAD_DIM
FOX_W = N_HEADS_FOX * HEAD_DIM
PROJ_SIZES = (NSA_Q_W, NSA_KV_W, NSA_KV_W, NSA_KV_W, NSA_KV_W, NSA_KV_W, NSA_KV_W,
              3 * N_HEADS_NSA, FOX_W, FOX_W, FOX_W, N_HEADS_FOX)
IN_WIDTH = sum(PROJ_SIZES)
D_FF = 2816
D_PLE = 256
ROPE_THETA = 500000.0
ROT_DIM = HEAD_DIM // 4
CMP_BLOCK = 32
CMP_STRIDE = 16
CMP_HIDDEN = 256
SEL_BLOCK = 64
SEL_TOPK = 16
WINDOW = 512
NSA_Q_BLOCK = 32
FOX_Q_BLOCK = 128
FORCED_SCORE = 1e6
EPS = 1e-6
NEG = -1e30


def rmsnorm(x, g):
    xf = x.astype(jnp.float32)
    y = xf * lax.rsqrt(jnp.mean(xf * xf, axis=-1, keepdims=True) + EPS)
    return (y * g.astype(jnp.float32)).astype(x.dtype)

def swiglu(x, wg, wu, wd):
    return (jax.nn.silu(x @ wg) * (x @ wu)) @ wd

def split_heads(t, n):
    b, s, _ = t.shape
    return t.reshape(b, s, n, HEAD_DIM).transpose(0, 2, 1, 3)

def merge_heads(t):
    b, n, s, d = t.shape
    return t.transpose(0, 2, 1, 3).reshape(b, s, n * d)

def rope_tables(seq):
    pos = jnp.arange(seq, dtype=jnp.float32)
    inv = ROPE_THETA ** (-jnp.arange(0, ROT_DIM, 2, dtype=jnp.float32) / ROT_DIM)
    ang = pos[:, None] * inv[None, :]
    return jnp.cos(ang), jnp.sin(ang)

def partial_rope(x, cos, sin):
    half = ROT_DIM // 2
    xf = x.astype(jnp.float32)
    x1, x2, rest = xf[..., :half], xf[..., half:ROT_DIM], xf[..., ROT_DIM:]
    out = jnp.concatenate([x1 * cos - x2 * sin, x2 * cos + x1 * sin, rest], axis=-1)
    return out.astype(x.dtype)

def masked_softmax(s, mask):
    return jax.nn.softmax(jnp.where(mask, s.astype(jnp.float32), NEG), axis=-1)

def compress_blocks(tok, pos_emb, w1, w2):
    s = tok.shape[2]
    n_cmp = (s - CMP_BLOCK) // CMP_STRIDE + 1
    idx = np.arange(n_cmp)[:, None] * CMP_STRIDE + np.arange(CMP_BLOCK)[None, :]
    blk = tok[:, :, idx, :] + pos_emb
    blk = blk.reshape(blk.shape[0], blk.shape[1], n_cmp, CMP_BLOCK * HEAD_DIM)
    return jax.nn.silu(blk @ w1) @ w2

def nsa_attention(q, k_cmp, v_cmp, k_slc, v_slc, k_win, v_win, gates):
    b, h, s, d = q.shape
    qg = q.reshape(b, N_KV_NSA, GROUP_NSA, s, d)
    gg_all = gates.reshape(b, N_KV_NSA, GROUP_NSA, s, 3)
    n_cmp = k_cmp.shape[2]
    n_sel = s // SEL_BLOCK
    top = min(SEL_TOPK, n_sel)
    cmp_start = np.arange(n_cmp) * CMP_STRIDE
    cmp_end = jnp.asarray(cmp_start + CMP_BLOCK - 1)
    sel_start = np.arange(n_sel) * SEL_BLOCK
    overlap = jnp.asarray(((cmp_start[:, None] <= sel_start[None, :] + SEL_BLOCK - 1)
                           & (cmp_start[:, None] + CMP_BLOCK - 1 >= sel_start[None, :])).astype(np.float32))
    ks_blocks = k_slc.reshape(b, N_KV_NSA, n_sel, SEL_BLOCK, d)
    vs_blocks = v_slc.reshape(b, N_KV_NSA, n_sel, SEL_BLOCK, d)
    pad = ((0, 0), (0, 0), (WINDOW, 0), (0, 0))
    kw_pad = jnp.pad(k_win, pad)
    vw_pad = jnp.pad(v_win, pad)
    bi = np.arange(b)[:, None, None, None]
    hi = np.arange(N_KV_NSA)[None, :, None, None]
    blk_j = jnp.arange(n_sel)
    scale = HEAD_DIM ** -0.5
    qn = NSA_Q_BLOCK

    def block(qb):
        t0 = qb * qn
        tpos = t0 + jnp.arange(qn)
        qq = lax.dynamic_slice_in_dim(qg, t0, qn, axis=3)
        gg = lax.dynamic_slice_in_dim(gg_all, t0, qn, axis=3)
        m_c = cmp_end[None, :] <= tpos[:, None]
        s_c = jnp.einsum('bkgqd,bknd->bkgqn', qq, k_cmp) * scale
        p_c = masked_softmax(s_c, m_c) * m_c
        o_c = jnp.einsum('bkgqn,bknd->bkgqd', p_c.astype(v_cmp.dtype), v_cmp)
        imp = jnp.einsum('bkgqn,nj->bkqj', p_c, overlap)
        cur = tpos // SEL_BLOCK
        valid = blk_j[None, :] <= cur[:, None]
        forced = (blk_j[None, :] == 0) | (blk_j[None, :] == cur[:, None]) | (blk_j[None, :] == cur[:, None] - 1)
        imp = jnp.where(valid, jnp.where(forced, FORCED_SCORE, imp), -1.0)
        vals, sel = lax.top_k(imp, top)
        kg = ks_blocks[bi, hi, sel].reshape(b, N_KV_NSA, qn, top * SEL_BLOCK, d)
        vg = vs_blocks[bi, hi, sel].reshape(b, N_KV_NSA, qn, top * SEL_BLOCK, d)
        kpos = (sel[..., None] * SEL_BLOCK + jnp.arange(SEL_BLOCK)).reshape(b, N_KV_NSA, qn, top * SEL_BLOCK)
        m_s = (kpos <= tpos[:, None]) & jnp.repeat(vals >= 0, SEL_BLOCK, axis=-1)
        s_s = jnp.einsum('bkgqd,bkqnd->bkgqn', qq, kg) * scale
        p_s = masked_softmax(s_s, m_s[:, :, None])
        o_s = jnp.einsum('bkgqn,bkqnd->bkgqd', p_s.astype(vg.dtype), vg)
        kw = lax.dynamic_slice_in_dim(kw_pad, t0, qn + WINDOW, axis=2)
        vw = lax.dynamic_slice_in_dim(vw_pad, t0, qn + WINDOW, axis=2)
        kpos_w = t0 - WINDOW + jnp.arange(qn + WINDOW)
        diff = tpos[:, None] - kpos_w[None, :]
        m_w = (kpos_w[None, :] >= 0) & (diff >= 0) & (diff < WINDOW)
        s_w = jnp.einsum('bkgqd,bknd->bkgqn', qq, kw) * scale
        p_w = masked_softmax(s_w, m_w)
        o_w = jnp.einsum('bkgqn,bknd->bkgqd', p_w.astype(vw.dtype), vw)
        return gg[..., 0:1] * o_c + gg[..., 1:2] * o_s + gg[..., 2:3] * o_w

    out = lax.map(block, jnp.arange(s // qn))
    return jnp.moveaxis(out, 0, 3).reshape(b, h, s, d)

def forgetting_attention(q, k, v, log_f):
    b, h, s, d = q.shape
    c = jnp.cumsum(log_f, axis=-1)
    kpos = jnp.arange(s)
    scale = HEAD_DIM ** -0.5
    qn = FOX_Q_BLOCK

    def block(qb):
        t0 = qb * qn
        tpos = t0 + jnp.arange(qn)
        qq = lax.dynamic_slice_in_dim(q, t0, qn, axis=2)
        cq = lax.dynamic_slice_in_dim(c, t0, qn, axis=2)
        logits = (jnp.einsum('bhqd,bhsd->bhqs', qq, k).astype(jnp.float32) * scale
                  + cq[..., :, None] - c[:, :, None, :])
        p = masked_softmax(logits, kpos[None, :] <= tpos[:, None])
        return jnp.einsum('bhqs,bhsd->bhqd', p.astype(v.dtype), v)

    out = lax.map(block, jnp.arange(s // qn))
    return jnp.moveaxis(out, 0, 2).reshape(b, h, s, d)

def first_inputs(seed: int = 0) -> dict:
    key = jax.random.key(seed)
    ks = iter(jax.random.split(key, 40))
    nrm = lambda shape, sc: jax.random.normal(next(ks), shape, jnp.float32) * sc
    gain = lambda n: 1.0 + nrm((DEPTH, n), 0.05)
    L = DEPTH
    return {
        'x': nrm((BATCH, SEQ, D_MODEL), 1.0),
        'p': nrm((DEPTH, BATCH, SEQ, D_PLE), 1.0),
        'ffn1_norm': gain(D_MODEL),
        'ffn1_wg': nrm((L, D_MODEL, D_FF), D_MODEL ** -0.5),
        'ffn1_wu': nrm((L, D_MODEL, D_FF), D_MODEL ** -0.5),
        'ffn1_wd': nrm((L, D_FF, D_MODEL), D_FF ** -0.5),
        'mix_norm': gain(D_MODEL),
        'w_in': nrm((L, D_MODEL, IN_WIDTH), D_MODEL ** -0.5),
        'b_forget': 4.0 + nrm((L, N_HEADS_FOX), 0.5),
        'q_norm_nsa': gain(HEAD_DIM),
        'k_norm_cmp': gain(HEAD_DIM),
        'k_norm_slc': gain(HEAD_DIM),
        'k_norm_win': gain(HEAD_DIM),
        'cmp_pos_k': nrm((L, CMP_BLOCK, HEAD_DIM), 0.02),
        'cmp_pos_v': nrm((L, CMP_BLOCK, HEAD_DIM), 0.02),
        'cmp_k_w1': nrm((L, CMP_BLOCK * HEAD_DIM, CMP_HIDDEN), (CMP_BLOCK * HEAD_DIM) ** -0.5),
        'cmp_k_w2': nrm((L, CMP_HIDDEN, HEAD_DIM), CMP_HIDDEN ** -0.5),
        'cmp_v_w1': nrm((L, CMP_BLOCK * HEAD_DIM, CMP_HIDDEN), (CMP_BLOCK * HEAD_DIM) ** -0.5),
        'cmp_v_w2': nrm((L, CMP_HIDDEN, HEAD_DIM), CMP_HIDDEN ** -0.5),
        'q_norm_fox': gain(HEAD_DIM),
        'k_norm_fox': gain(HEAD_DIM),
        'out_norm_nsa': gain(NSA_Q_W),
        'out_norm_fox': gain(FOX_W),
        'w_out': nrm((L, MIX_WIDTH, D_MODEL), MIX_WIDTH ** -0.5),
        'ffn2_norm': gain(D_MODEL),
        'ffn2_wg': nrm((L, D_MODEL, D_FF), D_MODEL ** -0.5),
        'ffn2_wu': nrm((L, D_MODEL, D_FF), D_MODEL ** -0.5),
        'ffn2_wd': nrm((L, D_FF, D_MODEL), D_FF ** -0.5),
        'ple_gate_norm': gain(D_MODEL),
        'ple_w_gate': nrm((L, D_MODEL, D_MODEL), D_MODEL ** -0.5),
        'ple_w_proj': nrm((L, D_PLE, D_MODEL), D_PLE ** -0.5),
        'ple_norm': gain(D_MODEL),
    }

def first_block(x, p, ffn1_norm, ffn1_wg, ffn1_wu, ffn1_wd, mix_norm, w_in, b_forget,
              q_norm_nsa, k_norm_cmp, k_norm_slc, k_norm_win, cmp_pos_k, cmp_pos_v,
              cmp_k_w1, cmp_k_w2, cmp_v_w1, cmp_v_w2, q_norm_fox, k_norm_fox,
              out_norm_nsa, out_norm_fox, w_out, ffn2_norm, ffn2_wg, ffn2_wu, ffn2_wd,
              ple_gate_norm, ple_w_gate, ple_w_proj, ple_norm):
    b, s, _ = x.shape
    cos, sin = rope_tables(s)
    split_points = [int(v) for v in np.cumsum(PROJ_SIZES)[:-1]]
    h = x
    for i in range(DEPTH):
        h = h + 0.5 * swiglu(rmsnorm(h, ffn1_norm[i]), ffn1_wg[i], ffn1_wu[i], ffn1_wd[i])
        a = rmsnorm(h, mix_norm[i])
        u = a @ w_in[i]
        (qa, kc, vc, ksl, vsl, kwn, vwn, ga, qf, kf, vf, fl) = jnp.split(u, split_points, axis=-1)
        q_a = partial_rope(rmsnorm(split_heads(qa, N_HEADS_NSA), q_norm_nsa[i]), cos, sin)
        kc_tok = partial_rope(split_heads(kc, N_KV_NSA), cos, sin)
        k_cmp = rmsnorm(compress_blocks(kc_tok, cmp_pos_k[i], cmp_k_w1[i], cmp_k_w2[i]), k_norm_cmp[i])
        v_cmp = compress_blocks(split_heads(vc, N_KV_NSA), cmp_pos_v[i], cmp_v_w1[i], cmp_v_w2[i])
        k_slc = partial_rope(rmsnorm(split_heads(ksl, N_KV_NSA), k_norm_slc[i]), cos, sin)
        k_win = partial_rope(rmsnorm(split_heads(kwn, N_KV_NSA), k_norm_win[i]), cos, sin)
        gates = jax.nn.sigmoid(ga).reshape(b, s, N_HEADS_NSA, 3).transpose(0, 2, 1, 3)
        o_a = nsa_attention(q_a, k_cmp, v_cmp, k_slc, split_heads(vsl, N_KV_NSA),
                            k_win, split_heads(vwn, N_KV_NSA), gates)
        q_b = rmsnorm(split_heads(qf, N_HEADS_FOX), q_norm_fox[i])
        k_b = rmsnorm(split_heads(kf, N_HEADS_FOX), k_norm_fox[i])
        log_f = jax.nn.log_sigmoid((fl + b_forget[i]).astype(jnp.float32)).transpose(0, 2, 1)
        o_b = forgetting_attention(q_b, k_b, split_heads(vf, N_HEADS_FOX), log_f)
        mixed = jnp.concatenate([rmsnorm(merge_heads(o_a), out_norm_nsa[i]),
                                 rmsnorm(merge_heads(o_b), out_norm_fox[i])], axis=-1)
        h = h + mixed @ w_out[i]
        h = h + 0.5 * swiglu(rmsnorm(h, ffn2_norm[i]), ffn2_wg[i], ffn2_wu[i], ffn2_wd[i])
        gate = jax.nn.sigmoid(rmsnorm(h, ple_gate_norm[i]) @ ple_w_gate[i])
        e = rmsnorm(p[i] @ ple_w_proj[i], ple_norm[i])
        h = h + gate * e
    return h


N_META = 16
HGRN_HEADS = 8
HGRN_EXPAND = 128
HGRN_FDIM = HGRN_HEADS * HGRN_EXPAND
HGRN_VDIM = D_MODEL
HGRN_HEAD_V = HGRN_VDIM // HGRN_HEADS
CONV_DIM = D_MODEL
CONV_WIDTH = 3
FFN_CONV_WIDTH = 3
CHUNK = 64
IN_SIZES = (HGRN_FDIM,
            HGRN_FDIM,
            HGRN_VDIM,
            HGRN_VDIM,
            CONV_DIM,
            CONV_DIM,
            CONV_DIM,
            D_MODEL,
            D_MODEL)
IN_TOTAL = sum(IN_SIZES)


def _split_points(sizes):
    pts, acc = [], 0
    for s in sizes[:-1]:
        acc += s
        pts.append(acc)
    return pts

def rmsnorm_2(x, w):
    xf = x.astype(jnp.float32)
    y = xf * lax.rsqrt(jnp.mean(xf * xf, axis=-1, keepdims=True) + EPS)
    return (y * w.astype(jnp.float32)).astype(x.dtype)

def causal_dwconv(x, w, b=None):
    K = w.shape[0]
    L = x.shape[1]
    xp = jnp.pad(x, ((0, 0), (K - 1, 0), (0, 0)))
    y = w[0] * xp[:, 0:L]
    for j in range(1, K):
        y = y + w[j] * xp[:, j:j + L]
    if b is not None:
        y = y + b
    return y

def layer_lower_bounds(lb_param):
    p = jax.nn.softmax(lb_param.astype(jnp.float32), axis=0)
    return jnp.cumsum(p, axis=0)[:DEPTH]

def hgrn2_chunked(q, k, v, logf):
    Bsz, H, T, DK = q.shape
    DV = v.shape[-1]
    n = T // CHUNK

    def to_chunks(a):
        return jnp.moveaxis(a.reshape(Bsz, H, n, CHUNK, a.shape[-1]), 2, 0)

    qc, kc, vc, gc = to_chunks(q), to_chunks(k), to_chunks(v), to_chunks(logf)
    causal = jnp.tril(jnp.ones((CHUNK, CHUNK), dtype=bool))[:, :, None]

    def step(S, inp):
        qb, kb, vb, gb = inp
        G = jnp.cumsum(gb, axis=-2)
        o_inter = jnp.einsum('bhtd,bhdv->bhtv', qb * jnp.exp(G), S)
        diff = G[:, :, :, None, :] - G[:, :, None, :, :]
        decay = jnp.exp(jnp.where(causal, diff, -jnp.inf))
        A = jnp.sum(qb[:, :, :, None, :] * kb[:, :, None, :, :] * decay, axis=-1)
        o = o_inter + jnp.einsum('bhts,bhsv->bhtv', A, vb)
        G_last = G[:, :, -1:, :]
        k_dec = kb * jnp.exp(G_last - G)
        S_new = jnp.exp(G_last[:, :, 0, :])[..., None] * S + jnp.einsum('bhsd,bhsv->bhdv', k_dec, vb)
        return S_new, o

    S0 = jnp.zeros((Bsz, H, DK, DV), jnp.float32)
    _, o = lax.scan(step, S0, (qc, kc, vc, gc))
    return jnp.moveaxis(o, 0, 2).reshape(Bsz, H, T, DV)

def hybrid_layer(h, lb, attn_norm_w, w_in, hgrn_norm_w, conv_w, w_out,
                 ffn_norm_w, w_up, ffn_conv_w, ffn_conv_b, w_down):
    Bsz, L, _ = h.shape
    dt = h.dtype
    u = rmsnorm_2(h, attn_norm_w)
    proj = u @ w_in
    q, f_raw, i_in, g_out, b_gate, c_gate, x_conv, gate_a, gate_b = jnp.split(
        proj, _split_points(IN_SIZES), axis=-1)

    q = jax.nn.silu(q.astype(jnp.float32))
    f = lb + (1.0 - lb) * jax.nn.sigmoid(f_raw.astype(jnp.float32))
    logf = jnp.log(f)
    k = 1.0 - f
    v = i_in.astype(jnp.float32)

    def heads(a):
        return jnp.transpose(a.reshape(Bsz, L, HGRN_HEADS, -1), (0, 2, 1, 3))

    pad = (-N_META) % CHUNK
    tpad = ((0, 0), (0, 0), (pad, 0), (0, 0))
    qh, kh, vh, gh = (jnp.pad(heads(a), tpad) for a in (q, k, v, logf))
    o = hgrn2_chunked(qh, kh, vh, gh)[:, :, pad:]
    o = jnp.transpose(o, (0, 2, 1, 3))
    o = rmsnorm_2(o, hgrn_norm_w).reshape(Bsz, L, HGRN_VDIM)
    y_a = (o * jax.nn.silu(g_out.astype(jnp.float32))).astype(dt)

    y_b = b_gate * causal_dwconv(c_gate * x_conv, conv_w)

    merged = jax.nn.sigmoid(gate_a) * y_a + jax.nn.sigmoid(gate_b) * y_b
    h = h + merged @ w_out

    u2 = rmsnorm_2(h, ffn_norm_w)
    a, val = jnp.split(u2 @ w_up, 2, axis=-1)
    a = causal_dwconv(a, ffn_conv_w, ffn_conv_b)
    h = h + (jax.nn.silu(a) * val) @ w_down
    return h

def second_inputs(seed: int = 0) -> dict:
    key = jax.random.key(seed)
    ks = jax.random.split(key, 16)
    f32 = jnp.float32
    nrm = lambda k, shape, s: jax.random.normal(k, shape, f32) * s
    return {
        "x": nrm(ks[0], (BATCH, SEQ, D_MODEL), 1.0),
        "meta_tokens": nrm(ks[1], (N_META, D_MODEL), 1.0),
        "lb_param": nrm(ks[2], (DEPTH + 1, HGRN_FDIM), 0.1),
        "attn_norm_w": 1.0 + nrm(ks[3], (DEPTH, D_MODEL), 0.02),
        "w_in": nrm(ks[4], (DEPTH, D_MODEL, IN_TOTAL), D_MODEL ** -0.5),
        "hgrn_norm_w": 1.0 + nrm(ks[5], (DEPTH, HGRN_HEAD_V), 0.02),
        "conv_w": nrm(ks[6], (DEPTH, CONV_WIDTH, CONV_DIM), CONV_WIDTH ** -0.5),
        "w_out": nrm(ks[7], (DEPTH, D_MODEL, D_MODEL), D_MODEL ** -0.5),
        "ffn_norm_w": 1.0 + nrm(ks[8], (DEPTH, D_MODEL), 0.02),
        "w_up": nrm(ks[9], (DEPTH, D_MODEL, 2 * D_FF), D_MODEL ** -0.5),
        "ffn_conv_w": nrm(ks[10], (DEPTH, FFN_CONV_WIDTH, D_FF), FFN_CONV_WIDTH ** -0.5),
        "ffn_conv_b": nrm(ks[11], (DEPTH, D_FF), 0.02),
        "w_down": nrm(ks[12], (DEPTH, D_FF, D_MODEL), D_FF ** -0.5),
        "final_norm_w": 1.0 + nrm(ks[13], (D_MODEL,), 0.02),
    }

def second_block(x, meta_tokens, lb_param, attn_norm_w, w_in, hgrn_norm_w, conv_w, w_out,
              ffn_norm_w, w_up, ffn_conv_w, ffn_conv_b, w_down, final_norm_w):
    Bsz = x.shape[0]
    meta = jnp.broadcast_to(meta_tokens.astype(x.dtype)[None], (Bsz, N_META, D_MODEL))
    h = jnp.concatenate([meta, x], axis=1)
    lbs = layer_lower_bounds(lb_param)
    for l in range(DEPTH):
        h = hybrid_layer(h, lbs[l], attn_norm_w[l], w_in[l], hgrn_norm_w[l], conv_w[l],
                         w_out[l], ffn_norm_w[l], w_up[l], ffn_conv_w[l], ffn_conv_b[l],
                         w_down[l])
    h = rmsnorm_2(h, final_norm_w)
    return h[:, N_META:]


def setup_inputs(seed=0):
    out = dict(first_inputs(seed))
    for name, value in second_inputs(seed + 1).items():
        if name != "x":
            out[name + "_2"] = value
    return out


def reference(
    x, p, ffn1_norm, ffn1_wg, ffn1_wu, ffn1_wd, mix_norm, w_in, b_forget, q_norm_nsa,
    k_norm_cmp, k_norm_slc, k_norm_win, cmp_pos_k, cmp_pos_v, cmp_k_w1, cmp_k_w2, cmp_v_w1,
    cmp_v_w2, q_norm_fox, k_norm_fox, out_norm_nsa, out_norm_fox, w_out, ffn2_norm, ffn2_wg,
    ffn2_wu, ffn2_wd, ple_gate_norm, ple_w_gate, ple_w_proj, ple_norm, meta_tokens_2,
    lb_param_2, attn_norm_w_2, w_in_2, hgrn_norm_w_2, conv_w_2, w_out_2, ffn_norm_w_2, w_up_2,
    ffn_conv_w_2, ffn_conv_b_2, w_down_2, final_norm_w_2,
):
    x = first_block(
        x, p, ffn1_norm, ffn1_wg, ffn1_wu, ffn1_wd, mix_norm, w_in, b_forget, q_norm_nsa,
        k_norm_cmp, k_norm_slc, k_norm_win, cmp_pos_k, cmp_pos_v, cmp_k_w1, cmp_k_w2, cmp_v_w1,
        cmp_v_w2, q_norm_fox, k_norm_fox, out_norm_nsa, out_norm_fox, w_out, ffn2_norm, ffn2_wg,
        ffn2_wu, ffn2_wd, ple_gate_norm, ple_w_gate, ple_w_proj, ple_norm,
    )
    return second_block(
        x, meta_tokens_2, lb_param_2, attn_norm_w_2, w_in_2, hgrn_norm_w_2, conv_w_2, w_out_2,
        ffn_norm_w_2, w_up_2, ffn_conv_w_2, ffn_conv_b_2, w_down_2, final_norm_w_2,
    )


_drawn_inputs = setup_inputs


def setup_inputs(seed=0):
    import zlib

    import numpy as np

    out = dict(_drawn_inputs(seed))
    spreads = {}
    factors = {'q_norm_nsa': 2.757,
     'k_norm_cmp': 3.819,
     'k_norm_slc': 5.796,
     'k_norm_win': 6.628,
     'cmp_pos_k': 8.0,
     'cmp_pos_v': 3.469,
     'ffn2_norm': 3.491,
     'ple_gate_norm': 6.872,
     'ple_norm': 2.844,
     'lb_param_2': 8.0,
     'attn_norm_w_2': 4.246,
     'hgrn_norm_w_2': 61.747,
     'ffn_norm_w_2': 26.692,
     'ffn_conv_b_2': 40.075,
     'final_norm_w_2': 7.79}
    for name, (base, spread) in spreads.items():
        noise = np.random.default_rng([zlib.crc32(name.encode()), seed]).standard_normal(out[name].shape)
        drawn = base * np.exp(spread * noise) if base else spread * noise
        out[name] = jnp.asarray(drawn.astype(out[name].dtype))
    for name, factor in factors.items():
        out[name] = (out[name] * factor).astype(out[name].dtype)
    return out
```

```python
from contextlib import ExitStack

import concourse.bass as bass
from concourse import mybir

F32 = mybir.dt.float32
F32R = mybir.dt.float32r
U8 = mybir.dt.uint8
ACT = mybir.ActivationFunctionType
ALU = mybir.AluOpType
AX_X = mybir.AxisListType.X

P = 128
D = 1024
KD = D // P
S = 512
M = 16
T = M + S
TT = S // P
F = 2816
FT = F // P
HD = 64
NH = 8
NKV = 2
DP = 256
CB, CS = 32, 16
NC = (S - CB) // CS + 1
CH = 256
HB = T // 2
UNIT = 2048
UC = UNIT // KD
EPS = 1e-6
NEG = -1e30
VH = 8
LEVELS = 9

QA, KC, GA_C, QF, FL_C = 0, 512, 1280, 1304, 2840
U_QA, U_KC, U_VC, U_KS, U_VS, U_KW, U_VW, U_QF, U_KF, U_VF = 0, 4, 5, 6, 7, 8, 9, 10, 14, 18
U_N = 22
NORMED = [0, 1, 2, 3, 6, 8] + list(range(10, 18))
ROPED = [0, 1, 2, 3, 4, 6, 8]

W_UP1 = 0
W_DN1 = W_UP1 + 22
W_IN1 = W_DN1 + 11
W_OUT1 = W_IN1 + 12
W_UP2 = W_OUT1 + 4
W_DN2 = W_UP2 + 22
W_PLG = W_DN2 + 11
W_PLP = W_PLG + 4
W_IN2 = W_PLP + 1
W_OUT2 = W_IN2 + 36
W_UP3 = W_OUT2 + 4
W_DN3 = W_UP3 + 22
W_END = W_DN3 + 11
GATE_UNIT = W_IN1 + 5
FL0 = 32

C_Q, C_F, C_V, C_G, C_B, C_C, C_X, C_GA, C_GB = [D * n for n in range(9)]

ROWS = [
    [("ffn1_norm", 8), ("mix_norm", 8), ("ffn2_norm", 8), ("ple_gate_norm", 8), ("ple_norm", 8),
     ("out_norm_nsa", 4), ("out_norm_fox", 4), ("attn_norm_w_2", 8), ("ffn_norm_w_2", 8),
     ("ffn_conv_b_2", 22), ("hgrn_norm_w_2", 1)],
    [("conv_w_2", 24), ("ffn_conv_w_2", 66), ("lb_param_2", 16)],
    [("cmp_pos_k", 16), ("cmp_pos_v", 16)],
]
HEAD_ROWS = ["q_norm_nsa", "k_norm_slc", "k_norm_win", "q_norm_fox", "k_norm_fox", "k_norm_cmp"]
NROWS = [sum(n for _, n in r) for r in ROWS]
NROWS[2] += len(HEAD_ROWS)


def column(name, c=0):
    for t, rows in enumerate(ROWS):
        at = 0
        for n, k in rows:
            if n == name:
                return t, at + c
            at += k
        if t == 2:
            return t, at + HEAD_ROWS.index(name)
    raise KeyError(name)


def raw_count(u):
    return 16 * (u // 2 + 1) + (32 if u >= GATE_UNIT and u % 2 == GATE_UNIT % 2 else 0)


def used_count(u):
    return 1 + 2 * (u + 1) + 6 * sum(u >= w for w in (W_DN1 + 10, W_DN2 + 10, W_PLP, W_DN3 + 10))


NSA_STEPS = [(hh, i, b) for hh in range(4) for i in range(TT) for b in (0, 1, 2)]
FOX_STEPS = [(hh, i, 0) for hh in range(4) for i in range(TT)]
STEPS = 2 * len(NSA_STEPS) + 2 * len(FOX_STEPS)
GATE_OF = (1, 2, 0)


def tile0(first):
    return used_count(first - 1) if first else 1


def level_sequence():
    seq, b = [], 0
    for lv in range(-1, LEVELS):
        if 1 << max(lv, 0) < M:
            seq.append((lv, META, 7))
        for n in range(VH):
            seq.append((lv, n, b % 7))
            b += 1
    return seq


def level_updates():
    n, out = 2, [2]
    for lv in range(LEVELS):
        n += 3 if lv < LEVELS - 1 else 1
        if 1 << lv < M:
            n += 3 if 2 << lv < M else 1
        out.append(n)
    return out


META = -1
LEVEL_SEQ = level_sequence()
LEVEL_UP = level_updates()
LEVEL_CP0 = sum(lv < 7 for lv, _, _ in LEVEL_SEQ)
P2 = 5
N_ROWS = sum(len(r) for r in ROWS) + 2 * len(HEAD_ROWS)
N_CONST = 8
SLAB = 212800


def build(nc, a, out):
    ctx = ExitStack()
    with ctx:
        place = {"end": 0}

        def area(nbytes):
            at = place["end"]
            place["end"] = at + (nbytes + 31) // 32 * 32
            return at

        base = (nc.sbuf_base + 31) // 32 * 32
        ctx.enter_context(nc.sbuf_tensor("slab", [P, SLAB // 4], F32))

        def at(name, shape, off, dt=F32):
            return nc.alloc_sbuf_tensor_at(name, shape, dt, offset=base + off)

        def sb(name, shape, dt=F32):
            n = 1 if dt == U8 else 4
            for x in shape[1:]:
                n *= x
            return at(name, shape, area(n), dt)

        h = sb("h", [P, KD, T])
        XN = area(2 * KD * T * 4)
        xh = at("xh", [P, KD, T], XN, F32R)
        xl = at("xl", [P, KD, T], XN + KD * T * 4, F32R)
        raw = sb("raw", [P, 2, UNIT])
        whi = sb("whi", [P, 2, UNIT], F32R)
        wlo = sb("wlo", [P, 2, UNIT], F32R)
        TMP = area(4 * T * 4)
        tmp = at("tmp", [P, 4, T], TMP)
        ident = sb("ident", [P, P])
        causal = sb("causal", [P, P])
        headones = sb("headones", [P, P])
        rot = sb("rot", [P, P])
        COS = area(2 * S * 4)
        cosb = at("cosb", [P, S], COS)
        sinb = at("sinb", [P, S], COS + S * 4)
        cmpneg = sb("cmpneg", [P, TT, 32])
        cmprow = sb("cmprow", [P, TT])
        levelmask = sb("levelmask", [P, 8, P], U8)
        cols = sb("cols", [P, 3, P])
        ones1 = sb("ones1", [P, 1])
        epsc = sb("epsc", [P, 1])
        negones = sb("negones", [8, P])
        forget_b = sb("forget_b", [FL0 + NH, 1])
        std = sb("std", [P, 112])
        rstd = sb("rstd", [P, 112])
        lb = sb("lb", [P, 2, 8])
        lbt = sb("lbt", [P, 4, 8])
        ttm = sb("ttm", [P, 2, VH, 8])
        AR = area(2 * FT * S * 4)
        act_h = at("act_h", [P, FT, S], AR, F32R)
        act_l = at("act_l", [P, FT, S], AR + FT * S * 4, F32R)
        x_tok = at("x_tok", [P, TT, D], AR)
        meta_tok = at("meta_tok", [M, D], AR + 16384)
        rows_t = at("rows_t", [P, 3, P], AR + 20480)
        levels_f = at("levels_f", [P, 8, P], AR + 22528)
        uT = at("uT", [P, U_N, S], AR)
        R2 = AR + U_N * S * 4
        w1 = at("w1", [P, 2, 16, CH], R2)
        blk = at("blk", [P, 2, 16, NKV, 32], R2 + 32768)
        vtok = at("vtok", [P, TT, 768], R2)
        otok = at("otok", [P, TT, D], R2 + 12288)
        prob = at("prob", [P, 3, S], R2 + 28672)
        probT = at("probT", [P, 3, TT, P], R2 + 34816)
        hid = at("hid", [P, 2, 2, NKV, 32], R2 + 40960)
        kcmp = at("kcmp", [P, 64], R2 + 41984)
        kcsq = at("kcsq", [P, 64], R2 + 42240)
        kcr = at("kcr", [P, 64], R2 + 42496)
        vcmp = at("vcmp", [32, NKV, HD], R2 + 42752)
        gsig = at("gsig", [P, TT, 24], R2 + 43264)
        w2 = at("w2", [P, 2, 2, HD], R2 + 43776)
        stat = at("stat", [P, 4, 4], R2 + 44800)
        kD = at("kD", [P, 2, NKV, S], XN)
        qst = at("qst", [P, 2, S], XN + 8192)
        cst = at("cst", [8, 4, S], XN + 12288)
        cum = at("cum", [8, S], XN + 20480)
        flg = at("flg", [8, 3, S], XN + 22528)
        kst = at("kst", [P, 2, S], XN + 22528)
        osq = at("osq", [P, S], XN + 28672)
        gateT1 = at("gateT1", [FL0 + NH, S], R2 + 40960)
        kcst = at("kcst", [P, 32], XN + 30720)
        vcst = at("vcst", [32, HD], XN + 30848)
        gateT = at("gateT", [P, KD, S], AR)
        eT = at("eT", [P, KD, S], AR + 16384)
        p_tok = at("p_tok", [P, TT, DP], AR + 32768)
        p_h = at("p_h", [P, 2, S], AR + 36864, F32R)
        p_l = at("p_l", [P, 2, S], AR + 40960, F32R)
        Q = at("Q", [P, VH, T], AR)
        Fg = at("Fg", [P, VH, T], AR + 16896)
        V = at("V", [P, TT + 1, D], AR + 33792)
        GA = at("GA", [P, KD, T], AR + 54272)
        YB = at("YB", [P, KD, T], AR + 71168)
        K = at("K", [P, VH, T], XN)
        Ad = at("Ad", [P, VH, S], XN + 16896)
        Am = sb("Am", [M, VH, M])
        Amx = at("Amx", [M, 2, S], COS)
        Tev = at("Tev", [P, 4224], AR + 16896)
        Tod = at("Tod", [P, 4 * T], TMP)
        gainb = at("gainb", [P, D], AR)
        y_tok = at("y_tok", [P, TT, D], AR + 4096)
        assert place["end"] <= SLAB, place["end"]

        ps = ctx.enter_context(nc.psum_tensor("ps", [P, 8, 512], F32))

        def sem(name):
            return ctx.enter_context(nc.semaphore(name))

        const_in = sem("const_in"); ident_in = sem("ident_in"); levels_in = sem("levels_in"); rows_in = sem("rows_in"); x_in = sem("x_in")
        raw_in = [sem("raw_in0"), sem("raw_in1")]
        cmp_in = sem("cmp_in"); p_in = sem("p_in"); gain_in = sem("gain_in"); stored = sem("stored")
        hi_ready = sem("hi_ready"); lo_ready = sem("lo_ready"); tiles_done = sem("tiles_done")
        setup = sem("setup"); colsT = sem("colsT"); cols_ready = sem("cols_ready")
        xT = sem("xT"); meta_ready = sem("meta_ready"); hid_zero = sem("hid_zero"); gc_ready = sem("gc_ready"); e_step = sem("e_step"); fsum = sem("fsum"); lb_step = sem("lb_step"); lb_exp = sem("lb_exp"); q_scaled = sem("q_scaled")
        h_ready = sem("h_ready"); sq_ready = sem("sq_ready"); sq_added = sem("sq_added"); ssq_done = sem("ssq_done")
        std_ready = sem("std_ready"); rstd_ready = sem("rstd_ready"); rb_done = sem("rb_done")
        normed = sem("normed"); xh_ready = sem("xh_ready"); xl_ready = sem("xl_ready")
        gate_done = sem("gate_done"); prod_done = sem("prod_done")
        acth_done = sem("acth_done"); actl_done = sem("actl_done")
        conv_in = sem("conv_in"); conv_step = sem("conv_step")
        u_ready = sem("u_ready"); gatep_done = sem("gatep_done")
        usq = sem("usq"); ussq = sem("ussq"); ustd = sem("ustd"); urstd = sem("urstd")
        urb = sem("urb"); unorm = sem("unorm"); urot = sem("urot"); rope_step = sem("rope_step")
        kdup = sem("kdup"); vtr = sem("vtr"); v_ready = sem("v_ready")
        blk_cp = sem("blk_cp"); blk_ready = sem("blk_ready"); hid_mm = sem("hid_mm")
        hid_ready = sem("hid_ready"); cmp_mm = sem("cmp_mm"); cmp_sq = sem("cmp_sq"); cmp_step = sem("cmp_step")
        g_ready = sem("g_ready"); gate_mm = sem("gate_mm"); fl_step = sem("fl_step"); fl_v = sem("fl_v")
        q_staged = sem("q_staged"); c_staged = sem("c_staged")
        score_done = sem("score_done"); nmax_done = sem("nmax_done"); exp_done = sem("exp_done")
        trans_done = sem("trans_done"); ptev_done = sem("ptev_done"); pv_done = sem("pv_done")
        o_step = sem("o_step"); o_done = sem("o_done")
        osq_done = sem("osq_done"); ostd = sem("ostd"); orstd = sem("orstd"); oscaled = sem("oscaled")
        otr = sem("otr")
        pT_done = sem("pT_done"); pT_cp = sem("pT_cp"); ph_ready = sem("ph_ready"); pl_ready = sem("pl_ready")
        gate_ready = sem("gate_ready"); e_mm = sem("e_mm"); e_ready = sem("e_ready")
        sig_done = sem("sig_done"); p2_step = sem("p2_step"); p2_free = sem("p2_free")
        lev_cp = sem("lev_cp"); hsq = sem("hsq"); hssq = sem("hssq"); hstd = sem("hstd"); hrstd = sem("hrstd")
        hrb = sem("hrb"); h2_step = sem("h2_step")
        vev = sem("vev"); k_ready = sem("k_ready"); az = sem("az")
        lev_mm = sem("lev_mm"); lev_sel = sem("lev_sel"); lev_up = sem("lev_up")
        amx_mm = sem("amx_mm"); amx_cp = sem("amx_cp"); o2_mm = sem("o2_mm"); o2_cp = sem("o2_cp")
        fT = sem("fT"); fsq = sem("fsq"); fstd = sem("fstd"); frstd = sem("frstd"); f_ready = sem("f_ready")

        block = ctx.enter_context(nc.Block())

        def col(name, c=0, n=1):
            t, r = column(name, c)
            return cols[:, t, r:r + n]

        def w_view(buf, slot, kt):
            return buf[:, slot, :].rearrange("p (k n) -> p k n", k=kt)

        WHOLE = [(M, S, 0)]
        BOTH = [(0, HB, 0), (HB, HB, 1)]
        CONV = [(M - 4, 258, 0), (M + 254, 258, 1)]

        SSQ, RB = 5, 6

        def rb_view(whole):
            return ps[:, RB, :] if whole else ps[:, RB:RB + 2, 0:HB]

        def halves(ap):
            return ap.rearrange("p (a b) -> p a b", a=2)

        @block.sync
        def _(sp):
            def const(dst, src):
                sp.dma_start(dst, src).then_inc(const_in, 16)

            sp.dma_start(ident[:], a["k_ident"]).then_inc(ident_in, 16)
            for i in range(TT):
                sp.dma_start(x_tok[:, i, :], a["x"][0, i * P:(i + 1) * P, :]).then_inc(x_in, 16)
            sp.dma_start(meta_tok[:], a["meta_tokens_2"]).then_inc(x_in, 16)
            sp.dma_start(levels_f[:], a["k_levels"]).then_inc(levels_in, 16)
            for t, rows in enumerate(ROWS):
                r = 0
                for name, n in rows:
                    src = a[name]
                    for _ in range(len(src.shape) - 1):
                        src = src.flatten_outer_dims() if len(src.shape) > 2 else src
                    if len(src.shape) == 2:
                        src = src.rearrange("a b -> (a b)")
                    sp.dma_start(rows_t[r:r + n, t, :], src.rearrange("(a b) -> a b", b=P)).then_inc(rows_in, 16)
                    r += n
            for name in HEAD_ROWS:
                for half in range(2):
                    sp.dma_start(rows_t[r:r + 1, 2, half * HD:(half + 1) * HD], a[name]).then_inc(rows_in, 16)
                r += 1
            const(causal[:], a["k_causal"])
            const(headones[:], a["k_headones"])
            const(rot[:], a["k_rot"])
            const(cosb[:], a["k_cos"])
            const(sinb[:], a["k_sin"])
            const(cmpneg[:], a["k_cmpneg"])
            const(cmprow[:], a["k_cmprow"])
            const(forget_b[FL0:FL0 + NH, :], a["b_forget"].rearrange("a n -> n a"))

            def load(u, slot, kt, src, free=True):
                if free:
                    sp.wait_ge(lo_ready, u - 1)
                sp.dma_start(w_view(raw, slot, kt), src).then_inc(raw_in[slot], 16)

            def col_unit(name):
                w = a[name][0].rearrange("(k p) n -> p k n", p=P)
                return lambda c: w[:, :, bass.ds(c, UC)]

            def up(first, wa, wb):
                wa, wb = col_unit(wa), col_unit(wb) if isinstance(wb, str) else wb
                s = first % 2
                if first == 0:
                    load(0, 0, KD, wa(0), free=False)
                    load(1, 1, KD, wb(0), free=False)
                with sp.Fori(1 if first == 0 else 0, F // UC) as i:
                    load(first + 2 * i, s, KD, wa(i * UC))
                    load(first + 2 * i + 1, 1 - s, KD, wb(i * UC))

            def down(first, name):
                w = a[name][0].rearrange("(u k p) n -> p u k n", p=P, k=2)
                s = first % 2
                load(first, s, 2, w[:, 0])
                with sp.Fori(0, 5) as i:
                    for e in range(2):
                        load(first + 1 + 2 * i + e, (s + 1 + e) % 2, 2, w[:, bass.ds(2 * i + 1 + e, 1)].rearrange("p u k n -> p (u k) n"))

            def square(first, name):
                w = col_unit(name)
                s = first % 2
                with sp.Fori(0, 2) as i:
                    for e in range(2):
                        load(first + 2 * i + e, (s + e) % 2, KD, w((2 * i + e) * UC))

            up(W_UP1, "ffn1_wg", "ffn1_wu")
            down(W_DN1, "ffn1_wd")
            w = col_unit("w_in")
            s = W_IN1 % 2
            with sp.Fori(0, 2) as i:
                for e in range(2):
                    load(W_IN1 + 2 * i + e, (s + e) % 2, KD, w((2 * i + e) * UC))
            load(W_IN1 + 4, s, KD, w(4 * UC))
            gate_w = a["w_in"][0].rearrange("(k p) n -> p k n", p=P)
            gslot = raw[:, 1 - s, 0:KD * P].rearrange("p (k n) -> p k n", k=KD)
            sp.wait_ge(lo_ready, GATE_UNIT - 1)
            for c0, c1, col0 in ((0, FL0, GA_C), (FL0, FL0 + NH, FL_C), (FL0 + NH, P, 0)):
                sp.dma_start(gslot[:, :, c0:c1], gate_w[:, :, col0:col0 + c1 - c0]).then_inc(raw_in[1 - s], 16)
            with sp.Fori(0, 3) as i:
                for e in range(2):
                    load(W_IN1 + 6 + 2 * i + e, (s + e) % 2, KD, w(QF + (2 * i + e) * UC))
            sp.wait_ge(h_ready, 2 * KD)
            for n, name in enumerate(("cmp_k_w1", "cmp_v_w1")):
                sp.dma_start(w1[:, n], a[name][0].rearrange("(k p) n -> p k n", p=P)).then_inc(cmp_in, 16)
            for n, name in enumerate(("cmp_k_w2", "cmp_v_w2")):
                sp.dma_start(w2[:, n], a[name][0].rearrange("(k p) n -> p k n", p=P)).then_inc(cmp_in, 16)
            square(W_OUT1, "w_out")
            up(W_UP2, "ffn2_wg", "ffn2_wu")
            down(W_DN2, "ffn2_wd")
            square(W_PLG, "ple_w_gate")
            sp.wait_ge(h_ready, 4 * KD)
            sp.dma_start(p_tok[:], a["p"][0, 0].rearrange("(i p) n -> p i n", p=P)).then_inc(p_in, 16)
            load(W_PLP, W_PLP % 2, 2, a["ple_w_proj"][0].rearrange("(k p) n -> p k n", p=P))
            w = col_unit("w_in_2")
            s = W_IN2 % 2
            for n, (c0, c1) in enumerate(((C_Q, C_F), (C_G, C_GA), (C_C, C_X), (C_B, C_GB))):
                with sp.Fori(0, 4) as i:
                    load(W_IN2 + 8 * n + 2 * i, s, KD, w(c0 + i * UC))
                    load(W_IN2 + 8 * n + 2 * i + 1, 1 - s, KD, w(c1 + i * UC))
            with sp.Fori(0, 2) as i:
                for e in range(2):
                    load(W_IN2 + 32 + 2 * i + e, (s + e) % 2, KD, w(C_V + (2 * i + e) * UC))
            square(W_OUT2, "w_out_2")
            w = col_unit("w_up_2")
            up(W_UP3, "w_up_2", lambda c: w(c + F))
            down(W_DN3, "w_down_2")
            sp.wait_ge(h_ready, 7 * KD)
            sp.dma_start(gainb[:], a["final_norm_w_2"].rearrange("(a n) -> a n", a=1).to_broadcast([P, D])).then_inc(gain_in, 16)
            for i in range(TT):
                sp.wait_ge(f_ready, 2 * (i + 1))
                sp.dma_start(out[0, i * P:(i + 1) * P, :], y_tok[:, i, :]).then_inc(stored, 16)
            sp.wait_ge(stored, 16 * TT)

        @block.gpsimd
        def _(pool):
            nc.gpsimd.memset(ones1[:], 1.0).then_inc(setup, 1)
            nc.gpsimd.memset(epsc[:], EPS).then_inc(setup, 1)
            nc.gpsimd.memset(negones[:], -1.0).then_inc(setup, 1)
            pool.wait_ge(levels_in, 16)
            nc.gpsimd.tensor_copy(levelmask[:], levels_f[:]).then_inc(setup, 1)

            def lo(u, slot, n=UNIT):
                pool.wait_ge(hi_ready, u + 1)
                nc.gpsimd.tensor_tensor(wlo[:, slot, 0:n], raw[:, slot, 0:n], whi[:, slot, 0:n].bitcast(F32),
                                        ALU.subtract).then_inc(lo_ready, 1)

            def lo_run(u0, u1):
                s = u0 % 2
                with pool.Fori(0, (u1 - u0) // 2) as i:
                    for e in range(2):
                        lo(u0 + 2 * i + e, (s + e) % 2)
                if (u1 - u0) % 2:
                    lo(u1 - 1, (u1 - 1) % 2)

            lo_run(0, GATE_UNIT)
            lo(GATE_UNIT, GATE_UNIT % 2, KD * P)
            lo_run(GATE_UNIT + 1, W_END)

        @block.scalar
        def _(act):
            def hi(u, slot, landed, used=None, n=UNIT):
                act.wait_ge(raw_in[slot], landed)
                if used is not None:
                    act.wait_ge(tiles_done, used)
                nc.scalar.activation(whi[:, slot, 0:n], raw[:, slot, 0:n], ACT.Copy).then_inc(hi_ready, 1)

            def hi_pair(first, i, at=0):
                for e in (1, 2):
                    u = first + at + e
                    if u < W_END:
                        hi(u + 2 * i, u % 2, raw_count(u) + 16 * i, tile0(first) + 2 * (at + e - 1) + 4 * i)

            def hi_one(u, n=UNIT):
                if u < W_END:
                    hi(u, u % 2, raw_count(u), used_count(u - 2) if u >= 2 else None, n)

            def squares(m, ready, src, c0):
                for n in range(KD):
                    act.wait_ge(*ready(n))
                    if n >= 4:
                        act.wait_ge(sq_added, (KD - 1) * m + n - 3)
                    nc.scalar.activation(tmp[:, n % 3 if n else 3, c0:T], src(n), ACT.Square).then_inc(sq_ready, 1)
                act.wait_ge(ssq_done, m + 1)
                first = 1 if c0 else 0
                nc.scalar.activation(std[:, first:5], ps[:, SSQ, first:5], ACT.Sqrt, bias=epsc[:, 0:1],
                                     scale=1.0 / D).then_inc(std_ready, 1)

            def norm(m, v, w, x_only):
                c0 = M if x_only else 0
                squares(m, lambda n: (h_ready, KD * w + n + 1), lambda n: h[:, n, c0:T], c0)
                for n in range(KD):
                    act.wait_ge(normed, KD * v + n + 1)
                    nc.scalar.activation(xh[:, n, c0:T], tmp[:, n % 4, c0:T], ACT.Copy).then_inc(xh_ready, 1)

            def ffn_up(g, first, conv=False):
                with act.Fori(0, F // UC) as i:
                    t0 = tile0(first) + 4 * i
                    hi_pair(first, i)
                    for j in range(2):
                        act.wait_ge(tiles_done, t0 + j + 1)
                        if conv:
                            nc.scalar.activation(tmp[:, j, M - 4:T].rearrange("p (a b) -> p a b", a=2),
                                                 ps[:, 2 * j:2 * j + 2, 0:258], ACT.Copy).then_inc(conv_in, 1)
                        else:
                            nc.scalar.activation(tmp[:, j, M:T], ps[:, j, :], ACT.Silu).then_inc(gate_done, 1)
                    if conv:
                        for j in range(2):
                            act.wait_ge(conv_step, 6 * i + 3 * j + 3)
                            nc.scalar.activation(tmp[:, j, M:T], tmp[:, 2 + j, 0:S], ACT.Silu).then_inc(gate_done, 1)
                    for j in range(2):
                        act.wait_ge(prod_done, FT * g + 2 * i + j + 1)
                        nc.scalar.activation(act_h[:, bass.ds(2 * i + j, 1), :],
                                             tmp[:, 2 + j:3 + j, 0:S], ACT.Copy).then_inc(acth_done, 1)

            def ffn_down(first):
                with act.Fori(0, 5) as i:
                    hi_pair(first, i)
                hi_one(first + 11)

            def square(first):
                with act.Fori(0, 2) as i:
                    hi_pair(first, i)

            act.wait_ge(setup, 4)
            for t in range(3):
                act.wait_ge(colsT, t + 1)
                nc.scalar.activation(cols[:, t, 0:NROWS[t]], ps[:, t, 0:NROWS[t]], ACT.Copy).then_inc(cols_ready, 1)
            hi_one(0)
            act.wait_ge(tiles_done, 1)
            nc.scalar.activation(h[:, :, 0:M], ps[:, 3, 0:KD * M].rearrange("p (n m) -> p n m", n=KD), ACT.Copy).then_inc(meta_ready, 1)
            for n in range(KD):
                act.wait_ge(xT, n + 1)
                nc.scalar.activation(h[:, n, M:T], ps[:, (n + 4) % 8, :], ACT.Copy).then_inc(h_ready, 1)
            act.wait_ge(lb_step, 2)
            nc.scalar.activation(lbt[:, 0:2, :], lbt[:, 0:2, :], ACT.Exp).then_inc(lb_exp, 1)
            norm(0, 0, 0, True)
            ffn_up(0, W_UP1)
            ffn_down(W_DN1)
            norm(1, 1, 1, True)
            t0 = tile0(W_IN1)
            with act.Fori(0, 2) as i:
                hi_pair(W_IN1, i)
                for j in range(4):
                    act.wait_ge(tiles_done, t0 + 4 * i + j + 1)
                    nc.scalar.activation(uT[:, bass.ds(4 * i + j, 1), :], ps[:, j:j + 1, :], ACT.Copy).then_inc(u_ready, 1)
            hi_one(GATE_UNIT, KD * P)
            hi_one(GATE_UNIT + 1)
            for j in range(2):
                act.wait_ge(tiles_done, t0 + 8 + j + 1)
                nc.scalar.activation(uT[:, 8 + j, :], ps[:, j, :], ACT.Copy).then_inc(u_ready, 1)
            act.wait_ge(tiles_done, used_count(GATE_UNIT))
            nc.scalar.activation(gateT1[:], ps[0:FL0 + NH, 2, :], ACT.Copy).then_inc(u_ready, 1)
            with act.Fori(0, 3) as i:
                hi_pair(W_IN1, i, 6)
                for j in range(4):
                    act.wait_ge(tiles_done, t0 + 12 + 4 * i + j + 1)
                    nc.scalar.activation(uT[:, bass.ds(U_QF + 4 * i + j, 1), :], ps[:, j:j + 1, :], ACT.Copy).then_inc(u_ready, 1)
            act.wait_ge(u_ready, U_N + 1)
            for n, t in enumerate(NORMED):
                if n >= 4:
                    act.wait_ge(ussq, n - 3)
                nc.scalar.activation(tmp[:, n % 4, 0:S], uT[:, t, :], ACT.Square).then_inc(usq, 1)
            act.wait_ge(ussq, len(NORMED))
            nc.scalar.activation(std[:, 0:112], ps[:, 7, 0:112], ACT.Sqrt, bias=epsc[:, 0:1], scale=1.0 / HD).then_inc(ustd, 1)
            for n, t in enumerate((U_VC, U_KC)):
                if t == U_KC:
                    act.wait_ge(rope_step, 3 * ROPED.index(t) + 3)
                for par in range(2):
                    for g in range(NKV):
                        s0 = uT[g * HD:(g + 1) * HD, t, par:par + 1]
                        win = bass.AP(tensor=s0.tensor, offset=s0.offset, ap=[s0.ap[0], [2, CB // 2], [CS, NC]])
                        nc.scalar.activation(blk[par * HD:(par + 1) * HD, 1 - n, :, g, 0:NC], win, ACT.Copy).then_inc(blk_cp, 1)
            act.wait_ge(gate_mm, 1)
            nc.scalar.activation(gsig[:], ps[:, 7, 0:TT * 24].rearrange("p (i n) -> p i n", i=TT), ACT.Sigmoid).then_inc(g_ready, 1)
            act.wait_ge(fl_v, 2)
            nc.scalar.activation(flg[:, 1, :], flg[:, 0, :], ACT.Exp).then_inc(fl_step, 1)
            act.wait_ge(fl_step, 1)
            nc.scalar.activation(flg[:, 0, :], flg[:, 1, :], ACT.Ln, bias=1.0).then_inc(fl_step, 1)
            act.wait_ge(hid_zero, 1)
            for n in range(2):
                for mt in range(2):
                    q = 2 * n + mt
                    act.wait_ge(hid_mm, q + 1)
                    nc.scalar.activation(hid[:, 1 - n, mt, :, 0:NC], ps[:, q, 0:NKV * NC].rearrange("p (g n) -> p g n", g=NKV),
                                         ACT.Silu).then_inc(hid_ready, 1)
            act.wait_ge(cmp_mm, 3)
            nc.scalar.activation(kcsq[:], ps[:, 6, 256:320], ACT.Square).then_inc(cmp_sq, 1)
            nc.scalar.activation(vcmp[:], ps[0:32, 6, 320:448].rearrange("p (g d) -> p g d", g=NKV), ACT.Copy).then_inc(cmp_sq, 1)
            act.wait_ge(cmp_mm, 4)
            nc.scalar.activation(kcr[:], ps[:, 6, 448:512], ACT.Sqrt, bias=epsc[:, 0:1], scale=1.0 / HD).then_inc(cmp_sq, 1)
            for n in range(6):
                act.wait_ge(vtr, n + 1)
                nc.scalar.activation(vtok[:, :, n * P:(n + 1) * P], ps[:, 2 + n % 2, :].rearrange("p (i d) -> p i d", i=TT),
                                     ACT.Copy).then_inc(v_ready, 1)
            act.wait_ge(rope_step, 3 * len(ROPED))
            for b, t in enumerate((U_KS, U_KW)):
                for g in range(NKV):
                    for half in range(2):
                        nc.scalar.activation(kD[half * HD:(half + 1) * HD, b, g, :], uT[g * HD:(g + 1) * HD, t, :],
                                             ACT.Copy).then_inc(kdup, 1)
            act.wait_ge(unorm, len(NORMED))

            def attention(n0, steps, t_q, fox):
                NS = len(steps)
                with act.Fori(0, 2) as it:
                    s0 = n0 + NS * it
                    for e in range(2):
                        nc.scalar.activation(qst[:, e:e + 1, :], uT[:, bass.ds(t_q + 2 * it + e, 1), :], ACT.Copy).then_inc(q_staged, 1)
                    if fox:
                        for e in range(2):
                            nc.scalar.activation(kst[:, e:e + 1, :], uT[:, bass.ds(U_KF + 2 * it + e, 1), :], ACT.Copy).then_inc(q_staged, 1)
                    else:
                        nc.scalar.activation(kst[:, :, :].unsqueeze(2), kD[:, :, bass.ds(it, 1), :], ACT.Copy).then_inc(q_staged, 1)
                        nc.scalar.activation(kcst[:], kcmp[:, bass.ds(32 * it, 32)], ACT.Copy).then_inc(q_staged, 1)
                    for s in range(NS + 1):
                        if s < NS:
                            hh, i, b = steps[s]
                            n = 32 if b == 2 else (i + 1) * P
                            act.wait_ge(nmax_done, s0 + s + 1)
                            if s >= 3:
                                act.wait_ge(trans_done, s0 + s - 2)
                            nc.scalar.activation(prob[:, s % 3, 0:n], ps[:, s % 3, 0:n], ACT.Exp, bias=stat[:, 0, s % 4:s % 4 + 1],
                                                 accum_out=stat[:, 1, s % 4:s % 4 + 1]).then_inc(exp_done, 1)
                        if s >= 1:
                            q = s - 1
                            hh, i, b = steps[q]
                            act.wait_ge(trans_done, s0 + q + 1)
                            if q >= 3:
                                act.wait_ge(pv_done, s0 + q - 2)
                            if q == 2 and not fox:
                                act.wait_ge(pv_done, s0 + 1)
                                nc.scalar.activation(vcst[:], vcmp[:, bass.ds(it, 1), :].rearrange("p a d -> p (a d)"), ACT.Copy).then_inc(q_staged, 1)
                            if b == 2:
                                nc.scalar.activation(probT[0:32, q % 3, 0, :], ps[0:32, 3 + q % 3, 0:P], ACT.Copy).then_inc(ptev_done, 1)
                            else:
                                nc.scalar.activation(probT[:, q % 3, 0:i + 1, :],
                                                     ps[:, 3 + q % 3, 0:(i + 1) * P].rearrange("p (k q) -> p k q", k=i + 1),
                                                     ACT.Copy).then_inc(ptev_done, 1)

            act.wait_ge(fl_v, 4)
            act.wait_ge(cmp_step, 2)
            act.wait_ge(kdup, 8)
            attention(0, NSA_STEPS, U_QA, False)
            attention(2 * len(NSA_STEPS), FOX_STEPS, U_QF, True)
            act.wait_ge(o_done, STEPS)
            for n in range(2 * TT):
                if n:
                    act.wait_ge(osq_done, n)
                nc.scalar.activation(osq[:], otok[:, n // 2, n % 2 * S:(n % 2 + 1) * S], ACT.Square,
                                     accum_out=rstd[:, n:n + 1]).then_inc(osq_done, 1)
            act.wait_ge(osq_done, 8)
            nc.scalar.activation(std[:, 0:8], rstd[:, 0:8], ACT.Sqrt, bias=epsc[:, 0:1], scale=1.0 / S).then_inc(ostd, 1)
            for n in range(KD):
                act.wait_ge(otr, n + 1)
                if n >= 4:
                    act.wait_ge(xl_ready, 2 * KD + n - 3)
                gain = col("out_norm_nsa", n) if n < 4 else col("out_norm_fox", n - 4)
                nc.scalar.activation(tmp[:, n % 4, M:T], ps[:, 4 + n % 4, :], ACT.Copy, scale=gain).then_inc(normed, 1)
                act.wait_ge(normed, 2 * KD + n + 1)
                nc.scalar.activation(xh[:, n, M:T], tmp[:, n % 4, M:T], ACT.Copy).then_inc(xh_ready, 1)
            square(W_OUT1)
            norm(2, 3, 2, True)
            ffn_up(1, W_UP2)
            ffn_down(W_DN2)
            norm(3, 4, 3, True)
            t0 = tile0(W_PLG)
            with act.Fori(0, 2) as i:
                hi_pair(W_PLG, i)
                for j in range(4):
                    act.wait_ge(tiles_done, t0 + 4 * i + j + 1)
                    nc.scalar.activation(gateT[:, bass.ds(4 * i + j, 1), :], ps[:, j:j + 1, :], ACT.Sigmoid).then_inc(gate_ready, 1)
            for e in range(2):
                act.wait_ge(pT_done, e + 1)
                nc.scalar.activation(p_h[:, e, :], ps[:, 4 + e, :], ACT.Copy).then_inc(ph_ready, 1)
            hi_one(W_IN2)
            for n in range(KD):
                act.wait_ge(tiles_done, used_count(W_PLP - 1) + n + 1)
                nc.scalar.activation(eT[:, n, :], ps[:, (n + 6) % 8, :], ACT.Copy).then_inc(e_ready, 1)
            squares(4, lambda n: (e_ready, n + 1), lambda n: eT[:, n, :], M)
            norm(5, 5, 4, False)
            for n in range(4):
                with act.Fori(0, 4) as i:
                    t0 = tile0(W_IN2) + 16 * n + 4 * i
                    hi_pair(W_IN2, i, 8 * n)
                    act.wait_ge(p2_free, P2 + 16 * n + 4 * i)
                    for j in range(4):
                        if (n == 2 and j >= 2) or (n == 3 and j < 2):
                            continue
                        act.wait_ge(tiles_done, t0 + j + 1)
                        nc.scalar.activation(halves(tmp[:, j, :]), ps[:, 2 * j:2 * j + 2, 0:HB],
                                             ACT.Copy if n == 2 else ACT.Sigmoid).then_inc(sig_done, 1)
            for i in range(2):
                hi_pair(W_IN2, i, 32)
                for e in range(2):
                    act.wait_ge(tiles_done, used_count(W_IN2 + 32 + 2 * i + e))
                    nc.scalar.activation(V[:, :, (2 * i + e) * UC:(2 * i + e + 1) * UC],
                                         ps[:, 3 * e:3 * e + 3, :].rearrange("p b c -> p (b c)")[:, 0:5 * UC].rearrange("p (i c) -> p i c", i=5),
                                         ACT.Copy).then_inc(vev, 1)
            for idx, (lv, n, bank) in enumerate(LEVEL_SEQ):
                if lv >= 7:
                    act.wait_ge(lev_mm, idx + 1)
                    w = 256 if lv == 7 else 512
                    dst = Tod[:, 64 + n * 256:64 + (n + 1) * 256] if lv == 7 else Tev[:, 128 + n * 512:128 + (n + 1) * 512]
                    nc.scalar.activation(dst, ps[:, bank, 0:w], ACT.Copy).then_inc(lev_cp, 1)
            for n in range(VH):
                act.wait_ge(amx_mm, n + 1)
                if n >= 2:
                    act.wait_ge(o2_mm, n - 1)
                nc.scalar.activation(Amx[:, n % 2, :], ps[0:M, n % 2, :], ACT.Copy).then_inc(amx_cp, 1)
                act.wait_ge(o2_mm, n + 1)
                nc.scalar.activation(Q[:, n, M:T], ps[:, 2 + n % 2, :], ACT.Copy).then_inc(o2_cp, 1)
            nc.scalar.activation(Q[:, :, 0:M], ps[:, 4, 0:VH * M].rearrange("p (n m) -> p n m", n=VH), ACT.Copy).then_inc(o2_cp, 1)
            act.wait_ge(o2_cp, VH + 1)
            for n in range(VH):
                if n >= 4:
                    act.wait_ge(hssq, n - 3)
                nc.scalar.activation(tmp[:, n % 4, :], Q[:, n, :], ACT.Square).then_inc(hsq, 1)
            act.wait_ge(hssq, VH)
            nc.scalar.activation(std[:, 0:40], ps[:, 5, 0:40], ACT.Sqrt, bias=epsc[:, 0:1], scale=1.0 / P).then_inc(hstd, 1)
            for n in range(VH):
                act.wait_ge(normed, 6 * KD + n + 1)
                nc.scalar.activation(xh[:, n, :], tmp[:, n % 4, :], ACT.Copy).then_inc(xh_ready, 1)
            square(W_OUT2)
            norm(6, 7, 5, False)
            ffn_up(2, W_UP3, conv=True)
            ffn_down(W_DN3)
            for i in range(TT):
                for e in range(2):
                    n = 2 * i + e
                    act.wait_ge(fT, n + 1)
                    if n:
                        act.wait_ge(fsq, n)
                    nc.scalar.activation(tmp[:, 0, 0:S], ps[:, n, :], ACT.Square, accum_out=rstd[:, n:n + 1]).then_inc(fsq, 1)
            act.wait_ge(fsum, 1)
            nc.scalar.activation(std[:, 0:TT], std[:, 8:8 + TT], ACT.Sqrt, bias=epsc[:, 0:1], scale=1.0 / D).then_inc(fstd, 1)
        @block.vector
        def _(dve):
            def split_lo(v, n, c0):
                dve.wait_ge(xh_ready, KD * v + n + 1)
                nc.vector.tensor_tensor(xl[:, n, c0:T], tmp[:, n % 4, c0:T], xh[:, n, c0:T].bitcast(F32),
                                        ALU.subtract).then_inc(xl_ready, 1)

            def add_square(m, n, c0):
                dve.wait_ge(sq_ready, KD * m + n + 1)
                if n > 1:
                    dve.wait_ge(sq_added, (KD - 1) * m + n - 1)
                nc.vector.tensor_tensor(tmp[:, 3, c0:T], tmp[:, 3, c0:T], tmp[:, n % 3, c0:T], ALU.add).then_inc(sq_added, 1)

            def updates(m, x_only, update):
                c0 = M if x_only else 0
                for n in range(KD):
                    update(n)
                    if n > 1:
                        add_square(m, n - 1, c0)
                add_square(m, KD - 1, c0)

            def rsqrt(m, first):
                dve.wait_ge(std_ready, m + 1)
                nc.vector.reciprocal(rstd[:, first:5], std[:, first:5]).then_inc(rstd_ready, 1)

            def norm(m, v, gain, x_only):
                c0 = M if x_only else 0
                rsqrt(m, 1 if x_only else 0)
                dve.wait_ge(rb_done, m + 1)
                for n in range(KD):
                    if n >= 4:
                        dve.wait_ge(xl_ready, KD * v + n - 3)
                    if x_only:
                        nc.vector.scalar_tensor_tensor(tmp[:, n % 4, M:T], h[:, n, M:T], col(gain, n), ps[:, RB, :],
                                                       ALU.mult, ALU.mult).then_inc(normed, 1)
                    else:
                        nc.vector.scalar_tensor_tensor(halves(tmp[:, n % 4, :]), halves(h[:, n, :]), col(gain, n),
                                                       ps[:, RB:RB + 2, 0:HB], ALU.mult, ALU.mult).then_inc(normed, 1)
                    if n:
                        split_lo(v, n - 1, c0)
                split_lo(v, KD - 1, c0)

            def ffn_up(g, first, conv=False):
                with dve.Fori(0, F // UC) as i:
                    t0 = tile0(first) + 4 * i
                    if conv:
                        for j in range(2):
                            wc = lambda k: cols[:, 1, bass.ds(24 + FT * k + 2 * i + j, 1)]
                            t, r = column("ffn_conv_b_2")
                            bc = cols[:, t, bass.ds(r + 2 * i + j, 1)]
                            y, at_ = tmp[:, 2 + j, 0:S], tmp[:, j, :]
                            s0 = 6 * i + 3 * j
                            dve.wait_ge(conv_in, 2 * i + j + 1)
                            nc.vector.tensor_scalar(y, at_[:, M:T], wc(2), bc, ALU.mult, ALU.add).then_inc(conv_step, 1)
                            dve.wait_ge(conv_step, s0 + 1)
                            nc.vector.scalar_tensor_tensor(y, at_[:, M - 1:T - 1], wc(1), y, ALU.mult, ALU.add).then_inc(conv_step, 1)
                            dve.wait_ge(conv_step, s0 + 2)
                            nc.vector.scalar_tensor_tensor(y, at_[:, M - 2:T - 2], wc(0), y, ALU.mult, ALU.add).then_inc(conv_step, 1)
                    for j in range(2):
                        dve.wait_ge(gate_done, FT * g + 2 * i + j + 1)
                        dve.wait_ge(tiles_done, t0 + 2 + j + 1)
                        nc.vector.tensor_tensor(tmp[:, 2 + j, 0:S], tmp[:, j, M:T], ps[:, 4 + 2 * j if conv else 2 + j, :],
                                                ALU.mult).then_inc(prod_done, 1)
                        dve.wait_ge(acth_done, FT * g + 2 * i + j + 1)
                        nc.vector.tensor_tensor(act_l[:, bass.ds(2 * i + j, 1), :], tmp[:, 2 + j:3 + j, 0:S],
                                                act_h[:, bass.ds(2 * i + j, 1), :].bitcast(F32),
                                                ALU.subtract).then_inc(actl_done, 1)

            def ffn_down(first, scale, m=None):
                def add(n):
                    dve.wait_ge(tiles_done, used_count(first + 9) + n + 1)
                    nc.vector.scalar_tensor_tensor(h[:, n, M:T], ps[:, (n + 5) % 8, :], scale, h[:, n, M:T],
                                                   ALU.mult, ALU.add).then_inc(h_ready, 1)

                if m is None:
                    for n in range(KD):
                        add(n)
                else:
                    updates(m, True, add)

            dve.wait_ge(cols_ready, 3)
            for n in ("q_norm_nsa", "q_norm_fox"):
                nc.vector.tensor_scalar(col(n), col(n), HD ** -0.5, None, ALU.mult).then_inc(q_scaled, 1)
            t, r = column("lb_param_2")
            l0, l1 = cols[:, t, r:r + 8], cols[:, t, r + 8:r + 16]
            nc.vector.tensor_tensor(lbt[:, 2, :], l0, l1, ALU.max).then_inc(lb_step, 1)
            dve.wait_ge(lb_step, 1)
            nc.vector.tensor_tensor(lbt[:, 0:2, :], cols[:, t, r:r + 16].rearrange("p (a b) -> p a b", a=2),
                                    lbt[:, 2:3, :].to_broadcast([P, 2, 8]), ALU.subtract).then_inc(lb_step, 1)
            dve.wait_ge(lb_exp, 1)
            nc.vector.tensor_tensor(lbt[:, 2, :], lbt[:, 0, :], lbt[:, 1, :], ALU.add).then_inc(lb_step, 1)
            dve.wait_ge(lb_step, 3)
            nc.vector.reciprocal(lbt[:, 3, :], lbt[:, 2, :]).then_inc(lb_step, 1)
            dve.wait_ge(lb_step, 4)
            nc.vector.tensor_tensor(lb[:, 0, :], lbt[:, 0, :], lbt[:, 3, :], ALU.mult).then_inc(lb_step, 1)
            dve.wait_ge(lb_step, 5)
            nc.vector.tensor_scalar(lb[:, 1, :], lb[:, 0, :], -1.0, 1.0, ALU.mult, ALU.add).then_inc(p2_free, P2)
            updates(0, True, lambda n: None)
            norm(0, 0, "ffn1_norm", True)
            ffn_up(0, W_UP1)
            ffn_down(W_DN1, 0.5, 1)
            norm(1, 1, "mix_norm", True)
            dve.wait_ge(ustd, 1)
            nc.vector.reciprocal(rstd[:, 0:112], std[:, 0:112]).then_inc(urstd, 1)
            dve.wait_ge(q_scaled, 2)
            for n, t in enumerate(NORMED):
                gain = col("q_norm_nsa" if t < 4 else "k_norm_slc" if t == U_KS else "k_norm_win" if t == U_KW
                           else "q_norm_fox" if t < U_KF else "k_norm_fox")
                dve.wait_ge(urb, n + 1)
                nc.vector.scalar_tensor_tensor(uT[:, t, :], uT[:, t, :], gain, ps[:, n % 2, :], ALU.mult, ALU.mult).then_inc(unorm, 1)
            dve.wait_ge(const_in, 16 * N_CONST)
            for n, t in enumerate(ROPED):
                if t in NORMED:
                    dve.wait_ge(unorm, NORMED.index(t) + 1)
                nc.vector.tensor_tensor(tmp[:, n % 2, 0:S], uT[:, t, :], cosb[:], ALU.mult).then_inc(rope_step, 1)
                dve.wait_ge(urot, n + 1)
                nc.vector.tensor_tensor(tmp[:, 2 + n % 2, 0:S], ps[:, 4 + n % 2, :], sinb[:], ALU.mult).then_inc(rope_step, 1)
                dve.wait_ge(rope_step, 3 * n + 2)
                nc.vector.tensor_tensor(uT[:, t, :], tmp[:, n % 2, 0:S], tmp[:, 2 + n % 2, 0:S], ALU.add).then_inc(rope_step, 1)
            dve.wait_ge(u_ready, 11)
            nc.vector.tensor_scalar(flg[:, 2, :], gateT1[FL0:FL0 + NH, :], forget_b[FL0:FL0 + NH, 0:1], None, ALU.add).then_inc(fl_v, 1)
            dve.wait_ge(gate_mm, 1)
            dve.wait_ge(fl_v, 1)
            nc.vector.memset(hid[:], 0.0).then_inc(hid_zero, 1)
            nc.vector.scalar_tensor_tensor(flg[:, 0, :], flg[:, 2, :], -1.0, flg[:, 2, :], ALU.mult, ALU.min).then_inc(fl_v, 1)
            for n in range(2):
                kind = 1 - n
                dve.wait_ge(blk_cp, 4 * (n + 1))
                t, r = column("cmp_pos_v" if kind else "cmp_pos_k")
                pos = cols[:, t, r:r + 16].unsqueeze(2).to_broadcast([P, 16, NC])
                for g in range(NKV):
                    nc.vector.tensor_tensor(blk[:, kind, :, g, 0:NC], blk[:, kind, :, g, 0:NC], pos, ALU.add).then_inc(blk_ready, 1)
            dve.wait_ge(fl_step, 2)
            nc.vector.scalar_tensor_tensor(flg[:, 1, :], flg[:, 2, :], 0.0, flg[:, 0, :], ALU.min, ALU.subtract).then_inc(fl_v, 1)
            dve.wait_ge(fl_v, 3)
            nc.vector.tensor_tensor_scan(cum[:], ones1[0:8, 0:1].to_broadcast([8, S]), flg[:, 1, :], 0.0,
                                         ALU.mult, ALU.add).then_inc(fl_v, 1)
            dve.wait_ge(cmp_sq, 3)
            nc.vector.reciprocal(kcr[:], kcr[:]).then_inc(cmp_step, 1)
            dve.wait_ge(cmp_step, 1)
            nc.vector.scalar_tensor_tensor(kcmp[:], ps[:, 6, 256:320], col("k_norm_cmp"), kcr[:], ALU.mult, ALU.mult).then_inc(cmp_step, 1)
            dve.wait_ge(g_ready, 1)
            for i in range(TT):
                gc = gsig[:, i, :].rearrange("p (n c) -> p n c", c=3)[:, :, 0]
                nc.vector.tensor_scalar(gc, gc, cmprow[:, i:i + 1], None, ALU.mult).then_inc(gc_ready, 1)
            dve.wait_ge(gc_ready, TT)
            dve.wait_ge(fl_v, 4)

            def attention(n0, steps, fox):
                NS = len(steps)
                with dve.Fori(0, 2) as it:
                    s0 = n0 + NS * it
                    t0 = 3 * n0 + 3 * NS * it
                    if fox:
                        for hh in range(4):
                            nc.vector.tensor_scalar(cst[:, hh, :], cum[:], ident[0:8, bass.ds(4 * it + hh, 1)], None,
                                                    ALU.mult).then_inc(c_staged, 1)
                    for s in range(NS + 2):
                        if s < NS:
                            hh, i, b = steps[s]
                            n = 32 if b == 2 else (i + 1) * P
                            dve.wait_ge(score_done, s0 + s + 1)
                            nc.vector.tensor_reduce(stat[:, 0, s % 4:s % 4 + 1], ps[:, s % 3, 0:n], AX_X, ALU.max,
                                                    negate=True).then_inc(nmax_done, 1)
                        if s >= 2:
                            q = s - 2
                            hh, i, b = steps[q]
                            dve.wait_ge(exp_done, s0 + q + 1)
                            rc, rg = stat[:, 2, q % 4:q % 4 + 1], stat[:, 3, q % 4:q % 4 + 1]
                            nc.vector.reciprocal(rc, stat[:, 1, q % 4:q % 4 + 1]).then_inc(o_step, 1)
                            dve.wait_ge(o_step, 2 * (s0 + q) + 1)
                            if fox:
                                nc.vector.tensor_copy(rg, rc).then_inc(o_step, 1)
                            else:
                                gate = gsig[:, i, bass.ds(12 * it + 3 * hh + GATE_OF[b], 1)]
                                nc.vector.tensor_tensor(rg, rc, gate, ALU.mult).then_inc(o_step, 1)
                            dve.wait_ge(o_step, 2 * (s0 + q) + 2)
                            dve.wait_ge(pv_done, s0 + q + 1)
                            o = otok[:, i, bass.ds((S if fox else 0) + 4 * HD * it + HD * hh, HD)]
                            if b == 0:
                                nc.vector.tensor_scalar(o, ps[:, 6 + q % 2, 0:HD], rg, None, ALU.mult).then_inc(o_done, 1)
                            else:
                                dve.wait_ge(o_done, s0 + q)
                                nc.vector.scalar_tensor_tensor(o, ps[:, 6 + q % 2, 0:HD], rg, o, ALU.mult, ALU.add).then_inc(o_done, 1)

            attention(0, NSA_STEPS, False)
            attention(2 * len(NSA_STEPS), FOX_STEPS, True)
            dve.wait_ge(ostd, 1)
            nc.vector.reciprocal(rstd[:, 0:8], std[:, 0:8]).then_inc(orstd, 1)
            dve.wait_ge(orstd, 1)
            for n in range(2 * TT):
                o = otok[:, n // 2, n % 2 * S:(n % 2 + 1) * S]
                nc.vector.tensor_scalar(o, o, rstd[:, n:n + 1], None, ALU.mult).then_inc(oscaled, 1)
            for n in range(KD):
                split_lo(2, n, M)

            def add_attention(n):
                dve.wait_ge(tiles_done, tile0(W_OUT1) + n + 1)
                nc.vector.tensor_tensor(h[:, n, M:T], h[:, n, M:T], ps[:, n % 4, :], ALU.add).then_inc(h_ready, 1)

            updates(2, True, add_attention)
            norm(2, 3, "ffn2_norm", True)
            ffn_up(1, W_UP2)
            ffn_down(W_DN2, 0.5, 3)
            norm(3, 4, "ple_gate_norm", True)
            for e in range(2):
                dve.wait_ge(ph_ready, e + 1)
                nc.vector.tensor_tensor(p_l[:, e, :], ps[:, 4 + e, :], p_h[:, e, :].bitcast(F32), ALU.subtract).then_inc(pl_ready, 1)
            updates(4, True, lambda n: None)
            rsqrt(4, 1)
            dve.wait_ge(rb_done, 5)

            def add_embedding(n):
                t = eT[:, n, :]
                nc.vector.scalar_tensor_tensor(t, t, col("ple_norm", n), ps[:, RB, :], ALU.mult, ALU.mult).then_inc(e_step, 1)
                dve.wait_ge(e_step, 2 * n + 1)
                nc.vector.tensor_tensor(t, t, gateT[:, n, :], ALU.mult).then_inc(e_step, 1)
                dve.wait_ge(e_step, 2 * n + 2)
                nc.vector.tensor_tensor(h[:, n, M:T], h[:, n, M:T], t, ALU.add).then_inc(h_ready, 1)

            updates(5, False, add_embedding)
            norm(5, 5, "attn_norm_w_2", False)

            def bank2(j):
                return ps[:, 2 * j:2 * j + 2, 0:HB]

            def tile_of(buf, i, j):
                return buf[:, bass.ds(2 * i + j, 1), :].rearrange("p a (b c) -> p (a b) c", b=2)

            t2 = [halves(tmp[:, j, :]) for j in range(4)]
            for n in range(4):
                s1 = 4 * (2, 1, 1, 1)[n]
                with dve.Fori(0, 4) as i:
                    t0 = tile0(W_IN2) + 16 * n + 4 * i
                    f0 = P2 + 16 * n + 4 * i
                    if n == 0:
                        for j in range(2):
                            dve.wait_ge(sig_done, 4 * i + j + 1)
                            nc.vector.tensor_tensor(tile_of(Q, i, j), bank2(j), t2[j], ALU.mult).then_inc(p2_free, 1)
                        for j in range(2):
                            dve.wait_ge(sig_done, 4 * i + j + 3)
                            nc.vector.tensor_scalar(Fg[:, bass.ds(2 * i + j, 1), :], tmp[:, 2 + j:3 + j, :], lb[:, 1, bass.ds(2 * i + j, 1)],
                                                    lb[:, 0, bass.ds(2 * i + j, 1)], ALU.mult, ALU.add).then_inc(p2_free, 1)
                    if n == 1:
                        for j in range(2):
                            dve.wait_ge(sig_done, 16 + 4 * i + j + 1)
                            nc.vector.tensor_tensor(t2[j], bank2(j), t2[j], ALU.mult).then_inc(p2_free, 1)
                        for j in range(2):
                            dve.wait_ge(sig_done, 16 + 4 * i + j + 3)
                            dve.wait_ge(p2_free, f0 + j + 1)
                            nc.vector.tensor_tensor(GA[:, bass.ds(2 * i + j, 1), :], tmp[:, j:j + 1, :], tmp[:, 2 + j:3 + j, :], ALU.mult).then_inc(p2_free, 1)
                    if n == 2:
                        for j in range(2):
                            wc = lambda k: cols[:, 1, bass.ds(8 * k + 2 * i + j, 1)]
                            y = YB[:, bass.ds(2 * i + j, 1), :]
                            cx = tmp[:, j:j + 1, :]
                            dve.wait_ge(sig_done, 32 + 2 * i + j + 1)
                            dve.wait_ge(tiles_done, t0 + 2 + j + 1)
                            nc.vector.tensor_tensor(t2[j], t2[j], bank2(2 + j), ALU.mult).then_inc(p2_step, 1)
                            s0 = 6 * i + 3 * j
                            dve.wait_ge(p2_step, s0 + 1)
                            nc.vector.tensor_scalar(y, cx, wc(2), None, ALU.mult).then_inc(p2_step, 1)
                            dve.wait_ge(p2_step, s0 + 2)
                            y1 = YB[:, bass.ds(2 * i + j, 1), 1:T]
                            nc.vector.scalar_tensor_tensor(y1, tmp[:, j:j + 1, 0:T - 1], wc(1), y1, ALU.mult, ALU.add).then_inc(p2_step, 1)
                            dve.wait_ge(p2_step, s0 + 3)
                            y2 = YB[:, bass.ds(2 * i + j, 1), 2:T]
                            nc.vector.scalar_tensor_tensor(y2, tmp[:, j:j + 1, 0:T - 2], wc(0), y2, ALU.mult, ALU.add).then_inc(p2_free, 2)
                    if n == 3:
                        for j in range(2):
                            dve.wait_ge(tiles_done, t0 + j + 1)
                            nc.vector.tensor_tensor(tile_of(YB, i, j), tile_of(YB, i, j), bank2(j), ALU.mult).then_inc(p2_free, 1)
                        for j in range(2):
                            dve.wait_ge(sig_done, 40 + 2 * i + j + 1)
                            dve.wait_ge(p2_free, f0 + j + 1)
                            nc.vector.tensor_tensor(YB[:, bass.ds(2 * i + j, 1), :], YB[:, bass.ds(2 * i + j, 1), :], tmp[:, 2 + j:3 + j, :], ALU.mult).then_inc(p2_free, 1)

            dve.wait_ge(tiles_done, used_count(W_IN2 + 35))
            dve.wait_ge(p2_free, P2 + 64)
            up_n = [0]

            def link(ins):
                up_n[0] += 1
                ins.then_inc(lev_up, 1)
                dve.wait_ge(lev_up, up_n[0])

            link(nc.vector.tensor_scalar(K[:], Fg[:], -1.0, 1.0, ALU.mult, ALU.add))
            nc.vector.memset(Ad[:], 0.0).then_inc(az, 1)
            nc.vector.memset(Am[:], 0.0).then_inc(az, 1)
            dve.wait_ge(az, 2)
            idx = 0
            for lv in range(-1, LEVELS):
                while idx < len(LEVEL_SEQ) and LEVEL_SEQ[idx][0] == lv:
                    _, n, bank = LEVEL_SEQ[idx]
                    dve.wait_ge(lev_mm, idx + 1)
                    if lv < 7:
                        if n == META:
                            nc.vector.copy_predicated(Am[:], levelmask[0:M, lv + 1, 0:M].unsqueeze(1).to_broadcast([M, VH, M]),
                                                      ps[0:M, bank, 0:VH * M].rearrange("p (n m) -> p n m", n=VH)).then_inc(lev_sel, 1)
                        else:
                            nc.vector.copy_predicated(Ad[:, n, :].rearrange("p (i t) -> p i t", i=TT),
                                                      levelmask[:, lv + 1, :].unsqueeze(1).to_broadcast([P, TT, P]),
                                                      ps[:, bank, :].rearrange("p (i t) -> p i t", i=TT)).then_inc(lev_sel, 1)
                    idx += 1
                if lv == -1:
                    link(nc.vector.tensor_tensor(Q[:], Q[:], Fg[:], ALU.mult))
                    continue
                H = 1 << lv
                nb = S // (2 * H)
                def pairs(buf, lo_, hi_, w):
                    return buf[:, :, lo_:hi_].rearrange("p n (b e w) -> p n b e w", e=2, w=w)
                if lv == 0:
                    tot = pairs(Fg, M, T, 1)[:, :, :, :, 0]
                else:
                    src = Tod if lv % 2 else Tev
                    tot = src[:, 0:VH * 2 * nb].rearrange("p (n b e) -> p n b e", n=VH, e=2)
                nxt = (Tev if lv % 2 else Tod)[:, 0:VH * nb].rearrange("p (n b) -> p n b", n=VH)
                q2 = pairs(Q, M, T, H)[:, :, :, 1, :]
                link(nc.vector.tensor_tensor(q2, q2, tot[:, :, :, 0].unsqueeze(3).to_broadcast([P, VH, nb, H]), ALU.mult))
                if lv < LEVELS - 1:
                    k2 = pairs(K, M, T, H)[:, :, :, 0, :]
                    link(nc.vector.tensor_tensor(k2, k2, tot[:, :, :, 1].unsqueeze(3).to_broadcast([P, VH, nb, H]), ALU.mult))
                    link(nc.vector.tensor_tensor(nxt, tot[:, :, :, 0], tot[:, :, :, 1], ALU.mult))
                if H < M:
                    mb = M // (2 * H)
                    mt = pairs(Fg, 0, M, 1)[:, :, :, :, 0] if lv == 0 else \
                        ttm[:, lv % 2, :, 0:2 * mb].rearrange("p n (b e) -> p n b e", e=2)
                    mk = pairs(K, 0, M, H)[:, :, :, 0, :]
                    link(nc.vector.tensor_tensor(mk, mk, mt[:, :, :, 1].unsqueeze(3).to_broadcast([P, VH, mb, H]), ALU.mult))
                    if 2 * H < M:
                        mq = pairs(Q, 0, M, H)[:, :, :, 1, :]
                        link(nc.vector.tensor_tensor(mq, mq, mt[:, :, :, 0].unsqueeze(3).to_broadcast([P, VH, mb, H]), ALU.mult))
                        link(nc.vector.tensor_tensor(ttm[:, (lv + 1) % 2, :, 0:mb], mt[:, :, :, 0], mt[:, :, :, 1], ALU.mult))
                assert up_n[0] == LEVEL_UP[lv + 1], (lv, up_n[0])
            dve.wait_ge(hstd, 1)
            nc.vector.reciprocal(rstd[:, 0:40], std[:, 0:40]).then_inc(hrstd, 1)
            for n in range(KD):
                t = halves(tmp[:, n % 4, :])
                if n >= 4:
                    dve.wait_ge(xl_ready, 6 * KD + n - 3)
                dve.wait_ge(hrb, n + 1)
                b0 = 6 if n % 2 == 0 else 2
                nc.vector.scalar_tensor_tensor(t, halves(Q[:, n, :]), col("hgrn_norm_w_2"), ps[:, b0:b0 + 2, 0:HB],
                                               ALU.mult, ALU.mult).then_inc(h2_step, 1)
                dve.wait_ge(h2_step, 2 * n + 1)
                nc.vector.tensor_tensor(tmp[:, n % 4, :], tmp[:, n % 4, :], GA[:, n, :], ALU.mult).then_inc(h2_step, 1)
                dve.wait_ge(h2_step, 2 * n + 2)
                nc.vector.tensor_tensor(tmp[:, n % 4, :], tmp[:, n % 4, :], YB[:, n, :], ALU.add).then_inc(normed, 1)
                if n:
                    split_lo(6, n - 1, 0)
            split_lo(6, KD - 1, 0)

            def add_mixed(n):
                dve.wait_ge(tiles_done, tile0(W_OUT2) + n + 1)
                nc.vector.tensor_tensor(halves(h[:, n, :]), halves(h[:, n, :]), bank2(n % 4), ALU.add).then_inc(h_ready, 1)

            updates(6, False, add_mixed)
            norm(6, 7, "ffn_norm_w_2", False)
            ffn_up(2, W_UP3, conv=True)
            ffn_down(W_DN3, 1.0)
            dve.wait_ge(fsq, 2 * TT)
            sums = rstd[:, 0:2 * TT].rearrange("p (i e) -> p i e", e=2)
            nc.vector.tensor_tensor(std[:, 8:8 + TT], sums[:, :, 0], sums[:, :, 1], ALU.add).then_inc(fsum, 1)
            dve.wait_ge(fstd, 1)
            nc.vector.reciprocal(rstd[:, 8:8 + TT], std[:, 0:TT]).then_inc(frstd, 1)
            dve.wait_ge(frstd, 1)
            dve.wait_ge(gain_in, 16)
            for n in range(2 * TT):
                i, e = n // 2, n % 2
                nc.vector.scalar_tensor_tensor(y_tok[:, i, e * S:(e + 1) * S], ps[:, n, :], rstd[:, 8 + i:9 + i],
                                               gainb[:, e * S:(e + 1) * S], ALU.mult, ALU.mult).then_inc(f_ready, 1)
        @block.tensor
        def _(pe):
            mm = nc.tensor.matmul

            def tile_mm(j, e, slot, xs, splits, banks, ready=None):
                wh, wl = w_view(whi, slot, KD), w_view(wlo, slot, KD)
                for k in range(KD):
                    if ready is not None:
                        pe.wait_ge(xl_ready, KD * ready + k + 1)
                    for q, (w, x) in enumerate(((wh, xs[0]), (wl, xs[0]), (wh, xs[1]))):
                        for c0, n, b in splits:
                            last = mm(ps[:, j * banks + b, 0:n], w[:, k, e * P:(e + 1) * P], x[:, k, c0:c0 + n],
                                      start=(k == 0 and q == 0), stop=(k == KD - 1 and q == 2))
                last.then_inc(tiles_done, 1)

            X = (xh, xl)

            def pair(u, p, free, ready=None, banks=1, splits=(WHOLE, WHOLE)):
                for half in range(2):
                    pe.wait_ge(lo_ready, u + half + 1)
                    for e in range(2):
                        j = 2 * half + e
                        if free is not None:
                            free(j)
                        tile_mm(j, e, (p + half) % 2, X, splits[half], banks, ready if j == 0 else None)

            def norm_stats(m, x_only):
                c0s = [0] * (not x_only) + [M + i * P for i in range(TT)]
                f = 1 if x_only else 0
                pe.wait_ge(sq_added, (KD - 1) * (m + 1))
                for i, c0 in enumerate(c0s):
                    last = mm(ps[:, SSQ, f + i:f + i + 1], tmp[:, 3, c0:c0 + P], ones1[:], start=True, stop=True)
                last.then_inc(ssq_done, 1)
                pe.wait_ge(rstd_ready, m + 1)
                spread(lambda i: rstd[:, i:i + 1], x_only, RB).then_inc(rb_done, 1)

            def spread(colof, x_only, bank):
                if x_only:
                    for i in range(TT):
                        last = mm(ps[:, bank, i * P:(i + 1) * P], colof(1 + i).to_broadcast([P, P]), ident[:], start=True, stop=True)
                    return last
                mm(ps[:, bank, 0:M], colof(0)[0:M].to_broadcast([M, P]), ident[0:M, 0:M], start=True, stop=True)
                for i in range(TT):
                    c = M + i * P
                    while c < M + (i + 1) * P:
                        b = c // HB
                        end = min(M + (i + 1) * P, (b + 1) * HB)
                        at_ = c - M - i * P
                        last = mm(ps[:, bank + b, c - b * HB:end - b * HB], colof(1 + i).to_broadcast([P, P]),
                                  ident[:, at_:at_ + end - c], start=True, stop=True)
                        c = end
                return last

            def ffn_up(g, v, first, conv=False):
                s = first % 2
                splits = (CONV, WHOLE) if conv else (WHOLE, WHOLE)
                banks = 2 if conv else 1

                def step(i, free, ready=None):
                    pair(first + 2 * i, s, free, ready, banks, splits)

                step(0, None, v)
                with pe.Fori(1, F // UC) as i:
                    def free(j):
                        if j < 2:
                            pe.wait_ge(conv_in if conv else gate_done, (0 if conv else FT * g) + 2 * i + j - 1)
                        else:
                            pe.wait_ge(prod_done, FT * g + 2 * i + j - 3)
                    step(i, free)

            def ffn_down(g, first):
                s = first % 2

                def unit(u, slot, k, start=False, stop=False):
                    pe.wait_ge(lo_ready, u + 1)
                    pe.wait_ge(actl_done, FT * g + k + 2)
                    wh, wl = w_view(whi, slot, 2), w_view(wlo, slot, 2)
                    for n in range(KD):
                        for e in range(2):
                            for q, (w, x) in enumerate(((wh, act_h), (wl, act_h), (wh, act_l))):
                                last = mm(ps[:, (n + 5) % 8, :], w[:, e, n * P:(n + 1) * P],
                                          x[:, bass.ds(k + e, 1), :].rearrange("p a s -> p (a s)"),
                                          start=(start and e == 0 and q == 0), stop=(stop and e == 1 and q == 2))
                        if stop:
                            last.then_inc(tiles_done, 1)
                    if not stop:
                        last.then_inc(tiles_done, 2)

                pe.wait_ge(prod_done, FT * (g + 1))
                unit(first, s, 0, start=True)
                with pe.Fori(0, 4) as i:
                    for e in range(2):
                        unit(first + 1 + 2 * i + e, (s + 1 + e) % 2, 4 * i + 2 + 2 * e)
                unit(first + 9, (s + 9) % 2, 18)
                unit(first + 10, s, 20, stop=True)

            def square(first, v, ready, w, banks=1, splits=(WHOLE, WHOLE)):
                for i in range(2):
                    pair(first + 2 * i, first % 2,
                         (lambda j: pe.wait_ge(ready, w + j + 1)) if i else None, v if i == 0 else None, banks, splits)

            pe.wait_ge(ident_in, 16)
            pe.wait_ge(rows_in, 16 * N_ROWS)
            for t in range(3):
                nc.tensor.transpose(ps[:, t, 0:NROWS[t]], rows_t[0:NROWS[t], t, :], ident[0:NROWS[t], 0:NROWS[t]]).then_inc(colsT, 1)
            pe.wait_ge(x_in, 16 * (TT + 1))
            for n in range(KD):
                last = nc.tensor.transpose(ps[:, 3, n * M:(n + 1) * M], meta_tok[:, n * P:(n + 1) * P], ident[0:M, 0:M])
            last.then_inc(tiles_done, 1)
            for n in range(KD):
                b = (n + 4) % 8
                if b < 3:
                    pe.wait_ge(cols_ready, b + 1)
                if b == 3:
                    pe.wait_ge(meta_ready, 1)
                for i in range(TT):
                    last = nc.tensor.transpose(ps[:, b, i * P:(i + 1) * P], x_tok[:, i, n * P:(n + 1) * P], ident[:])
                last.then_inc(xT, 1)
            pe.wait_ge(setup, 3)
            norm_stats(0, True)
            ffn_up(0, 0, W_UP1)
            ffn_down(0, W_DN1)
            norm_stats(1, True)
            s = W_IN1 % 2
            pair(W_IN1, s, None, 1)
            pair(W_IN1 + 2, s, lambda j: pe.wait_ge(u_ready, j + 1))
            pe.wait_ge(lo_ready, W_IN1 + 5)
            for e in range(2):
                pe.wait_ge(u_ready, 4 + e + 1)
                tile_mm(e, e, s, X, WHOLE, 1)
            pe.wait_ge(lo_ready, GATE_UNIT + 1)
            pe.wait_ge(u_ready, 7)
            gh, gl = [w[:, 1 - s, 0:KD * P].rearrange("p (k n) -> p k n", k=KD) for w in (whi, wlo)]
            for k in range(KD):
                for q, (w, x) in enumerate(((gh, xh), (gl, xh), (gh, xl))):
                    last = mm(ps[:, 2, :], w[:, k, :], x[:, k, M:T], start=(k == 0 and q == 0), stop=(k == KD - 1 and q == 2))
            last.then_inc(tiles_done, 2)
            pe.wait_ge(u_ready, 11)
            with pe.Fori(0, 3) as i:
                pair(W_IN1 + 6 + 2 * i, s, lambda j: pe.wait_ge(u_ready, 8 + 4 * i + j))
            pe.wait_ge(const_in, 16 * N_CONST)
            two = headones[:, 0:P:HD]
            for n in range(len(NORMED)):
                pe.wait_ge(usq, n + 1)
                for i in range(TT):
                    last = mm(ps[:, 7, 28 * i + 2 * n:28 * i + 2 * n + 2], tmp[:, n % 4, i * P:(i + 1) * P], two, start=True, stop=True)
                last.then_inc(ussq, 1)
            pe.wait_ge(urstd, 1)
            for i in range(TT):
                last = nc.tensor.transpose(ps[:, 7, i * 24:(i + 1) * 24], gateT1[0:24, i * P:(i + 1) * P], ident[0:24, 0:24])
            last.then_inc(gate_mm, 1)

            def turned(n):
                t = ROPED[n]
                if t in NORMED:
                    pe.wait_ge(unorm, NORMED.index(t) + 1)
                if n >= 2:
                    pe.wait_ge(rope_step, 3 * n - 4)
                mm(ps[:, 4 + n % 2, :], rot[:], uT[:, t, :], start=True, stop=True).then_inc(urot, 1)

            for n in range(len(NORMED)):
                if n >= 2:
                    pe.wait_ge(unorm, n - 1)
                for i in range(TT):
                    for e in range(2):
                        c = 28 * i + 2 * n + e
                        last = mm(ps[e * HD:(e + 1) * HD, n % 2, i * P:(i + 1) * P], rstd[:, c:c + 1].to_broadcast([P, HD]), ident[:],
                                  start=True, stop=True)
                last.then_inc(urb, 1)
            for n in range(len(ROPED)):
                turned(n)
            pe.wait_ge(cmp_in, 64)
            for n in range(2):
                kind = 1 - n
                pe.wait_ge(blk_ready, 2 * (n + 1))
                for mt in range(2):
                    q = 2 * n + mt
                    for kt in range(16):
                        last = mm(ps[:, q, 0:NKV * NC], w1[:, kind, kt, mt * P:(mt + 1) * P], blk[:, kind, kt, :, 0:NC],
                                  start=(kt == 0), stop=(kt == 15))
                    last.then_inc(hid_mm, 1)
            pe.wait_ge(hid_ready, 4)
            for e in range(2):
                for kt in range(2):
                    last = mm(ps[e * HD:(e + 1) * HD, 6, 256:320], w2[:, 0, kt, :],
                              hid[:, 0, kt, :, :].rearrange("p g n -> p (g n)"), start=(kt == 0), stop=(kt == 1))
            last.then_inc(cmp_mm, 1)
            for g in range(NKV):
                for kt in range(2):
                    last = mm(ps[0:32, 6, 320 + 64 * g:384 + 64 * g], hid[:, 1, kt, g, :], w2[:, 1, kt, :], start=(kt == 0), stop=(kt == 1))
                last.then_inc(cmp_mm, 1)
            pe.wait_ge(cmp_sq, 2)
            mm(ps[:, 6, 448:512], headones[:], kcsq[:], start=True, stop=True).then_inc(cmp_mm, 1)
            for n, t in enumerate((U_VS, U_VW, U_VF, U_VF + 1, U_VF + 2, U_VF + 3)):
                if n >= 2:
                    pe.wait_ge(v_ready, n - 1)
                for i in range(TT):
                    last = nc.tensor.transpose(ps[:, 2 + n % 2, i * P:(i + 1) * P], uT[:, t, i * P:(i + 1) * P], ident[:])
                last.then_inc(vtr, 1)
            pe.wait_ge(v_ready, 6)
            pe.wait_ge(kdup, 8)
            pe.wait_ge(cmp_step, 2)
            pe.wait_ge(fl_v, 4)

            def attention(n0, steps, fox):
                NS = len(steps)
                with pe.Fori(0, 2) as it:
                    s0 = n0 + NS * it
                    pe.wait_ge(q_staged, (10 + 4 * it + 4) if fox else (5 * it + 4))
                    if fox:
                        pe.wait_ge(c_staged, 4 * it + 4)
                    for s in range(NS + 2):
                        if s < NS:
                            hh, i, b = steps[s]
                            d = slice(hh % 2 * HD, hh % 2 * HD + HD)
                            q = qst[d, hh // 2, i * P:(i + 1) * P]
                            n = (i + 1) * P
                            if s >= 3:
                                pe.wait_ge(exp_done, s0 + s - 2)
                            if fox:
                                mm(ps[:, s % 3, n - P:n], ident[:], causal[:], start=True, stop=False, skip_group_check=True)
                                mm(ps[:, s % 3, 0:n], negones[:], cst[:, hh, 0:n], start=False, stop=False, skip_group_check=True)
                                last = mm(ps[:, s % 3, 0:n], q, kst[d, hh // 2, 0:n], start=False, stop=True, skip_group_check=True)
                            elif b == 2:
                                mm(ps[:, s % 3, 0:32], ident[:], cmpneg[:, i, :], start=True, stop=False, skip_group_check=True)
                                last = mm(ps[:, s % 3, 0:32], q, kcst[d, :], start=False, stop=True, skip_group_check=True)
                            else:
                                mm(ps[:, s % 3, n - P:n], ident[:], causal[:], start=True, stop=False, skip_group_check=True)
                                last = mm(ps[:, s % 3, 0:n], q, kst[d, b, 0:n], start=False, stop=True, skip_group_check=True)
                            last.then_inc(score_done, 1)
                        if 1 <= s <= NS:
                            q_ = s - 1
                            hh, i, b = steps[q_]
                            pe.wait_ge(exp_done, s0 + q_ + 1)
                            if q_ >= 3:
                                pe.wait_ge(ptev_done, s0 + q_ - 2)
                            if b == 2:
                                last = nc.tensor.transpose(ps[0:32, 3 + q_ % 3, 0:P], prob[:, q_ % 3, 0:32], ident[:])
                            else:
                                for k in range(i + 1):
                                    last = nc.tensor.transpose(ps[:, 3 + q_ % 3, k * P:(k + 1) * P], prob[:, q_ % 3, k * P:(k + 1) * P], ident[:])
                            last.then_inc(trans_done, 1)
                        if s >= 2:
                            q_ = s - 2
                            hh, i, b = steps[q_]
                            pe.wait_ge(ptev_done, s0 + q_ + 1)
                            if q_ >= 2:
                                pe.wait_ge(o_done, s0 + q_ - 1)
                            o = ps[:, 6 + q_ % 2, 0:HD]
                            if q_ == 2 and not fox:
                                pe.wait_ge(q_staged, 5 * it + 5)
                            if b == 2:
                                last = mm(o, probT[0:32, q_ % 3, 0, :], vcst[:], start=True, stop=True)
                            else:
                                for k in range(i + 1):
                                    v = bass.ds(2 * P + 4 * HD * it + HD * hh, HD) if fox else bass.ds(b * P + HD * it, HD)
                                    last = mm(o, probT[:, q_ % 3, k, :], vtok[:, k, v], start=(k == 0), stop=(k == i))
                            last.then_inc(pv_done, 1)

            attention(0, NSA_STEPS, False)
            attention(2 * len(NSA_STEPS), FOX_STEPS, True)
            pe.wait_ge(oscaled, 2 * TT)
            for n in range(KD):
                if n >= 4:
                    pe.wait_ge(normed, 2 * KD + n - 3)
                for i in range(TT):
                    last = nc.tensor.transpose(ps[:, 4 + n % 4, i * P:(i + 1) * P], otok[:, i, n * P:(n + 1) * P], ident[:])
                last.then_inc(otr, 1)
            square(W_OUT1, 2, h_ready, 2 * KD)
            norm_stats(2, True)
            ffn_up(1, 3, W_UP2)
            ffn_down(1, W_DN2)
            norm_stats(3, True)
            square(W_PLG, 4, gate_ready, 0)
            pe.wait_ge(p_in, 16)
            for e in range(2):
                for i in range(TT):
                    last = nc.tensor.transpose(ps[:, 4 + e, i * P:(i + 1) * P], p_tok[:, i, e * P:(e + 1) * P], ident[:])
                last.then_inc(pT_done, 1)
            pe.wait_ge(lo_ready, W_PLP + 1)
            pe.wait_ge(pl_ready, 2)
            pe.wait_ge(gate_ready, KD)
            wh, wl = w_view(whi, W_PLP % 2, 2), w_view(wlo, W_PLP % 2, 2)
            for n in range(KD):
                for k in range(2):
                    for q, (w, x) in enumerate(((wh, p_h), (wl, p_h), (wh, p_l))):
                        last = mm(ps[:, (n + 6) % 8, :], w[:, k, n * P:(n + 1) * P], x[:, k, :], start=(k == 0 and q == 0), stop=(k == 1 and q == 2))
                last.then_inc(tiles_done, 1)
            pe.wait_ge(e_ready, KD)
            norm_stats(4, True)
            norm_stats(5, False)
            s = W_IN2 % 2
            for n in range(4):
                need = (2, 4, 2, 4) if n == 2 else (1, 2, 3, 4)

                def step(i, ready):
                    pair(W_IN2 + 8 * n + 2 * i, s, lambda j: pe.wait_ge(p2_free, P2 + 16 * n + 4 * i - 4 + need[j]), ready, 2, (BOTH, BOTH))

                if n == 0:
                    step(0, 5)
                with pe.Fori(1 if n == 0 else 0, 4) as i:
                    if n:
                        pe.wait_ge(p2_free, P2 + 16 * n)
                    step(i, None)
            pe.wait_ge(p2_free, P2 + 64)
            for u in range(4):
                pe.wait_ge(lo_ready, W_IN2 + 32 + u + 1)
                if u >= 2:
                    pe.wait_ge(vev, u - 1)
                slot = (s + u) % 2
                wh, wl = w_view(whi, slot, KD), w_view(wlo, slot, KD)
                for g in range(TT + 1):
                    c0 = 0 if g == 0 else M + (g - 1) * P
                    for k in range(KD):
                        for q, (w, x) in enumerate(((wh, xh), (wl, xh), (wh, xl))):
                            last = mm(ps[:, 3 * (u % 2) + g // 2, g % 2 * UC:(g % 2 + 1) * UC], x[:, k, c0:c0 + P], w[:, k, :],
                                      start=(k == 0 and q == 0), stop=(k == KD - 1 and q == 2))
                last.then_inc(tiles_done, 2)
            pe.wait_ge(vev, 4)
            last_user = {}
            for idx, (lv, n, bank) in enumerate(LEVEL_SEQ):
                pe.wait_ge(lev_up, 1 if lv < 0 else LEVEL_UP[lv])
                if bank in last_user:
                    was, at_lv = last_user[bank]
                    if at_lv < 7:
                        pe.wait_ge(lev_sel, was + 1)
                    else:
                        pe.wait_ge(lev_cp, was + 1 - LEVEL_CP0)
                last_user[bank] = (idx, lv)
                xc = lambda i, k=1: slice(M + i * P, M + (i + k) * P)
                if n == META:
                    for m in range(VH):
                        last = mm(ps[0:M, bank, m * M:(m + 1) * M], K[:, m, 0:M], Q[:, m, 0:M], start=True, stop=True)
                elif lv < 7:
                    for i in range(TT):
                        last = mm(ps[:, bank, i * P:(i + 1) * P], K[:, n, xc(i)], Q[:, n, xc(i)], start=True, stop=True)
                elif lv == 7:
                    for i in range(2):
                        last = mm(ps[:, bank, i * P:(i + 1) * P], K[:, n, xc(2 * i)], Q[:, n, xc(2 * i + 1)], start=True, stop=True)
                else:
                    for i in range(2):
                        last = mm(ps[:, bank, i * 2 * P:(i + 1) * 2 * P], K[:, n, xc(i)], Q[:, n, xc(2, 2)], start=True, stop=True)
                last.then_inc(lev_mm, 1)
            pe.wait_ge(lev_up, LEVEL_UP[LEVELS])
            pe.wait_ge(lev_cp, 2 * VH)
            pe.wait_ge(lev_sel, LEVEL_CP0)
            for n in range(VH):
                f = slice(n * P, (n + 1) * P)
                if n >= 2:
                    pe.wait_ge(amx_cp, n - 1)
                mm(ps[0:M, n % 2, :], K[:, n, 0:M], Q[:, n, M:T], start=True, stop=True).then_inc(amx_mm, 1)
                pe.wait_ge(amx_cp, n + 1)
                if n >= 2:
                    pe.wait_ge(o2_cp, n - 1)
                o = ps[:, 2 + n % 2, :]
                for i in range(TT):
                    mm(o[:, i * P:(i + 1) * P], V[:, 1 + i, f], Ad[:, n, i * P:(i + 1) * P], start=(i == 0), stop=False, skip_group_check=True)
                for i in range(2):
                    mm(o[:, (2 * i + 1) * P:(2 * i + 2) * P], V[:, 1 + 2 * i, f], Tod[:, 64 + n * 256 + i * P:64 + n * 256 + (i + 1) * P],
                       start=False, stop=False, skip_group_check=True)
                for i in range(2):
                    mm(o[:, 2 * P:4 * P], V[:, 1 + i, f], Tev[:, 128 + n * 512 + i * 256:128 + n * 512 + (i + 1) * 256],
                       start=False, stop=False, skip_group_check=True)
                mm(o, V[0:M, 0, f], Amx[:, n % 2, :], start=False, stop=True, skip_group_check=True)
                mm(ps[:, 4, n * M:(n + 1) * M], V[0:M, 0, f], Am[:, n, :], start=True, stop=True).then_inc(o2_mm, 1)
            for n in range(VH):
                pe.wait_ge(hsq, n + 1)
                for i in range(TT + 1):
                    c0 = 0 if i == 0 else M + (i - 1) * P
                    last = mm(ps[:, 5, n * 5 + i:n * 5 + i + 1], tmp[:, n % 4, c0:c0 + P], ones1[:], start=True, stop=True)
                last.then_inc(hssq, 1)
            pe.wait_ge(hrstd, 1)
            for n in range(VH):
                if n >= 2:
                    pe.wait_ge(h2_step, 2 * (n - 2) + 1)
                spread(lambda i: rstd[:, n * 5 + i:n * 5 + i + 1], False, 6 if n % 2 == 0 else 2).then_inc(hrb, 1)
            pe.wait_ge(h2_step, 2 * VH)
            square(W_OUT2, 6, h_ready, 5 * KD, 2, (BOTH, BOTH))
            norm_stats(6, False)
            ffn_up(2, 7, W_UP3, conv=True)
            ffn_down(2, W_DN3)
            for i in range(TT):
                for e in range(2):
                    n = 2 * i + e
                    pe.wait_ge(h_ready, 7 * KD)
                    for c in range(4):
                        last = nc.tensor.transpose(ps[:, n, c * P:(c + 1) * P], h[:, 4 * e + c, M + i * P:M + (i + 1) * P], ident[:])
                    last.then_inc(fT, 1)


_IN = ["x", "p", "ffn1_norm", "ffn1_wg", "ffn1_wu", "ffn1_wd", "mix_norm", "w_in", "b_forget", "q_norm_nsa",
       "k_norm_cmp", "k_norm_slc", "k_norm_win", "cmp_pos_k", "cmp_pos_v", "cmp_k_w1", "cmp_k_w2", "cmp_v_w1",
       "cmp_v_w2", "q_norm_fox", "k_norm_fox", "out_norm_nsa", "out_norm_fox", "w_out", "ffn2_norm", "ffn2_wg",
       "ffn2_wu", "ffn2_wd", "ple_gate_norm", "ple_w_gate", "ple_w_proj", "ple_norm", "meta_tokens_2",
       "lb_param_2", "attn_norm_w_2", "w_in_2", "hgrn_norm_w_2", "conv_w_2", "w_out_2", "ffn_norm_w_2", "w_up_2",
       "ffn_conv_w_2", "ffn_conv_b_2", "w_down_2", "final_norm_w_2"]


def constants():
    import numpy as np
    f = np.float32
    r = np.arange(P)
    out = {"k_ident": np.eye(P, dtype=f)}
    out["k_causal"] = np.where(r[None, :] > r[:, None], f(NEG), f(0))
    out["k_headones"] = (r[:, None] // HD == r[None, :] // HD).astype(f)
    rot_dim = HD // 4
    half = rot_dim // 2
    turn = np.zeros((P, P), f)
    cos, sin = np.ones((P, S), f), np.zeros((P, S), f)
    inv = (500000.0 ** (-np.arange(0, rot_dim, 2, dtype=np.float64) / rot_dim)).astype(f)
    ang = (np.arange(S, dtype=f)[None, :] * inv[:, None]).astype(f)
    for b in range(0, P, HD):
        for j in range(half):
            turn[b + half + j, b + j] = -1.0
            turn[b + j, b + half + j] = 1.0
            for d in (j, half + j):
                cos[b + d], sin[b + d] = np.cos(ang[j]), np.sin(ang[j])
    out["k_rot"], out["k_cos"], out["k_sin"] = turn, cos, sin
    t = np.arange(S).reshape(TT, P).T
    n = np.arange(32)
    seen = (n[None, None, :] < NC) & (CS * n[None, None, :] + CB - 1 <= t[:, :, None])
    out["k_cmpneg"] = np.where(seen, f(0), f(NEG)).astype(f)
    out["k_cmprow"] = (t >= CB - 1).astype(f)
    lev = np.zeros((P, 8, P), f)
    lev[:, 0] = np.eye(P, dtype=f)
    for l in range(7):
        w = 1 << l
        same = r[:, None] // (2 * w) == r[None, :] // (2 * w)
        lev[:, l + 1] = same & (r[:, None] // w % 2 == 0) & (r[None, :] // w % 2 == 1)
    out["k_levels"] = lev
    return out


def kernel(**inputs):
    import numpy as np
    import concourse.bacc as bacc
    from concourse.bass_utils import run_bass_kernel_spmd as run

    nc = bacc.Bacc("TRN2", target_bir_lowering=False, num_devices=1)
    arrays, a = {}, {}
    for name, v in [(n, inputs[n]) for n in _IN] + list(constants().items()):
        v = np.ascontiguousarray(v)
        arrays["in_" + name] = v
        a[name] = nc.dram_tensor("in_" + name, v.shape, mybir.dt.from_np(v.dtype), kind="ExternalInput").ap()
    out = nc.dram_tensor("out", (1, S, D), F32, kind="ExternalOutput").ap()
    build(nc, a, out)
    return run(nc, [arrays], core_ids=[0]).results[0]["out"]
```

```python
from contextlib import ExitStack

import concourse.bass as bass
from concourse import mybir

F32 = mybir.dt.float32
F32R = mybir.dt.float32r
BF16 = mybir.dt.bfloat16
U8 = mybir.dt.uint8
ACT = mybir.ActivationFunctionType
ALU = mybir.AluOpType
AX_X = mybir.AxisListType.X

P = 128
D = 1024
KD = D // P
S = 512
M = 16
T = M + S
TT = S // P
F = 2816
FT = F // P
HD = 64
NH = 8
NKV = 2
DP = 256
CB, CS = 32, 16
NC = (S - CB) // CS + 1
CH = 256
HB = T // 2
UNIT = 2048
UC = UNIT // KD
EPS = 1e-6
NEG = -1e30
VH = 8
HG = VH // 2
LEVELS = 9

QA, KC, GA_C, QF, FL_C = 0, 512, 1280, 1304, 2840
U_QA, U_KC, U_VC, U_KS, U_VS, U_KW, U_VW, U_QF, U_KF, U_VF = 0, 4, 5, 6, 7, 8, 9, 10, 14, 18
U_N = 22
NORMED = [0, 1, 2, 3, 6, 8] + list(range(10, 18))
USQ = [range(0, 6), range(6, 10), range(10, 14)]
ROPED = [4, 0, 1, 2, 3, 6, 8]

W_UP1 = 0
W_DN1 = W_UP1 + 22
W_IN1 = W_DN1 + 11
W_OUT1 = W_IN1 + 12
W_UP2 = W_OUT1 + 4
W_DN2 = W_UP2 + 22
W_PLP = W_DN2 + 11
W_PLG = W_PLP + 1
W_IN2 = W_PLG + 4
W_OUT2 = W_IN2 + 36
W_UP3 = W_OUT2 + 4
W_DN3 = W_UP3 + 22
W_END = W_DN3 + 11
GATE_UNIT = W_IN1 + 5
FL0 = 32

C_Q, C_F, C_V, C_G, C_B, C_C, C_X, C_GA, C_GB = [D * n for n in range(9)]

ROWS = [
    [("ffn1_norm", 8), ("mix_norm", 8), ("ffn2_norm", 8), ("ple_gate_norm", 8), ("ple_norm", 8),
     ("out_norm_nsa", 4), ("out_norm_fox", 4), ("attn_norm_w_2", 8), ("ffn_norm_w_2", 8),
     ("ffn_conv_b_2", 22), ("hgrn_norm_w_2", 1)],
    [("conv_w_2", 24), ("ffn_conv_w_2", 66), ("lb_param_2", 16)],
    [("cmp_pos_k", 16), ("cmp_pos_v", 16)],
]
HEAD_ROWS = ["q_norm_nsa", "k_norm_slc", "k_norm_win", "q_norm_fox", "k_norm_fox", "k_norm_cmp"]
NROWS = [sum(n for _, n in r) for r in ROWS]
NROWS[2] += len(HEAD_ROWS)


def column(name, c=0):
    for t, rows in enumerate(ROWS):
        at = 0
        for n, k in rows:
            if n == name:
                return t, at + c
            at += k
        if t == 2:
            return t, at + HEAD_ROWS.index(name)
    raise KeyError(name)


def raw_count(u):
    return 16 * (u // 2 + 1) + (32 if u >= GATE_UNIT and u % 2 == GATE_UNIT % 2 else 0)


def used_count(u):
    return 1 + 2 * (u + 1) + 6 * sum(u >= w for w in (W_DN1 + 10, W_DN2 + 10, W_PLP, W_DN3 + 10))


NSA_STEPS = [(hh, i, b) for hh in range(4) for i in range(TT) for b in (0, 1, 2)]
FOX_STEPS = [(hh, i, 0) for hh in range(4) for i in range(TT)]
NSA_KEYS = [(b, t, g) for g in range(NKV) for b, t in enumerate((U_KS, U_KW))]
LAG_T, LAG_V, LAG_O = 2, 4, 5
STEPS = 2 * len(NSA_STEPS) + 2 * len(FOX_STEPS)
GATE_OF = (2, 0, 1)


def slot(s):
    return s % 12


def tile0(first):
    return used_count(first - 1) if first else 1


def level_sequence():
    seq, b = [], 0
    for lv in range(-1, LEVELS):
        for n in range(VH):
            seq.append((lv, n, b % 7))
            b += 1
        if 1 << max(lv, 0) < M:
            seq.append((lv, META, 7))
    return seq


def level_updates():
    n, out = 1, {}
    for lv in range(-1, LEVELS):
        for g in range(2):
            n += 2 if 0 <= lv < LEVELS - 1 else 1
            out[lv, g] = n
        if lv < 0:
            n += 1
        elif 1 << lv < M:
            n += 3 if 2 << lv < M else 1
        out[lv, META] = n
    return out


HID_BANK = [2, 3, 6, 7]
META = -1
E_BANK = [7, 0, 1, 2, 3, 4, 7, 0]
LEVEL_SEQ = level_sequence()
LEVEL_UP = level_updates()
LEVEL_CP0 = sum(lv < 7 for lv, _, _ in LEVEL_SEQ)
P2 = 5
N_ROWS = sum(len(r) for r in ROWS) + 2 * len(HEAD_ROWS)
N_CONST = 7
SLAB = 212800


def build(nc, a, out):
    ctx = ExitStack()
    with ctx:
        place = {"end": 0}

        def area(nbytes):
            at = place["end"]
            place["end"] = at + (nbytes + 31) // 32 * 32
            return at

        base = (nc.sbuf_base + 31) // 32 * 32
        ctx.enter_context(nc.sbuf_tensor("slab", [P, SLAB // 4], F32))

        def at(name, shape, off, dt=F32):
            return nc.alloc_sbuf_tensor_at(name, shape, dt, offset=base + off)

        def sb(name, shape, dt=F32):
            n = 1 if dt == U8 else 2 if dt == BF16 else 4
            for x in shape[1:]:
                n *= x
            return at(name, shape, area(n), dt)

        h = sb("h", [P, KD, T])
        XN = area(2 * KD * T * 4)
        xh = at("xh", [P, KD, T], XN, F32R)
        xl = at("xl", [P, KD, T], XN + KD * T * 4, F32R)
        raw = sb("raw", [P, 2, UNIT])
        whi = sb("whi", [P, 2, UNIT], F32R)
        wlo = sb("wlo", [P, 2, UNIT], F32R)
        TMP = area(4 * T * 4)
        tmp = at("tmp", [P, 4, T], TMP)
        ident = sb("ident", [P, P])
        ident_b = sb("ident_b", [P, P], BF16)
        causal = sb("causal", [P, P], BF16)
        headones = sb("headones", [P, P])
        rot = sb("rot", [P, P])
        COS = area(2 * S * 4)
        cosb = at("cosb", [P, S], COS)
        sinb = at("sinb", [P, S], COS + S * 4)
        cmpneg = sb("cmpneg", [P, TT, 32], BF16)
        cmprow = sb("cmprow", [P, TT])
        levelmask = sb("levelmask", [P, 8, P], U8)
        cols = sb("cols", [P, 3, P])
        ones1 = sb("ones1", [P, 1])
        epsc = sb("epsc", [P, 1])
        negones = sb("negones", [FL0 + NH, P])
        headsel = sb("headsel", [FL0 + NH, NH])
        forget_b = sb("forget_b", [FL0 + NH, 1])
        std = sb("std", [P, 112])
        rstd = sb("rstd", [P, 112])
        lb = sb("lb", [P, 2, 8])
        lbt = sb("lbt", [P, 4, 8])
        ttm = sb("ttm", [P, 2, VH, 8])
        AR = area(2 * FT * S * 4)
        act_h = at("act_h", [P, FT, S], AR, F32R)
        act_l = at("act_l", [P, FT, S], AR + FT * S * 4, F32R)
        x_tok = at("x_tok", [P, TT, D], AR)
        meta_tok = at("meta_tok", [M, D], AR + 16384)
        rows_t = at("rows_t", [P, 3, P], AR + 20480)
        levels_f = at("levels_f", [P, 8, P], AR + 22528)
        causal_f = at("causal_f", [P, P], AR + 26624)
        cmpneg_f = at("cmpneg_f", [P, TT, 32], AR + 27136)
        uT = at("uT", [P, U_N, S], AR)
        R2 = AR + U_N * S * 4
        w1 = at("w1", [P, 2, 16, CH], R2)
        blk = at("blk", [P, 2, 16, NKV, 32], R2 + 32768)
        vtok = at("vtok", [P, TT, 768], R2)
        otok = at("otok", [P, TT, D], R2 + 12288)
        prob = at("prob", [P, 3, S], R2 + 28672)
        probT = at("probT", [P, 3, TT, P], R2 + 34816)
        hid = at("hid", [P, 2, 2, NKV, 32], R2 + 40960)
        kcmp = at("kcmp", [P, 64], R2 + 41984)
        kcsq = at("kcsq", [P, 64], R2 + 42240)
        kcr = at("kcr", [P, 64], R2 + 42496)
        vcmp = at("vcmp", [32, NKV, HD], R2 + 42752)
        gsig = at("gsig", [P, TT, 24], R2 + 43264)
        w2 = at("w2", [P, 2, 2, HD], R2 + 43776)
        stat = at("stat", [P, 4, 12], R2 + 44800)
        qs = at("qs", [P, 2, S], XN, F32R)
        ksel = at("ksel", [P, NKV, 2, 2, S], XN + 4096, F32R)
        kfox = at("kfox", [P, 2, 2, S], XN + 4096, F32R)
        negsel = at("negsel", [FL0 + NH, 4, P], XN + 20480, F32R)
        csplit = at("csplit", [FL0 + NH, S], XN + 22528, F32R)
        cum = at("cum", [NH, S], XN + 26624)
        osq = at("osq", [P, S], XN + 28672)
        kch = at("kch", [P, 2, 64], XN + 30720, F32R)
        vcst = at("vcst", [32, HD], XN + 31232)
        flg = [at("flg_ln", [NH, S], XN + 28672), at("flg_log", [NH, S], XN + 31488), at("flg_in", [NH, S], XN + 20480)]
        gateT1 = at("gateT1", [FL0 + NH, S], R2 + 40960)
        gateT = at("gateT", [P, KD, S], AR)
        eT = at("eT", [P, KD, S], AR + 16384)
        p_tok = at("p_tok", [P, TT, DP], COS)
        p_h = at("p_h", [P, 2, S], AR + 36864, F32R)
        p_l = at("p_l", [P, 2, S], AR + 40960, F32R)
        Q = at("Q", [P, VH, T], AR)
        Fg = at("Fg", [P, VH, T], AR + 16896)
        V = at("V", [P, TT + 1, D], AR + 33792)
        GA = at("GA", [P, KD, T], AR + 54272)
        YB = at("YB", [P, KD, T], AR + 71168)
        K = at("K", [P, VH, T], XN)
        Ad = at("Ad", [P, VH, S], XN + 16896)
        Am = sb("Am", [M, VH, M])
        Amx = at("Amx", [M, 2, S], COS)
        Tev = at("Tev", [P, 4224], AR + 16896)
        Tod = at("Tod", [P, 4 * T], TMP)
        gainb = at("gainb", [P, D], AR)
        y_tok = at("y_tok", [P, TT, D], AR + 4096)
        assert place["end"] <= SLAB, place["end"]

        ps = ctx.enter_context(nc.psum_tensor("ps", [P, 8, 512], F32))

        def sem(name):
            return ctx.enter_context(nc.semaphore(name))

        const_in = sem("const_in")
        ident_in = sem("ident_in")
        masks_in = sem("masks_in")
        rows_in = sem("rows_in")
        x_in = sem("x_in")
        meta_in = sem("meta_in")
        raw_in = [sem("raw_in0"), sem("raw_in1")]
        cmp_in = sem("cmp_in")
        p_in = sem("p_in")
        gain_in = sem("gain_in")
        stored = sem("stored")
        hi_ready = sem("hi_ready")
        lo_ready = sem("lo_ready")
        tiles_done = sem("tiles_done")
        setup = sem("setup")
        colsT = sem("colsT")
        cols_ready = sem("cols_ready")
        xT = sem("xT")
        meta_ready = sem("meta_ready")
        hid_zero = sem("hid_zero")
        gc_ready = sem("gc_ready")
        e_step = sem("e_step")
        fsum = sem("fsum")
        lb_step = sem("lb_step")
        lb_exp = sem("lb_exp")
        q_scaled = sem("q_scaled")
        h_ready = sem("h_ready")
        sq_ready = sem("sq_ready")
        sq_added = sem("sq_added")
        ssq_done = sem("ssq_done")
        std_ready = sem("std_ready")
        rstd_ready = sem("rstd_ready")
        rb_done = sem("rb_done")
        normed = sem("normed")
        xh_ready = sem("xh_ready")
        xl_ready = sem("xl_ready")
        gate_done = sem("gate_done")
        prod_done = sem("prod_done")
        acth_done = sem("acth_done")
        actl_done = sem("actl_done")
        conv_in = sem("conv_in")
        conv_step = sem("conv_step")
        u_ready = sem("u_ready")
        usq = sem("usq")
        ussq = sem("ussq")
        ustd = sem("ustd")
        urstd = sem("urstd")
        urb = sem("urb")
        unorm = sem("unorm")
        urot = sem("urot")
        rope_step = sem("rope_step")
        k_hi = sem("k_hi")
        k_lo = sem("k_lo")
        q_hi = sem("q_hi")
        q_lo = sem("q_lo")
        vtr = sem("vtr")
        v_ready = sem("v_ready")
        blk_cp = sem("blk_cp")
        blk_ready = sem("blk_ready")
        hid_mm = sem("hid_mm")
        hid_ready = sem("hid_ready")
        cmp_mm = sem("cmp_mm")
        cmp_sq = sem("cmp_sq")
        cmp_step = sem("cmp_step")
        g_ready = sem("g_ready")
        gate_mm = sem("gate_mm")
        fl_step = sem("fl_step")
        fl_v = sem("fl_v")
        vc_staged = sem("vc_staged")
        c_staged = sem("c_staged")
        score_done = sem("score_done")
        nmax_done = sem("nmax_done")
        exp_done = sem("exp_done")
        trans_done = sem("trans_done")
        ptev_done = sem("ptev_done")
        pv_done = sem("pv_done")
        o_step = sem("o_step")
        o_done = sem("o_done")
        osq_done = sem("osq_done")
        ostd = sem("ostd")
        orstd = sem("orstd")
        oscaled = sem("oscaled")
        otr = sem("otr")
        pT_done = sem("pT_done")
        ph_ready = sem("ph_ready")
        pl_ready = sem("pl_ready")
        gate_ready = sem("gate_ready")
        e_ready = sem("e_ready")
        sig_done = sem("sig_done")
        p2_step = sem("p2_step")
        p2_free = sem("p2_free")
        lev_cp = sem("lev_cp")
        hsq = sem("hsq")
        hssq = sem("hssq")
        hstd = sem("hstd")
        hrstd = sem("hrstd")
        hrb = sem("hrb")
        h2_step = sem("h2_step")
        vev = sem("vev")
        az = sem("az")
        lev_mm = sem("lev_mm")
        lev_sel = sem("lev_sel")
        lev_up = sem("lev_up")
        lev_k = sem("lev_k")
        amx_mm = sem("amx_mm")
        amx_cp = sem("amx_cp")
        o2_mm = sem("o2_mm")
        o2_cp = sem("o2_cp")
        fT = sem("fT")
        fsq = sem("fsq")
        fstd = sem("fstd")
        frstd = sem("frstd")
        f_ready = sem("f_ready")

        block = ctx.enter_context(nc.Block())

        def col(name, c=0, n=1):
            t, r = column(name, c)
            return cols[:, t, r:r + n]

        def w_view(buf, slot, kt):
            return buf[:, slot, :].rearrange("p (k n) -> p k n", k=kt)

        WHOLE = [(M, S, 0)]
        BOTH = [(0, HB, 0), (HB, HB, 1)]
        CONV = [(M - 4, 258, 0), (M + 254, 258, 1)]

        def pairs(buf, lo_, hi_, w, g=None):
            x = buf if g is None else buf[:, HG * g:HG * (g + 1)]
            return x[:, :, lo_:hi_].rearrange("p n (b e w) -> p n b e w", e=2, w=w)

        def block_decays(lv, g):
            if lv == 0:
                return pairs(Fg, M, T, 1, g)[:, :, :, :, 0]
            n = VH * (S >> lv)
            return (Tod if lv % 2 else Tev)[:, 0:n].rearrange("p (n b e) -> p n b e", n=VH, e=2)[:, HG * g:HG * (g + 1)]

        def q_update(lv, g):
            q2 = pairs(Q, M, T, 1 << lv, g)[:, :, :, 1, :]
            return q2, block_decays(lv, g)[:, :, :, 0].unsqueeze(3).to_broadcast([P, HG, S >> lv + 1, 1 << lv])

        def k_update(lv, g):
            k2 = pairs(K, M, T, 1 << lv, g)[:, :, :, 0, :]
            return k2, block_decays(lv, g)[:, :, :, 1].unsqueeze(3).to_broadcast([P, HG, S >> lv + 1, 1 << lv])

        SSQ, RB = 5, 6

        def rb_view(whole):
            return ps[:, RB, :] if whole else ps[:, RB:RB + 2, 0:HB]

        def halves(ap):
            return ap.rearrange("p (a b) -> p a b", a=2)

        @block.sync
        def _(sp):
            def const(dst, src):
                sp.dma_start(dst, src).then_inc(const_in, 16)

            sp.dma_start(ident[:], a["k_ident"]).then_inc(ident_in, 16)
            for i in range(TT):
                sp.dma_start(x_tok[:, i, :], a["x"][0, i * P:(i + 1) * P, :]).then_inc(x_in, 16)
            w_gate, w_up = [a[name][0].rearrange("(k p) n -> p k n", p=P)[:, :, 0:UC] for name in ("ffn1_wg", "ffn1_wu")]
            sp.dma_start(raw[:, 0, :].rearrange("p (k n) -> p k n", k=KD), w_gate).then_inc(raw_in[0], 16)
            sp.dma_start(meta_tok[:], a["meta_tokens_2"]).then_inc(meta_in, 16)
            for dst, src in ((levels_f, "k_levels"), (causal_f, "k_causal"), (cmpneg_f, "k_cmpneg")):
                sp.dma_start(dst[:], a[src]).then_inc(masks_in, 16)
            for t, rows in enumerate(ROWS):
                r = 0
                for name, n in rows:
                    src = a[name]
                    if len(src.shape) > 2:
                        src = src.flatten_outer_dims()
                    if len(src.shape) == 2:
                        src = src.rearrange("a b -> (a b)")
                    sp.dma_start(rows_t[r:r + n, t, :], src.rearrange("(a b) -> a b", b=P)).then_inc(rows_in, 16)
                    r += n
            for name in HEAD_ROWS:
                for half in range(2):
                    sp.dma_start(rows_t[r:r + 1, 2, half * HD:(half + 1) * HD], a[name]).then_inc(rows_in, 16)
                r += 1
            sp.dma_start(raw[:, 1, :].rearrange("p (k n) -> p k n", k=KD), w_up).then_inc(raw_in[1], 16)
            const(headones[:], a["k_headones"])
            const(rot[:], a["k_rot"])
            const(cosb[:], a["k_cos"])
            const(sinb[:], a["k_sin"])
            const(cmprow[:], a["k_cmprow"])
            const(headsel[:], a["k_headsel"])
            const(forget_b[FL0:FL0 + NH, :], a["b_forget"].rearrange("a n -> n a"))

            def load(u, slot, kt, src):
                sp.wait_ge(lo_ready, u - 1)
                sp.dma_start(w_view(raw, slot, kt), src).then_inc(raw_in[slot], 16)

            def col_unit(name):
                w = a[name][0].rearrange("(k p) n -> p k n", p=P)
                return lambda c: w[:, :, bass.ds(c, UC)]

            def up(first, wa, wb):
                wa, wb = col_unit(wa), col_unit(wb) if isinstance(wb, str) else wb
                s = first % 2
                with sp.Fori(1 if first == 0 else 0, F // UC) as i:
                    load(first + 2 * i, s, KD, wa(i * UC))
                    load(first + 2 * i + 1, 1 - s, KD, wb(i * UC))

            def down(first, name):
                w = a[name][0].rearrange("(u k p) n -> p u k n", p=P, k=2)
                s = first % 2
                load(first, s, 2, w[:, 0])
                with sp.Fori(0, 5) as i:
                    for e in range(2):
                        load(first + 1 + 2 * i + e, (s + 1 + e) % 2, 2, w[:, bass.ds(2 * i + 1 + e, 1)].rearrange("p u k n -> p (u k) n"))

            def square(first, name):
                w = col_unit(name)
                s = first % 2
                with sp.Fori(0, 2) as i:
                    for e in range(2):
                        load(first + 2 * i + e, (s + e) % 2, KD, w((2 * i + e) * UC))

            up(W_UP1, "ffn1_wg", "ffn1_wu")
            down(W_DN1, "ffn1_wd")
            w = col_unit("w_in")
            s = W_IN1 % 2
            with sp.Fori(0, 2) as i:
                for e in range(2):
                    load(W_IN1 + 2 * i + e, (s + e) % 2, KD, w((2 * i + e) * UC))
            load(W_IN1 + 4, s, KD, w(4 * UC))
            gate_w = a["w_in"][0].rearrange("(k p) n -> p k n", p=P)
            gslot = raw[:, 1 - s, 0:KD * P].rearrange("p (k n) -> p k n", k=KD)
            sp.wait_ge(lo_ready, GATE_UNIT - 1)
            for c0, c1, col0 in ((0, FL0, GA_C), (FL0, FL0 + NH, FL_C), (FL0 + NH, P, 0)):
                sp.dma_start(gslot[:, :, c0:c1], gate_w[:, :, col0:col0 + c1 - c0]).then_inc(raw_in[1 - s], 16)
            with sp.Fori(0, 3) as i:
                for e in range(2):
                    load(W_IN1 + 6 + 2 * i + e, (s + e) % 2, KD, w(QF + (2 * i + e) * UC))
            sp.wait_ge(h_ready, 2 * KD)
            for n, name in enumerate(("cmp_k_w1", "cmp_v_w1")):
                sp.dma_start(w1[:, n], a[name][0].rearrange("(k p) n -> p k n", p=P)).then_inc(cmp_in, 16)
            for n, name in enumerate(("cmp_k_w2", "cmp_v_w2")):
                sp.dma_start(w2[:, n], a[name][0].rearrange("(k p) n -> p k n", p=P)).then_inc(cmp_in, 16)
            square(W_OUT1, "w_out")
            sp.wait_ge(rope_step, 3 * len(ROPED))
            sp.dma_start(p_tok[:], a["p"][0, 0].rearrange("(i p) n -> p i n", p=P)).then_inc(p_in, 16)
            up(W_UP2, "ffn2_wg", "ffn2_wu")
            down(W_DN2, "ffn2_wd")
            load(W_PLP, W_PLP % 2, 2, a["ple_w_proj"][0].rearrange("(k p) n -> p k n", p=P))
            square(W_PLG, "ple_w_gate")
            w = col_unit("w_in_2")
            s = W_IN2 % 2
            for n, (c0, c1) in enumerate(((C_Q, C_F), (C_G, C_GA), (C_C, C_X), (C_B, C_GB))):
                with sp.Fori(0, 4) as i:
                    load(W_IN2 + 8 * n + 2 * i, s, KD, w(c0 + i * UC))
                    load(W_IN2 + 8 * n + 2 * i + 1, 1 - s, KD, w(c1 + i * UC))
            with sp.Fori(0, 2) as i:
                for e in range(2):
                    load(W_IN2 + 32 + 2 * i + e, (s + e) % 2, KD, w(C_V + (2 * i + e) * UC))
            square(W_OUT2, "w_out_2")
            w = col_unit("w_up_2")
            up(W_UP3, "w_up_2", lambda c: w(c + F))
            down(W_DN3, "w_down_2")
            sp.wait_ge(h_ready, 7 * KD)
            sp.dma_start(gainb[:], a["final_norm_w_2"].rearrange("(a n) -> a n", a=1).to_broadcast([P, D])).then_inc(gain_in, 16)
            for i in range(TT):
                sp.wait_ge(f_ready, 2 * (i + 1))
                sp.dma_start(out[0, i * P:(i + 1) * P, :], y_tok[:, i, :]).then_inc(stored, 16)
            sp.wait_ge(stored, 16 * TT)

        @block.gpsimd
        def _(pool):
            nc.gpsimd.memset(ones1[:], 1.0).then_inc(setup, 1)
            nc.gpsimd.memset(epsc[:], EPS).then_inc(setup, 1)
            nc.gpsimd.memset(negones[:], -1.0).then_inc(setup, 1)
            pool.wait_ge(ident_in, 16)
            pool.wait_ge(masks_in, 48)
            for dst, src in ((levelmask, levels_f), (causal, causal_f), (cmpneg, cmpneg_f), (ident_b, ident)):
                nc.gpsimd.tensor_copy(dst[:], src[:]).then_inc(setup, 1)

            def lo(u, slot, n=UNIT):
                pool.wait_ge(hi_ready, u + 1)
                nc.gpsimd.tensor_tensor(wlo[:, slot, 0:n], raw[:, slot, 0:n], whi[:, slot, 0:n].bitcast(F32),
                                        ALU.subtract).then_inc(lo_ready, 1)

            def lo_run(u0, u1):
                s = u0 % 2
                with pool.Fori(0, (u1 - u0) // 2) as i:
                    for e in range(2):
                        lo(u0 + 2 * i + e, (s + e) % 2)
                if (u1 - u0) % 2:
                    lo(u1 - 1, (u1 - 1) % 2)

            lo_run(0, GATE_UNIT)
            lo(GATE_UNIT, GATE_UNIT % 2, KD * P)
            lo_run(GATE_UNIT + 1, W_OUT1 + 1)

            pool.wait_ge(lo_ready, W_OUT1 + 1)

            def k_lo_of(n, half, src, hi_part, lo_part):
                for e in range(2):
                    pool.wait_ge(k_hi, n + 2)
                    nc.gpsimd.tensor_tensor(lo_part[e * HD:(e + 1) * HD], src, hi_part[half * HD:(half + 1) * HD].bitcast(F32),
                                            ALU.subtract).then_inc(k_lo, 1)
                    pool.wait_ge(k_lo, n + e + 1)

            for n, (b, t, g) in enumerate(NSA_KEYS):
                k_lo_of(2 * n, g, uT[g * HD:(g + 1) * HD, t, :], ksel[:, g, b, 0, :], ksel[:, g, b, 1, :])
            pool.wait_ge(k_hi, 9)
            nc.gpsimd.tensor_tensor(kch[:, 1, :], kcmp[:], kch[:, 0, :].bitcast(F32), ALU.subtract).then_inc(k_lo, 1)
            pool.wait_ge(k_lo, 9)
            for fox in range(2):
                for n in range(NH):
                    e, t = n % 2, n // 2
                    d, other = slice(e * HD, (e + 1) * HD), slice((1 - e) * HD, (2 - e) * HD)
                    pool.wait_ge(q_hi, (NH + 2) * fox + n + 1)
                    nc.gpsimd.tensor_tensor(qs[other, e, :], uT[d, (U_QF if fox else U_QA) + t, :], qs[d, e, :].bitcast(F32),
                                            ALU.subtract).then_inc(q_lo, 1)
                    pool.wait_ge(q_lo, NH * fox + n + 1)
                    if fox:
                        k_lo_of(9 + 2 * n, e, uT[e * HD:(e + 1) * HD, U_KF + t, :], kfox[:, e, 0, :], kfox[:, e, 1, :])
            lo_run(W_OUT1 + 1, W_OUT2 + 1)
            pool.wait_ge(tiles_done, used_count(W_IN2 + 35))
            nc.gpsimd.memset(Ad[:], 0.0).then_inc(az, 1)
            for lv in range(LEVELS - 1):
                for g in range(2):
                    pool.wait_ge(lev_mm, 1 + max(i for i, (l, n, _) in enumerate(LEVEL_SEQ) if l == lv and n in range(HG * g, HG * (g + 1))))
                    k2, decay = k_update(lv, g)
                    nc.gpsimd.tensor_tensor(k2, k2, decay, ALU.mult).then_inc(lev_k, 1)
            lo_run(W_OUT2 + 1, W_END)

        @block.scalar
        def _(act):
            def hi(u, slot, landed, used=None, n=UNIT):
                act.wait_ge(raw_in[slot], landed)
                if used is not None:
                    act.wait_ge(tiles_done, used)
                nc.scalar.activation(whi[:, slot, 0:n], raw[:, slot, 0:n], ACT.Copy).then_inc(hi_ready, 1)

            def hi_pair(first, i, at=0):
                for e in (1, 2):
                    u = first + at + e
                    if u < W_END:
                        hi(u + 2 * i, u % 2, raw_count(u) + 16 * i, tile0(first) + 2 * (at + e - 1) + 4 * i)

            def hi_one(u, n=UNIT):
                if u < W_END:
                    hi(u, u % 2, raw_count(u), used_count(u - 2) if u >= 2 else None, n)

            def squares(m, ready, src, c0):
                for n in range(KD):
                    act.wait_ge(*ready(n))
                    if n >= 4:
                        act.wait_ge(sq_added, (KD - 1) * m + n - 3)
                    nc.scalar.activation(tmp[:, n % 3 if n else 3, c0:T], src(n), ACT.Square).then_inc(sq_ready, 1)
                act.wait_ge(ssq_done, m + 1)
                first = 1 if c0 else 0
                nc.scalar.activation(std[:, first:5], ps[:, SSQ, first:5], ACT.Sqrt, bias=epsc[:, 0:1],
                                     scale=1.0 / D).then_inc(std_ready, 1)

            def norm(m, v, w, x_only, between=None):
                c0 = M if x_only else 0
                squares(m, lambda n: (h_ready, KD * w + n + 1), lambda n: h[:, n, c0:T], c0)
                if between is not None:
                    between()
                for n in range(KD):
                    act.wait_ge(normed, KD * v + n + 1)
                    nc.scalar.activation(xh[:, n, c0:T], tmp[:, n % 4, c0:T], ACT.Copy).then_inc(xh_ready, 1)

            def ffn_up(g, first, conv=False):
                with act.Fori(0, F // UC) as i:
                    t0 = tile0(first) + 4 * i
                    hi_pair(first, i)
                    for j in range(2):
                        act.wait_ge(tiles_done, t0 + j + 1)
                        if conv:
                            nc.scalar.activation(tmp[:, j, M - 4:T].rearrange("p (a b) -> p a b", a=2),
                                                 ps[:, 2 * j:2 * j + 2, 0:258], ACT.Copy).then_inc(conv_in, 1)
                        else:
                            nc.scalar.activation(tmp[:, j, M:T], ps[:, j, :], ACT.Silu).then_inc(gate_done, 1)
                    if conv:
                        for j in range(2):
                            act.wait_ge(conv_step, 6 * i + 3 * j + 3)
                            nc.scalar.activation(tmp[:, j, M:T], tmp[:, 2 + j, 0:S], ACT.Silu).then_inc(gate_done, 1)
                    for j in range(2):
                        act.wait_ge(prod_done, FT * g + 2 * i + j + 1)
                        nc.scalar.activation(act_h[:, bass.ds(2 * i + j, 1), :],
                                             tmp[:, 2 + j:3 + j, 0:S], ACT.Copy).then_inc(acth_done, 1)

            def ffn_down(first):
                with act.Fori(0, 5) as i:
                    hi_pair(first, i)
                hi_one(first + 11)

            def square(first):
                with act.Fori(0, 2) as i:
                    hi_pair(first, i)

            act.wait_ge(setup, 3)
            for n in range(KD):
                act.wait_ge(xT, n + 1)
                nc.scalar.activation(h[:, n, M:T], ps[:, (n + 4) % 8, :], ACT.Copy).then_inc(h_ready, 1)

            def small_vectors():
                hi_one(0)
                for t in range(3):
                    act.wait_ge(colsT, t + 1)
                    nc.scalar.activation(cols[:, t, 0:NROWS[t]], ps[:, t, 0:NROWS[t]], ACT.Copy).then_inc(cols_ready, 1)
                act.wait_ge(tiles_done, 1)
                nc.scalar.activation(h[:, :, 0:M], ps[:, 3, 0:KD * M].rearrange("p (n m) -> p n m", n=KD), ACT.Copy).then_inc(meta_ready, 1)

            norm(0, 0, 0, True, small_vectors)
            act.wait_ge(lb_step, 2)
            nc.scalar.activation(lbt[:, 0:2, :], lbt[:, 0:2, :], ACT.Exp).then_inc(lb_exp, 1)
            act.wait_ge(setup, 7)
            ffn_up(0, W_UP1)
            ffn_down(W_DN1)
            norm(1, 1, 1, True)
            t0 = tile0(W_IN1)
            with act.Fori(0, 2) as i:
                hi_pair(W_IN1, i)
                for j in range(4):
                    act.wait_ge(tiles_done, t0 + 4 * i + j + 1)
                    nc.scalar.activation(uT[:, bass.ds(4 * i + j, 1), :], ps[:, j:j + 1, :], ACT.Copy).then_inc(u_ready, 1)
            hi_one(GATE_UNIT, KD * P)
            hi_one(GATE_UNIT + 1)
            for j in range(2):
                act.wait_ge(tiles_done, t0 + 8 + j + 1)
                nc.scalar.activation(uT[:, 8 + j, :], ps[:, j, :], ACT.Copy).then_inc(u_ready, 1)
            act.wait_ge(tiles_done, used_count(GATE_UNIT))
            nc.scalar.activation(gateT1[:], ps[0:FL0 + NH, 2, :], ACT.Copy).then_inc(u_ready, 1)
            act.wait_ge(xl_ready, 2 * KD)
            for i in range(3):
                hi_pair(W_IN1, i, 6)
                for j in range(4):
                    act.wait_ge(tiles_done, t0 + 12 + 4 * i + j + 1)
                    nc.scalar.activation(uT[:, U_QF + 4 * i + j, :], ps[:, j, :], ACT.Copy).then_inc(u_ready, 1)
                act.wait_ge(u_ready, 11 + 4 * (i + 1))
                for n in USQ[i]:
                    if n >= 4:
                        act.wait_ge(ussq, n - 3)
                    nc.scalar.activation(tmp[:, n % 4, 0:S], uT[:, NORMED[n], :], ACT.Square).then_inc(usq, 1)
            act.wait_ge(ussq, len(NORMED))
            nc.scalar.activation(std[:, 0:112], ps[:, 7, 0:112], ACT.Sqrt, bias=epsc[:, 0:1], scale=1.0 / HD).then_inc(ustd, 1)
            for n, t in enumerate((U_VC, U_KC)):
                if t == U_KC:
                    act.wait_ge(rope_step, 3)
                for par in range(2):
                    for g in range(NKV):
                        s0 = uT[g * HD:(g + 1) * HD, t, par:par + 1]
                        win = bass.AP(tensor=s0.tensor, offset=s0.offset, ap=[s0.ap[0], [2, CB // 2], [CS, NC]])
                        nc.scalar.activation(blk[par * HD:(par + 1) * HD, 1 - n, :, g, 0:NC], win, ACT.Copy).then_inc(blk_cp, 1)
            act.wait_ge(gate_mm, 1)
            for c in range(3):
                nc.scalar.activation(gsig[:, :, GATE_OF[c]:24:3], ps[:, 7, 0:TT * 24].rearrange("p (i n) -> p i n", i=TT)[:, :, c:24:3],
                                     ACT.Sigmoid).then_inc(g_ready, 1)
            act.wait_ge(fl_v, 2)
            nc.scalar.activation(flg[1][:], flg[0][:], ACT.Exp).then_inc(fl_step, 1)
            act.wait_ge(fl_step, 1)
            nc.scalar.activation(flg[0][:], flg[1][:], ACT.Ln, bias=1.0).then_inc(fl_step, 1)
            act.wait_ge(rope_step, 3 * len(ROPED))
            act.wait_ge(unorm, len(NORMED))
            for b, t, g in NSA_KEYS:
                for e in range(2):
                    nc.scalar.activation(ksel[e * HD:(e + 1) * HD, g, b, 0, :], uT[g * HD:(g + 1) * HD, t, :], ACT.Copy).then_inc(k_hi, 1)
            for e in range(2):
                d = slice(e * HD, (e + 1) * HD)
                nc.scalar.activation(qs[d, e, :], uT[d, U_QA, :], ACT.Copy).then_inc(q_hi, 1)
            act.wait_ge(hid_zero, 1)
            for n in range(2):
                for mt in range(2):
                    q = 2 * n + mt
                    act.wait_ge(hid_mm, q + 1)
                    nc.scalar.activation(hid[:, 1 - n, mt, :, 0:NC], ps[:, HID_BANK[q], 0:NKV * NC].rearrange("p (g n) -> p g n", g=NKV),
                                         ACT.Silu).then_inc(hid_ready, 1)
            act.wait_ge(cmp_mm, 3)
            nc.scalar.activation(kcsq[:], ps[:, 6, 256:320], ACT.Square).then_inc(cmp_sq, 1)
            nc.scalar.activation(vcmp[:], ps[0:32, 6, 320:448].rearrange("p (g d) -> p g d", g=NKV), ACT.Copy).then_inc(cmp_sq, 1)
            act.wait_ge(cmp_mm, 4)
            nc.scalar.activation(kcr[:], ps[:, 6, 448:512], ACT.Sqrt, bias=epsc[:, 0:1], scale=1.0 / HD).then_inc(cmp_sq, 1)
            for n in range(6):
                act.wait_ge(vtr, n + 1)
                nc.scalar.activation(vtok[:, :, n * P:(n + 1) * P], ps[:, 2 + n % 2, :].rearrange("p (i d) -> p i d", i=TT),
                                     ACT.Copy).then_inc(v_ready, 1)
            act.wait_ge(cmp_step, 2)
            nc.scalar.activation(kch[:, 0, :], kcmp[:], ACT.Copy).then_inc(k_hi, 1)

            def attention(n0, steps, t_q, fox):
                NS = len(steps)

                def stage(e, tile):
                    d = slice(e * HD, (e + 1) * HD)
                    nc.scalar.activation(qs[d, e:e + 1, :], uT[d, bass.ds(t_q + tile, 1), :], ACT.Copy).then_inc(q_hi, 1)

                if fox:
                    act.wait_ge(q_hi, NH + 2)
                    for e in range(2):
                        stage(e, 0)
                with act.Fori(0, 2) as it:
                    s0 = n0 + NS * it
                    for s in range(NS + LAG_T):
                        if s < NS:
                            hh, i, b = steps[s]
                            n = 32 if b == 2 else (i + 1) * P
                            act.wait_ge(nmax_done, s0 + s + 1)
                            if s >= 3:
                                act.wait_ge(trans_done, s0 + s - 2)
                            nc.scalar.activation(prob[:, s % 3, 0:n], ps[:, s % 3, 0:n], ACT.Exp, bias=stat[:, 0, slot(s):slot(s) + 1],
                                                 accum_out=stat[:, 1, slot(s):slot(s) + 1]).then_inc(exp_done, 1)
                            if s == NS - 1 or steps[s + 1][0] != hh:
                                stage(hh % 2, 2 * it + (hh + 2) // 2)
                        if s >= LAG_T:
                            q = s - LAG_T
                            hh, i, b = steps[q]
                            act.wait_ge(trans_done, s0 + q + 1)
                            if q >= 3:
                                act.wait_ge(pv_done, s0 + q - 2)
                            if q == 2 and not fox:
                                act.wait_ge(pv_done, s0 + 1)
                                nc.scalar.activation(vcst[:], vcmp[:, bass.ds(it, 1), :].rearrange("p a d -> p (a d)"), ACT.Copy).then_inc(vc_staged, 1)
                            if b == 2:
                                nc.scalar.activation(probT[0:32, q % 3, 0, :], ps[0:32, 3 + q % 3, 0:P], ACT.Copy).then_inc(ptev_done, 1)
                            else:
                                nc.scalar.activation(probT[:, q % 3, 0:i + 1, :],
                                                     ps[:, 3 + q % 3, 0:(i + 1) * P].rearrange("p (k q) -> p k q", k=i + 1),
                                                     ACT.Copy).then_inc(ptev_done, 1)

            attention(0, NSA_STEPS, U_QA, False)
            attention(2 * len(NSA_STEPS), FOX_STEPS, U_QF, True)
            act.wait_ge(o_done, STEPS)
            for n in range(2 * TT):
                if n:
                    act.wait_ge(osq_done, n)
                nc.scalar.activation(osq[:], otok[:, n // 2, n % 2 * S:(n % 2 + 1) * S], ACT.Square,
                                     accum_out=rstd[:, n:n + 1]).then_inc(osq_done, 1)
            act.wait_ge(osq_done, 8)
            nc.scalar.activation(std[:, 0:8], rstd[:, 0:8], ACT.Sqrt, bias=epsc[:, 0:1], scale=1.0 / S).then_inc(ostd, 1)
            for n in range(KD):
                act.wait_ge(otr, n + 1)
                if n >= 4:
                    act.wait_ge(xl_ready, 2 * KD + n - 3)
                gain = col("out_norm_nsa", n) if n < 4 else col("out_norm_fox", n - 4)
                nc.scalar.activation(tmp[:, n % 4, M:T], ps[:, 4 + n % 4, :], ACT.Copy, scale=gain).then_inc(normed, 1)
                act.wait_ge(normed, 2 * KD + n + 1)
                nc.scalar.activation(xh[:, n, M:T], tmp[:, n % 4, M:T], ACT.Copy).then_inc(xh_ready, 1)
            square(W_OUT1)
            norm(2, 3, 2, True)
            ffn_up(1, W_UP2)
            ffn_down(W_DN2)
            for e in range(2):
                act.wait_ge(pT_done, e + 1)
                nc.scalar.activation(p_h[:, e, :], ps[:, 5 + e, :], ACT.Copy).then_inc(ph_ready, 1)
            hi_one(W_PLG)

            def embedding_out():
                for n in range(KD):
                    act.wait_ge(tiles_done, tile0(W_PLP) + n + 1)
                    nc.scalar.activation(eT[:, n, :], ps[:, E_BANK[n], :], ACT.Copy).then_inc(e_ready, 1)

            norm(3, 4, 3, True, embedding_out)
            hi_pair(W_PLG, 0)
            act.wait_ge(xl_ready, 5 * KD)
            squares(4, lambda n: (e_ready, n + 1), lambda n: eT[:, n, :], M)
            for i in range(2):
                if i:
                    hi_pair(W_PLG, i)
                for j in range(4):
                    act.wait_ge(tiles_done, tile0(W_PLG) + 4 * i + j + 1)
                    nc.scalar.activation(gateT[:, 4 * i + j, :], ps[:, j, :], ACT.Sigmoid).then_inc(gate_ready, 1)
            norm(5, 5, 4, False)
            for n in range(4):
                with act.Fori(0, 4) as i:
                    t0 = tile0(W_IN2) + 16 * n + 4 * i
                    hi_pair(W_IN2, i, 8 * n)
                    act.wait_ge(p2_free, P2 + 16 * n + 4 * i)
                    for j in range(4):
                        if (n == 2 and j >= 2) or (n == 3 and j < 2):
                            continue
                        act.wait_ge(tiles_done, t0 + j + 1)
                        nc.scalar.activation(halves(tmp[:, j, :]), ps[:, 2 * j:2 * j + 2, 0:HB],
                                             ACT.Copy if n == 2 else ACT.Sigmoid).then_inc(sig_done, 1)
            for i in range(2):
                hi_pair(W_IN2, i, 32)
                for e in range(2):
                    act.wait_ge(tiles_done, used_count(W_IN2 + 32 + 2 * i + e))
                    nc.scalar.activation(V[:, :, (2 * i + e) * UC:(2 * i + e + 1) * UC],
                                         ps[:, 3 * e:3 * e + 3, :].rearrange("p b c -> p (b c)")[:, 0:5 * UC].rearrange("p (i c) -> p i c", i=5),
                                         ACT.Copy).then_inc(vev, 1)
            for idx, (lv, n, bank) in enumerate(LEVEL_SEQ):
                if lv >= 7:
                    act.wait_ge(lev_mm, idx + 1)
                    w = 256 if lv == 7 else 512
                    dst = Tod[:, 64 + n * 256:64 + (n + 1) * 256] if lv == 7 else Tev[:, 128 + n * 512:128 + (n + 1) * 512]
                    nc.scalar.activation(dst, ps[:, bank, 0:w], ACT.Copy).then_inc(lev_cp, 1)
            for n in range(VH + 1):
                if n < VH:
                    act.wait_ge(amx_mm, n + 1)
                    if n >= 2:
                        act.wait_ge(o2_mm, n - 1)
                    nc.scalar.activation(Amx[:, n % 2, :], ps[0:M, n % 2, :], ACT.Copy).then_inc(amx_cp, 1)
                if n:
                    act.wait_ge(o2_mm, n)
                    nc.scalar.activation(Q[:, n - 1, M:T], ps[:, 2 + (n - 1) % 2, :], ACT.Copy).then_inc(o2_cp, 1)
                    nc.scalar.activation(Q[:, n - 1, 0:M], ps[:, 4 + (n - 1) % 2, 0:M], ACT.Copy).then_inc(o2_cp, 1)
                    act.wait_ge(o2_cp, 2 * n)
                    nc.scalar.activation(K[:, n - 1, :], Q[:, n - 1, :], ACT.Square).then_inc(hsq, 1)
            act.wait_ge(hssq, VH)
            nc.scalar.activation(std[:, 0:40], ps[:, 6, 0:40], ACT.Sqrt, bias=epsc[:, 0:1], scale=1.0 / P).then_inc(hstd, 1)
            for n in range(VH):
                act.wait_ge(normed, 6 * KD + n + 1)
                nc.scalar.activation(xh[:, n, :], tmp[:, n % 4, :], ACT.Copy).then_inc(xh_ready, 1)
            square(W_OUT2)
            norm(6, 7, 5, False)
            ffn_up(2, W_UP3, conv=True)
            ffn_down(W_DN3)
            for i in range(TT):
                for e in range(2):
                    n = 2 * i + e
                    act.wait_ge(fT, n + 1)
                    if n:
                        act.wait_ge(fsq, n)
                    nc.scalar.activation(tmp[:, 0, 0:S], ps[:, n, :], ACT.Square, accum_out=rstd[:, n:n + 1]).then_inc(fsq, 1)
            act.wait_ge(fsum, 1)
            nc.scalar.activation(std[:, 0:TT], std[:, 8:8 + TT], ACT.Sqrt, bias=epsc[:, 0:1], scale=1.0 / D).then_inc(fstd, 1)
        @block.vector
        def _(dve):
            def split_lo(v, n, c0):
                dve.wait_ge(xh_ready, KD * v + n + 1)
                nc.vector.tensor_tensor(xl[:, n, c0:T], tmp[:, n % 4, c0:T], xh[:, n, c0:T].bitcast(F32),
                                        ALU.subtract).then_inc(xl_ready, 1)

            def add_square(m, n, c0):
                dve.wait_ge(sq_ready, KD * m + n + 1)
                if n > 1:
                    dve.wait_ge(sq_added, (KD - 1) * m + n - 1)
                nc.vector.tensor_tensor(tmp[:, 3, c0:T], tmp[:, 3, c0:T], tmp[:, n % 3, c0:T], ALU.add).then_inc(sq_added, 1)

            def updates(m, x_only, update):
                c0 = M if x_only else 0
                for n in range(KD):
                    update(n)
                    if n > 1:
                        add_square(m, n - 1, c0)
                add_square(m, KD - 1, c0)

            def rsqrt(m, first):
                dve.wait_ge(std_ready, m + 1)
                nc.vector.reciprocal(rstd[:, first:5], std[:, first:5]).then_inc(rstd_ready, 1)

            def norm(m, v, gain, x_only):
                c0 = M if x_only else 0
                rsqrt(m, 1 if x_only else 0)
                dve.wait_ge(rb_done, m + 1)
                for n in range(KD):
                    if n >= 4:
                        dve.wait_ge(xl_ready, KD * v + n - 3)
                    if x_only:
                        nc.vector.scalar_tensor_tensor(tmp[:, n % 4, M:T], h[:, n, M:T], col(gain, n), ps[:, RB, :],
                                                       ALU.mult, ALU.mult).then_inc(normed, 1)
                    else:
                        nc.vector.scalar_tensor_tensor(halves(tmp[:, n % 4, :]), halves(h[:, n, :]), col(gain, n),
                                                       ps[:, RB:RB + 2, 0:HB], ALU.mult, ALU.mult).then_inc(normed, 1)
                    if n:
                        split_lo(v, n - 1, c0)
                split_lo(v, KD - 1, c0)

            def ffn_up(g, first, conv=False):
                with dve.Fori(0, F // UC) as i:
                    t0 = tile0(first) + 4 * i
                    if conv:
                        for j in range(2):
                            wc = lambda k: cols[:, 1, bass.ds(24 + FT * k + 2 * i + j, 1)]
                            t, r = column("ffn_conv_b_2")
                            bc = cols[:, t, bass.ds(r + 2 * i + j, 1)]
                            y, at_ = tmp[:, 2 + j, 0:S], tmp[:, j, :]
                            s0 = 6 * i + 3 * j
                            dve.wait_ge(conv_in, 2 * i + j + 1)
                            nc.vector.tensor_scalar(y, at_[:, M:T], wc(2), bc, ALU.mult, ALU.add).then_inc(conv_step, 1)
                            dve.wait_ge(conv_step, s0 + 1)
                            nc.vector.scalar_tensor_tensor(y, at_[:, M - 1:T - 1], wc(1), y, ALU.mult, ALU.add).then_inc(conv_step, 1)
                            dve.wait_ge(conv_step, s0 + 2)
                            nc.vector.scalar_tensor_tensor(y, at_[:, M - 2:T - 2], wc(0), y, ALU.mult, ALU.add).then_inc(conv_step, 1)
                    for j in range(2):
                        dve.wait_ge(gate_done, FT * g + 2 * i + j + 1)
                        dve.wait_ge(tiles_done, t0 + 2 + j + 1)
                        nc.vector.tensor_tensor(tmp[:, 2 + j, 0:S], tmp[:, j, M:T], ps[:, 4 + 2 * j if conv else 2 + j, :],
                                                ALU.mult).then_inc(prod_done, 1)
                        dve.wait_ge(acth_done, FT * g + 2 * i + j + 1)
                        nc.vector.tensor_tensor(act_l[:, bass.ds(2 * i + j, 1), :], tmp[:, 2 + j:3 + j, 0:S],
                                                act_h[:, bass.ds(2 * i + j, 1), :].bitcast(F32),
                                                ALU.subtract).then_inc(actl_done, 1)

            def ffn_down(first, scale, m=None, between=None):
                def add(n):
                    if between is not None:
                        between(n)
                    dve.wait_ge(tiles_done, used_count(first + 9) + n + 1)
                    nc.vector.scalar_tensor_tensor(h[:, n, M:T], ps[:, (n + 5) % 8, :], scale, h[:, n, M:T],
                                                   ALU.mult, ALU.add).then_inc(h_ready, 1)

                if m is None:
                    for n in range(KD):
                        add(n)
                else:
                    updates(m, True, add)

            updates(0, True, lambda n: None)
            dve.wait_ge(cols_ready, 3)
            norm(0, 0, "ffn1_norm", True)
            for n in ("q_norm_nsa", "q_norm_fox"):
                nc.vector.tensor_scalar(col(n), col(n), HD ** -0.5, None, ALU.mult).then_inc(q_scaled, 1)
            t, r = column("lb_param_2")
            l0, l1 = cols[:, t, r:r + 8], cols[:, t, r + 8:r + 16]
            nc.vector.tensor_tensor(lbt[:, 2, :], l0, l1, ALU.max).then_inc(lb_step, 1)
            dve.wait_ge(lb_step, 1)
            nc.vector.tensor_tensor(lbt[:, 0:2, :], cols[:, t, r:r + 16].rearrange("p (a b) -> p a b", a=2),
                                    lbt[:, 2:3, :].to_broadcast([P, 2, 8]), ALU.subtract).then_inc(lb_step, 1)
            dve.wait_ge(lb_exp, 1)
            nc.vector.tensor_tensor(lbt[:, 2, :], lbt[:, 0, :], lbt[:, 1, :], ALU.add).then_inc(lb_step, 1)
            dve.wait_ge(lb_step, 3)
            nc.vector.reciprocal(lbt[:, 3, :], lbt[:, 2, :]).then_inc(lb_step, 1)
            dve.wait_ge(lb_step, 4)
            nc.vector.tensor_tensor(lb[:, 0, :], lbt[:, 0, :], lbt[:, 3, :], ALU.mult).then_inc(lb_step, 1)
            dve.wait_ge(lb_step, 5)
            nc.vector.tensor_scalar(lb[:, 1, :], lb[:, 0, :], -1.0, 1.0, ALU.mult, ALU.add).then_inc(p2_free, P2)
            ffn_up(0, W_UP1)
            ffn_down(W_DN1, 0.5, 1)
            norm(1, 1, "mix_norm", True)
            def rope(n):
                t = ROPED[n]
                if t in NORMED:
                    dve.wait_ge(unorm, NORMED.index(t) + 1)
                nc.vector.tensor_tensor(tmp[:, n % 2, 0:S], uT[:, t, :], cosb[:], ALU.mult).then_inc(rope_step, 1)
                dve.wait_ge(urot, n + 1)
                nc.vector.tensor_tensor(tmp[:, 2 + n % 2, 0:S], ps[:, 4 + n % 2, :], sinb[:], ALU.mult).then_inc(rope_step, 1)
                dve.wait_ge(rope_step, 3 * n + 2)
                nc.vector.tensor_tensor(uT[:, t, :], tmp[:, n % 2, 0:S], tmp[:, 2 + n % 2, 0:S], ALU.add).then_inc(rope_step, 1)

            def head_norm(n):
                t = NORMED[n]
                gain = col("q_norm_nsa" if t < 4 else "k_norm_slc" if t == U_KS else "k_norm_win" if t == U_KW
                           else "q_norm_fox" if t < U_KF else "k_norm_fox")
                dve.wait_ge(urb, n + 1)
                nc.vector.scalar_tensor_tensor(uT[:, t, :], uT[:, t, :], gain, ps[:, n % 2, :], ALU.mult, ALU.mult).then_inc(unorm, 1)

            dve.wait_ge(ussq, len(NORMED))
            dve.wait_ge(const_in, 16 * N_CONST)
            rope(0)
            dve.wait_ge(ustd, 1)
            nc.vector.reciprocal(rstd[:, 0:112], std[:, 0:112]).then_inc(urstd, 1)
            dve.wait_ge(q_scaled, 2)
            for n in range(6):
                head_norm(n)
            dve.wait_ge(u_ready, 11)
            nc.vector.tensor_scalar(flg[2][:], gateT1[FL0:FL0 + NH, :], forget_b[FL0:FL0 + NH, 0:1], None, ALU.add).then_inc(fl_v, 1)
            dve.wait_ge(gate_mm, 1)
            dve.wait_ge(fl_v, 1)
            nc.vector.memset(hid[:], 0.0).then_inc(hid_zero, 1)
            nc.vector.scalar_tensor_tensor(flg[0][:], flg[2][:], -1.0, flg[2][:], ALU.mult, ALU.min).then_inc(fl_v, 1)
            for n in range(2):
                kind = 1 - n
                dve.wait_ge(blk_cp, 4 * (n + 1))
                t, r = column("cmp_pos_v" if kind else "cmp_pos_k")
                pos = cols[:, t, r:r + 16].unsqueeze(2).to_broadcast([P, 16, NC])
                for g in range(NKV):
                    nc.vector.tensor_tensor(blk[:, kind, :, g, 0:NC], blk[:, kind, :, g, 0:NC], pos, ALU.add).then_inc(blk_ready, 1)
            for n in range(1, len(ROPED)):
                rope(n)
            for n in range(6, len(NORMED)):
                head_norm(n)
            dve.wait_ge(fl_step, 2)
            nc.vector.scalar_tensor_tensor(flg[1][:], flg[2][:], 0.0, flg[0][:], ALU.min, ALU.subtract).then_inc(fl_v, 1)
            dve.wait_ge(fl_v, 3)
            nc.vector.tensor_tensor_scan(cum[:], ones1[0:8, 0:1].to_broadcast([8, S]), flg[1][:], 0.0,
                                         ALU.mult, ALU.add).then_inc(fl_v, 1)
            dve.wait_ge(fl_v, 4)
            nc.vector.tensor_scalar(csplit[:], cosb[0:FL0 + NH, :], 0.0, None, ALU.mult).then_inc(fl_v, 1)
            dve.wait_ge(fl_v, 5)
            nc.vector.tensor_copy(csplit[0:NH, :], cum[:]).then_inc(fl_v, 1)
            dve.wait_ge(fl_v, 6)
            nc.vector.tensor_tensor(csplit[FL0:FL0 + NH, :], cum[:], csplit[0:NH, :].bitcast(F32), ALU.subtract).then_inc(fl_v, 1)
            dve.wait_ge(cmp_sq, 3)
            nc.vector.reciprocal(kcr[:], kcr[:]).then_inc(cmp_step, 1)
            dve.wait_ge(cmp_step, 1)
            nc.vector.scalar_tensor_tensor(kcmp[:], ps[:, 6, 256:320], col("k_norm_cmp"), kcr[:], ALU.mult, ALU.mult).then_inc(cmp_step, 1)
            dve.wait_ge(g_ready, 3)
            for i in range(TT):
                gc = gsig[:, i, :].rearrange("p (n c) -> p n c", c=3)[:, :, GATE_OF[0]]
                nc.vector.tensor_scalar(gc, gc, cmprow[:, i:i + 1], None, ALU.mult).then_inc(gc_ready, 1)
            dve.wait_ge(gc_ready, TT)

            def attention(n0, steps, fox):
                NS = len(steps)

                def stage(e, tile):
                    for f in range(2):
                        nc.vector.tensor_copy(kfox[f * HD:(f + 1) * HD, e:e + 1, 0, :],
                                              uT[e * HD:(e + 1) * HD, bass.ds(U_KF + tile, 1), :]).then_inc(k_hi, 1)

                if fox:
                    for e in range(2):
                        stage(e, 0)
                with dve.Fori(0, 2) as it:
                    s0 = n0 + NS * it
                    if fox:
                        for hh in range(4):
                            nc.vector.tensor_scalar(negsel[:, hh, :], negones[:], headsel[:, bass.ds(4 * it + hh, 1)], None,
                                                    ALU.mult).then_inc(c_staged, 1)
                    for s in range(NS + LAG_O):
                        if s < NS:
                            hh, i, b = steps[s]
                            n = 32 if b == 2 else (i + 1) * P
                            dve.wait_ge(score_done, s0 + s + 1)
                            nc.vector.tensor_reduce(stat[:, 0, slot(s):slot(s) + 1], ps[:, s % 3, 0:n], AX_X, ALU.max,
                                                    negate=True).then_inc(nmax_done, 1)
                            if fox and (s == NS - 1 or steps[s + 1][0] != hh):
                                stage(hh % 2, 2 * it + (hh + 2) // 2)
                        if s >= LAG_O:
                            q = s - LAG_O
                            hh, i, b = steps[q]
                            GS = 2 if fox else 3
                            c = slot(q)
                            if q % GS == 0:
                                dve.wait_ge(exp_done, s0 + q + GS)
                                nc.vector.reciprocal(stat[:, 2, c:c + GS], stat[:, 1, c:c + GS]).then_inc(o_step, 1)
                                if not fox:
                                    dve.wait_ge(o_step, 2 * (NS // GS * it + q // GS) + 1)
                                    nc.vector.tensor_tensor(stat[:, 3, c:c + GS], stat[:, 2, c:c + GS],
                                                            gsig[:, i, bass.ds(12 * it + 3 * hh, 3)], ALU.mult).then_inc(o_step, 1)
                            rg = stat[:, 2 if fox else 3, c:c + 1]
                            if q % GS == 0:
                                dve.wait_ge(o_step, (4 * len(NSA_STEPS) // 3 + NS // GS * it + q // GS + 1) if fox
                                            else 2 * (NS // GS * it + q // GS) + 2)
                            dve.wait_ge(pv_done, s0 + q + 1)
                            o = otok[:, i, bass.ds((S if fox else 0) + 4 * HD * it + HD * hh, HD)]
                            pv = ps[:, 6 + q % 2, hh % 2 * HD:(hh % 2 + 1) * HD] if fox else ps[:, 6 + q % 2, 0:HD]
                            if b == 0:
                                nc.vector.tensor_scalar(o, pv, rg, None, ALU.mult).then_inc(o_done, 1)
                            else:
                                dve.wait_ge(o_done, s0 + q)
                                nc.vector.scalar_tensor_tensor(o, pv, rg, o, ALU.mult, ALU.add).then_inc(o_done, 1)

            attention(0, NSA_STEPS, False)
            attention(2 * len(NSA_STEPS), FOX_STEPS, True)
            dve.wait_ge(ostd, 1)
            nc.vector.reciprocal(rstd[:, 0:8], std[:, 0:8]).then_inc(orstd, 1)
            dve.wait_ge(orstd, 1)
            for n in range(2 * TT):
                o = otok[:, n // 2, n % 2 * S:(n % 2 + 1) * S]
                nc.vector.tensor_scalar(o, o, rstd[:, n:n + 1], None, ALU.mult).then_inc(oscaled, 1)
            for n in range(KD):
                split_lo(2, n, M)

            def add_attention(n):
                dve.wait_ge(tiles_done, tile0(W_OUT1) + n + 1)
                nc.vector.tensor_tensor(h[:, n, M:T], h[:, n, M:T], ps[:, n % 4, :], ALU.add).then_inc(h_ready, 1)

            updates(2, True, add_attention)
            norm(2, 3, "ffn2_norm", True)
            ffn_up(1, W_UP2)

            def split_p(n):
                e = n - 4
                if 0 <= e < 2:
                    dve.wait_ge(ph_ready, e + 1)
                    nc.vector.tensor_tensor(p_l[:, e, :], ps[:, 5 + e, :], p_h[:, e, :].bitcast(F32), ALU.subtract).then_inc(pl_ready, 1)

            ffn_down(W_DN2, 0.5, 3, split_p)
            norm(3, 4, "ple_gate_norm", True)
            updates(4, True, lambda n: None)
            rsqrt(4, 1)
            dve.wait_ge(rb_done, 5)

            for n in range(KD):
                nc.vector.scalar_tensor_tensor(eT[:, n, :], eT[:, n, :], col("ple_norm", n), ps[:, RB, :], ALU.mult, ALU.mult).then_inc(e_step, 1)

            def add_embedding(n):
                t = eT[:, n, :]
                dve.wait_ge(gate_ready, n + 1)
                dve.wait_ge(e_step, KD + n if n else KD)
                nc.vector.tensor_tensor(t, t, gateT[:, n, :], ALU.mult).then_inc(e_step, 1)
                dve.wait_ge(e_step, KD + n + 1)
                nc.vector.tensor_tensor(h[:, n, M:T], h[:, n, M:T], t, ALU.add).then_inc(h_ready, 1)

            updates(5, False, add_embedding)
            norm(5, 5, "attn_norm_w_2", False)

            def bank2(j):
                return ps[:, 2 * j:2 * j + 2, 0:HB]

            def tile_of(buf, i, j):
                return buf[:, bass.ds(2 * i + j, 1), :].rearrange("p a (b c) -> p (a b) c", b=2)

            t2 = [halves(tmp[:, j, :]) for j in range(4)]
            for n in range(4):
                s1 = 4 * (2, 1, 1, 1)[n]
                with dve.Fori(0, 4) as i:
                    t0 = tile0(W_IN2) + 16 * n + 4 * i
                    f0 = P2 + 16 * n + 4 * i
                    if n == 0:
                        for j in range(2):
                            dve.wait_ge(sig_done, 4 * i + j + 1)
                            nc.vector.tensor_tensor(tile_of(Q, i, j), bank2(j), t2[j], ALU.mult).then_inc(p2_free, 1)
                        for j in range(2):
                            dve.wait_ge(sig_done, 4 * i + j + 3)
                            nc.vector.tensor_scalar(Fg[:, bass.ds(2 * i + j, 1), :], tmp[:, 2 + j:3 + j, :], lb[:, 1, bass.ds(2 * i + j, 1)],
                                                    lb[:, 0, bass.ds(2 * i + j, 1)], ALU.mult, ALU.add).then_inc(p2_free, 1)
                    if n == 1:
                        for j in range(2):
                            dve.wait_ge(sig_done, 16 + 4 * i + j + 1)
                            nc.vector.tensor_tensor(t2[j], bank2(j), t2[j], ALU.mult).then_inc(p2_free, 1)
                        for j in range(2):
                            dve.wait_ge(sig_done, 16 + 4 * i + j + 3)
                            dve.wait_ge(p2_free, f0 + j + 1)
                            nc.vector.tensor_tensor(GA[:, bass.ds(2 * i + j, 1), :], tmp[:, j:j + 1, :], tmp[:, 2 + j:3 + j, :], ALU.mult).then_inc(p2_free, 1)
                    if n == 2:
                        for j in range(2):
                            wc = lambda k: cols[:, 1, bass.ds(8 * k + 2 * i + j, 1)]
                            y = YB[:, bass.ds(2 * i + j, 1), :]
                            cx = tmp[:, j:j + 1, :]
                            dve.wait_ge(sig_done, 32 + 2 * i + j + 1)
                            dve.wait_ge(tiles_done, t0 + 2 + j + 1)
                            nc.vector.tensor_tensor(t2[j], t2[j], bank2(2 + j), ALU.mult).then_inc(p2_step, 1)
                            s0 = 6 * i + 3 * j
                            dve.wait_ge(p2_step, s0 + 1)
                            nc.vector.tensor_scalar(y, cx, wc(2), None, ALU.mult).then_inc(p2_step, 1)
                            dve.wait_ge(p2_step, s0 + 2)
                            y1 = YB[:, bass.ds(2 * i + j, 1), 1:T]
                            nc.vector.scalar_tensor_tensor(y1, tmp[:, j:j + 1, 0:T - 1], wc(1), y1, ALU.mult, ALU.add).then_inc(p2_step, 1)
                            dve.wait_ge(p2_step, s0 + 3)
                            y2 = YB[:, bass.ds(2 * i + j, 1), 2:T]
                            nc.vector.scalar_tensor_tensor(y2, tmp[:, j:j + 1, 0:T - 2], wc(0), y2, ALU.mult, ALU.add).then_inc(p2_free, 2)
                    if n == 3:
                        for j in range(2):
                            dve.wait_ge(tiles_done, t0 + j + 1)
                            nc.vector.tensor_tensor(tile_of(YB, i, j), tile_of(YB, i, j), bank2(j), ALU.mult).then_inc(p2_free, 1)
                        for j in range(2):
                            dve.wait_ge(sig_done, 40 + 2 * i + j + 1)
                            dve.wait_ge(p2_free, f0 + j + 1)
                            nc.vector.tensor_tensor(YB[:, bass.ds(2 * i + j, 1), :], YB[:, bass.ds(2 * i + j, 1), :], tmp[:, 2 + j:3 + j, :], ALU.mult).then_inc(p2_free, 1)

            dve.wait_ge(tiles_done, used_count(W_IN2 + 35))
            dve.wait_ge(p2_free, P2 + 64)
            up_n = [0]

            def link(ins):
                up_n[0] += 1
                ins.then_inc(lev_up, 1)
                dve.wait_ge(lev_up, up_n[0])

            link(nc.vector.tensor_scalar(K[:], Fg[:], -1.0, 1.0, ALU.mult, ALU.add))
            nc.vector.memset(Am[:], 0.0).then_inc(az, 1)
            dve.wait_ge(az, 2)
            idx = 0

            def select(lv, last):
                nonlocal idx
                while True:
                    _, n, bank = LEVEL_SEQ[idx]
                    idx += 1
                    dve.wait_ge(lev_mm, idx)
                    if lv < 7 and n == META:
                        nc.vector.copy_predicated(Am[:], levelmask[0:M, lv + 1, 0:M].unsqueeze(1).to_broadcast([M, VH, M]),
                                                  ps[0:M, bank, 0:VH * M].rearrange("p (n m) -> p n m", n=VH)).then_inc(lev_sel, 1)
                    elif lv < 7:
                        nc.vector.copy_predicated(Ad[:, n, :].rearrange("p (i t) -> p i t", i=TT),
                                                  levelmask[:, lv + 1, :].unsqueeze(1).to_broadcast([P, TT, P]),
                                                  ps[:, bank, :].rearrange("p (i t) -> p i t", i=TT)).then_inc(lev_sel, 1)
                    if n == last:
                        return

            for lv in range(-1, LEVELS):
                H = 1 << max(lv, 0)
                nb = S // (2 * H)
                for g in range(2):
                    heads = slice(HG * g, HG * (g + 1))
                    select(lv, HG * (g + 1) - 1)
                    if lv < 0:
                        link(nc.vector.tensor_tensor(Q[:, heads, M:T], Q[:, heads, M:T], Fg[:, heads, M:T], ALU.mult))
                    else:
                        q2, decay = q_update(lv, g)
                        link(nc.vector.tensor_tensor(q2, q2, decay, ALU.mult))
                        if lv < LEVELS - 1:
                            if lv:
                                dve.wait_ge(lev_k, 2 * lv)
                            tot = block_decays(lv, g)
                            nxt = (Tev if lv % 2 else Tod)[:, 0:VH * nb].rearrange("p (n b) -> p n b", n=VH)[:, heads]
                            link(nc.vector.tensor_tensor(nxt, tot[:, :, :, 0], tot[:, :, :, 1], ALU.mult))
                    assert up_n[0] == LEVEL_UP[lv, g]
                if H >= M:
                    continue
                select(lv, META)
                if lv < 0:
                    link(nc.vector.tensor_tensor(Q[:, :, 0:M], Q[:, :, 0:M], Fg[:, :, 0:M], ALU.mult))
                else:
                    mb = M // (2 * H)
                    mt = pairs(Fg, 0, M, 1)[:, :, :, :, 0] if lv == 0 else \
                        ttm[:, lv % 2, :, 0:2 * mb].rearrange("p n (b e) -> p n b e", e=2)
                    mk = pairs(K, 0, M, H)[:, :, :, 0, :]
                    link(nc.vector.tensor_tensor(mk, mk, mt[:, :, :, 1].unsqueeze(3).to_broadcast([P, VH, mb, H]), ALU.mult))
                    if 2 * H < M:
                        mq = pairs(Q, 0, M, H)[:, :, :, 1, :]
                        link(nc.vector.tensor_tensor(mq, mq, mt[:, :, :, 0].unsqueeze(3).to_broadcast([P, VH, mb, H]), ALU.mult))
                        link(nc.vector.tensor_tensor(ttm[:, (lv + 1) % 2, :, 0:mb], mt[:, :, :, 0], mt[:, :, :, 1], ALU.mult))
                assert up_n[0] == LEVEL_UP[lv, META]
            dve.wait_ge(hstd, 1)
            nc.vector.reciprocal(rstd[:, 0:40], std[:, 0:40]).then_inc(hrstd, 1)
            for n in range(KD):
                t = halves(tmp[:, n % 4, :])
                if n >= 4:
                    dve.wait_ge(xl_ready, 6 * KD + n - 3)
                dve.wait_ge(hrb, n + 1)
                b0 = 6 if n % 2 == 0 else 2
                nc.vector.scalar_tensor_tensor(t, halves(Q[:, n, :]), col("hgrn_norm_w_2"), ps[:, b0:b0 + 2, 0:HB],
                                               ALU.mult, ALU.mult).then_inc(h2_step, 1)
                dve.wait_ge(h2_step, 2 * n + 1)
                nc.vector.tensor_tensor(tmp[:, n % 4, :], tmp[:, n % 4, :], GA[:, n, :], ALU.mult).then_inc(h2_step, 1)
                dve.wait_ge(h2_step, 2 * n + 2)
                nc.vector.tensor_tensor(tmp[:, n % 4, :], tmp[:, n % 4, :], YB[:, n, :], ALU.add).then_inc(normed, 1)
                if n:
                    split_lo(6, n - 1, 0)
            split_lo(6, KD - 1, 0)

            def add_mixed(n):
                dve.wait_ge(tiles_done, tile0(W_OUT2) + n + 1)
                nc.vector.tensor_tensor(halves(h[:, n, :]), halves(h[:, n, :]), bank2(n % 4), ALU.add).then_inc(h_ready, 1)

            updates(6, False, add_mixed)
            norm(6, 7, "ffn_norm_w_2", False)
            ffn_up(2, W_UP3, conv=True)
            ffn_down(W_DN3, 1.0)
            dve.wait_ge(fsq, 2 * TT)
            sums = rstd[:, 0:2 * TT].rearrange("p (i e) -> p i e", e=2)
            nc.vector.tensor_tensor(std[:, 8:8 + TT], sums[:, :, 0], sums[:, :, 1], ALU.add).then_inc(fsum, 1)
            dve.wait_ge(fstd, 1)
            nc.vector.reciprocal(rstd[:, 8:8 + TT], std[:, 0:TT]).then_inc(frstd, 1)
            dve.wait_ge(frstd, 1)
            dve.wait_ge(gain_in, 16)
            for n in range(2 * TT):
                i, e = n // 2, n % 2
                nc.vector.scalar_tensor_tensor(y_tok[:, i, e * S:(e + 1) * S], ps[:, n, :], rstd[:, 8 + i:9 + i],
                                               gainb[:, e * S:(e + 1) * S], ALU.mult, ALU.mult).then_inc(f_ready, 1)
        @block.tensor
        def _(pe):
            mm = nc.tensor.matmul

            def tile_mm(j, e, slot, xs, splits, banks, ready=None):
                wh, wl = w_view(whi, slot, KD), w_view(wlo, slot, KD)
                for k in range(KD):
                    if ready is not None:
                        pe.wait_ge(xl_ready, KD * ready + k + 1)
                    for q, (w, x) in enumerate(((wh, xs[0]), (wl, xs[0]), (wh, xs[1]))):
                        for c0, n, b in splits:
                            last = mm(ps[:, j * banks + b, 0:n], w[:, k, e * P:(e + 1) * P], x[:, k, c0:c0 + n],
                                      start=(k == 0 and q == 0), stop=(k == KD - 1 and q == 2))
                last.then_inc(tiles_done, 1)

            X = (xh, xl)

            def pair(u, p, free, ready=None, banks=1, splits=(WHOLE, WHOLE), between=None):
                for half in range(2):
                    if half and between is not None:
                        between()
                    pe.wait_ge(lo_ready, u + half + 1)
                    for e in range(2):
                        j = 2 * half + e
                        if free is not None:
                            free(j)
                        tile_mm(j, e, (p + half) % 2, X, splits[half], banks, ready if j == 0 else None)

            def norm_stats(m, x_only):
                norm_sums(m, x_only)
                norm_spread(m, x_only)

            def norm_sums(m, x_only):
                c0s = [0] * (not x_only) + [M + i * P for i in range(TT)]
                f = 1 if x_only else 0
                pe.wait_ge(sq_added, (KD - 1) * (m + 1))
                for i, c0 in enumerate(c0s):
                    last = mm(ps[:, SSQ, f + i:f + i + 1], tmp[:, 3, c0:c0 + P], ones1[:], start=True, stop=True)
                last.then_inc(ssq_done, 1)

            def norm_spread(m, x_only):
                pe.wait_ge(rstd_ready, m + 1)
                spread(lambda i: rstd[:, i:i + 1], x_only, RB).then_inc(rb_done, 1)

            def spread(colof, x_only, bank):
                if x_only:
                    for i in range(TT):
                        last = mm(ps[:, bank, i * P:(i + 1) * P], colof(1 + i).to_broadcast([P, P]), ident[:], start=True, stop=True)
                    return last
                mm(ps[:, bank, 0:M], colof(0)[0:M].to_broadcast([M, P]), ident[0:M, 0:M], start=True, stop=True)
                for i in range(TT):
                    c = M + i * P
                    while c < M + (i + 1) * P:
                        b = c // HB
                        end = min(M + (i + 1) * P, (b + 1) * HB)
                        at_ = c - M - i * P
                        last = mm(ps[:, bank + b, c - b * HB:end - b * HB], colof(1 + i).to_broadcast([P, P]),
                                  ident[:, at_:at_ + end - c], start=True, stop=True)
                        c = end
                return last

            def ffn_up(g, v, first, conv=False):
                s = first % 2
                splits = (CONV, WHOLE) if conv else (WHOLE, WHOLE)
                banks = 2 if conv else 1

                def step(i, free, ready=None):
                    pair(first + 2 * i, s, free, ready, banks, splits)

                step(0, None, v)
                with pe.Fori(1, F // UC) as i:
                    def free(j):
                        if j < 2:
                            pe.wait_ge(conv_in if conv else gate_done, (0 if conv else FT * g) + 2 * i + j - 1)
                        else:
                            pe.wait_ge(prod_done, FT * g + 2 * i + j - 3)
                    step(i, free)

            def ffn_down(g, first):
                s = first % 2

                def unit(u, slot, k, start=False, stop=False):
                    pe.wait_ge(lo_ready, u + 1)
                    pe.wait_ge(actl_done, FT * g + k + 2)
                    wh, wl = w_view(whi, slot, 2), w_view(wlo, slot, 2)
                    for n in range(KD):
                        for e in range(2):
                            for q, (w, x) in enumerate(((wh, act_h), (wl, act_h), (wh, act_l))):
                                last = mm(ps[:, (n + 5) % 8, :], w[:, e, n * P:(n + 1) * P],
                                          x[:, bass.ds(k + e, 1), :].rearrange("p a s -> p (a s)"),
                                          start=(start and e == 0 and q == 0), stop=(stop and e == 1 and q == 2))
                        if stop:
                            last.then_inc(tiles_done, 1)
                    if not stop:
                        last.then_inc(tiles_done, 2)

                pe.wait_ge(prod_done, FT * (g + 1))
                unit(first, s, 0, start=True)
                with pe.Fori(0, 4) as i:
                    for e in range(2):
                        unit(first + 1 + 2 * i + e, (s + 1 + e) % 2, 4 * i + 2 + 2 * e)
                unit(first + 9, (s + 9) % 2, 18)
                unit(first + 10, s, 20, stop=True)

            def square(first, v, ready, w, banks=1, splits=(WHOLE, WHOLE)):
                for i in range(2):
                    pair(first + 2 * i, first % 2,
                         (lambda j: pe.wait_ge(ready, w + j + 1)) if i else None, v if i == 0 else None, banks, splits)

            pe.wait_ge(ident_in, 16)
            pe.wait_ge(x_in, 16 * TT)
            for n in range(KD):
                for i in range(TT):
                    last = nc.tensor.transpose(ps[:, (n + 4) % 8, i * P:(i + 1) * P], x_tok[:, i, n * P:(n + 1) * P], ident[:])
                last.then_inc(xT, 1)
            pe.wait_ge(setup, 3)
            norm_sums(0, True)
            pe.wait_ge(h_ready, KD)
            pe.wait_ge(rows_in, 16 * N_ROWS)
            for t in range(3):
                nc.tensor.transpose(ps[:, t, 0:NROWS[t]], rows_t[0:NROWS[t], t, :], ident[0:NROWS[t], 0:NROWS[t]]).then_inc(colsT, 1)
            pe.wait_ge(meta_in, 16)
            for n in range(KD):
                last = nc.tensor.transpose(ps[:, 3, n * M:(n + 1) * M], meta_tok[:, n * P:(n + 1) * P], ident[0:M, 0:M])
            last.then_inc(tiles_done, 1)
            norm_spread(0, True)
            pe.wait_ge(cols_ready, 3)
            pe.wait_ge(meta_ready, 1)
            ffn_up(0, 0, W_UP1)
            ffn_down(0, W_DN1)
            norm_stats(1, True)
            s = W_IN1 % 2
            pair(W_IN1, s, None, 1)
            pair(W_IN1 + 2, s, lambda j: pe.wait_ge(u_ready, j + 1))
            pe.wait_ge(lo_ready, W_IN1 + 5)
            for e in range(2):
                pe.wait_ge(u_ready, 4 + e + 1)
                tile_mm(e, e, s, X, WHOLE, 1)
            pe.wait_ge(lo_ready, GATE_UNIT + 1)
            pe.wait_ge(u_ready, 7)
            gh, gl = [w[:, 1 - s, 0:KD * P].rearrange("p (k n) -> p k n", k=KD) for w in (whi, wlo)]
            for k in range(KD):
                for q, (w, x) in enumerate(((gh, xh), (gl, xh), (gh, xl))):
                    last = mm(ps[:, 2, :], w[:, k, :], x[:, k, M:T], start=(k == 0 and q == 0), stop=(k == KD - 1 and q == 2))
            last.then_inc(tiles_done, 2)
            pe.wait_ge(u_ready, 11)
            pe.wait_ge(const_in, 16 * N_CONST)
            two = headones[:, 0:P:HD]
            for i in range(3):
                pair(W_IN1 + 6 + 2 * i, s, lambda j: pe.wait_ge(u_ready, 8 + 4 * i + j))
                for n in USQ[i]:
                    pe.wait_ge(usq, n + 1)
                    for t in range(TT):
                        last = mm(ps[:, 7, 28 * t + 2 * n:28 * t + 2 * n + 2], tmp[:, n % 4, t * P:(t + 1) * P], two, start=True, stop=True)
                    last.then_inc(ussq, 1)
            def turned(n):
                t = ROPED[n]
                if t in NORMED:
                    pe.wait_ge(unorm, NORMED.index(t) + 1)
                if n >= 2:
                    pe.wait_ge(rope_step, 3 * n - 4)
                mm(ps[:, 4 + n % 2, :], rot[:], uT[:, t, :], start=True, stop=True).then_inc(urot, 1)

            def head_spread(n):
                if n >= 2:
                    pe.wait_ge(unorm, n - 1)
                for i in range(TT):
                    for e in range(2):
                        c = 28 * i + 2 * n + e
                        last = mm(ps[e * HD:(e + 1) * HD, n % 2, i * P:(i + 1) * P], rstd[:, c:c + 1].to_broadcast([P, HD]), ident[:],
                                  start=True, stop=True)
                last.then_inc(urb, 1)

            def hidden(n):
                kind = 1 - n
                pe.wait_ge(blk_ready, 2 * (n + 1))
                for mt in range(2):
                    q = 2 * n + mt
                    for kt in range(16):
                        last = mm(ps[:, HID_BANK[q], 0:NKV * NC], w1[:, kind, kt, mt * P:(mt + 1) * P], blk[:, kind, kt, :, 0:NC],
                                  start=(kt == 0), stop=(kt == 15))
                    last.then_inc(hid_mm, 1)

            turned(0)
            pe.wait_ge(urstd, 1)
            for i in range(TT):
                last = nc.tensor.transpose(ps[:, 7, i * 24:(i + 1) * 24], gateT1[0:24, i * P:(i + 1) * P], ident[0:24, 0:24])
            last.then_inc(gate_mm, 1)
            for n in range(6):
                head_spread(n)
            pe.wait_ge(cmp_in, 64)
            hidden(0)
            for n in range(1, len(ROPED)):
                turned(n)
            pe.wait_ge(g_ready, 3)
            hidden(1)
            for n in range(6, len(NORMED)):
                head_spread(n)
            pe.wait_ge(hid_ready, 4)
            for e in range(2):
                for kt in range(2):
                    last = mm(ps[e * HD:(e + 1) * HD, 6, 256:320], w2[:, 0, kt, :],
                              hid[:, 0, kt, :, :].rearrange("p g n -> p (g n)"), start=(kt == 0), stop=(kt == 1))
            last.then_inc(cmp_mm, 1)
            for g in range(NKV):
                for kt in range(2):
                    last = mm(ps[0:32, 6, 320 + 64 * g:384 + 64 * g], hid[:, 1, kt, g, :], w2[:, 1, kt, :], start=(kt == 0), stop=(kt == 1))
                last.then_inc(cmp_mm, 1)
            pe.wait_ge(cmp_sq, 2)
            mm(ps[:, 6, 448:512], headones[:], kcsq[:], start=True, stop=True).then_inc(cmp_mm, 1)
            for n, t in enumerate((U_VS, U_VW, U_VF, U_VF + 1, U_VF + 2, U_VF + 3)):
                if n >= 2:
                    pe.wait_ge(v_ready, n - 1)
                for i in range(TT):
                    last = nc.tensor.transpose(ps[:, 2 + n % 2, i * P:(i + 1) * P], uT[:, t, i * P:(i + 1) * P], ident[:])
                last.then_inc(vtr, 1)
            pe.wait_ge(v_ready, 6)
            pe.wait_ge(k_lo, 9)
            pe.wait_ge(fl_v, 7)

            def attention(n0, steps, fox):
                NS = len(steps)
                with pe.Fori(0, 2) as it:
                    s0 = n0 + NS * it
                    if fox:
                        pe.wait_ge(c_staged, 4 * it + 4)
                    for s in range(NS + LAG_V):
                        if s < NS:
                            hh, i, b = steps[s]
                            e, out_ = hh % 2, ps[:, s % 3, 0:(i + 1) * P]
                            n = (i + 1) * P
                            if s == 0 or steps[s - 1][0] != hh:
                                pe.wait_ge(q_lo, (NH if fox else 0) + 4 * it + hh + 1)
                                if fox:
                                    pe.wait_ge(k_lo, 9 + 2 * (4 * it + hh + 1))
                            if s >= 3:
                                pe.wait_ge(exp_done, s0 + s - 2)
                            if b == 2:
                                out_ = ps[:, s % 3, 0:32]
                                mm(out_, ident_b[:], cmpneg[:, i, :], start=True, stop=False, skip_group_check=True)
                                keys = [kch[:, x, bass.ds(32 * it, 32)] for x in range(2)]
                            else:
                                mm(ps[:, s % 3, n - P:n], ident_b[:], causal[:], start=True, stop=False, skip_group_check=True)
                                keys = [kfox[:, e, x, 0:n] if fox else ksel[:, bass.ds(it, 1), b, x, 0:n].rearrange("p a s -> p (a s)") for x in range(2)]
                            if fox:
                                mm(out_, negsel[:, hh, :], csplit[:, 0:n], start=False, stop=False, skip_group_check=True)
                            for x in range(2):
                                last = mm(out_, qs[:, e, i * P:(i + 1) * P], keys[x], start=False, stop=(x == 1), skip_group_check=True)
                            last.then_inc(score_done, 1)
                        if LAG_T <= s < NS + LAG_T:
                            q_ = s - LAG_T
                            hh, i, b = steps[q_]
                            pe.wait_ge(exp_done, s0 + q_ + 1)
                            if q_ >= 3:
                                pe.wait_ge(ptev_done, s0 + q_ - 2)
                            if b == 2:
                                last = nc.tensor.transpose(ps[0:32, 3 + q_ % 3, 0:P], prob[:, q_ % 3, 0:32], ident[:])
                            else:
                                for k in range(i + 1):
                                    last = nc.tensor.transpose(ps[:, 3 + q_ % 3, k * P:(k + 1) * P], prob[:, q_ % 3, k * P:(k + 1) * P], ident[:])
                            last.then_inc(trans_done, 1)
                        if s >= LAG_V:
                            q_ = s - LAG_V
                            hh, i, b = steps[q_]
                            pe.wait_ge(ptev_done, s0 + q_ + 1)
                            if q_ >= 2:
                                pe.wait_ge(o_done, s0 + q_ - 1)
                            o = ps[:, 6 + q_ % 2, 0:2 * HD]
                            if q_ == 2 and not fox:
                                pe.wait_ge(vc_staged, it + 1)
                            if b == 2:
                                last = mm(o[:, 0:HD], probT[0:32, q_ % 3, 0, :], vcst[:], start=True, stop=True)
                            else:
                                for k in range(i + 1):
                                    v = bass.ds(2 * P + 4 * HD * it + 2 * HD * (hh // 2), 2 * HD) if fox else bass.ds(b * P + HD * it, 2 * HD)
                                    last = mm(o, probT[:, q_ % 3, k, :], vtok[:, k, v], start=(k == 0), stop=(k == i))
                            last.then_inc(pv_done, 1)

            attention(0, NSA_STEPS, False)
            attention(2 * len(NSA_STEPS), FOX_STEPS, True)
            pe.wait_ge(oscaled, 2 * TT)
            for n in range(KD):
                if n >= 4:
                    pe.wait_ge(normed, 2 * KD + n - 3)
                for i in range(TT):
                    last = nc.tensor.transpose(ps[:, 4 + n % 4, i * P:(i + 1) * P], otok[:, i, n * P:(n + 1) * P], ident[:])
                last.then_inc(otr, 1)
            square(W_OUT1, 2, h_ready, 2 * KD)
            norm_stats(2, True)
            ffn_up(1, 3, W_UP2)
            ffn_down(1, W_DN2)
            pe.wait_ge(p_in, 16)
            for e in range(2):
                pe.wait_ge(h_ready, 3 * KD + e + 1)
                for i in range(TT):
                    last = nc.tensor.transpose(ps[:, 5 + e, i * P:(i + 1) * P], p_tok[:, i, e * P:(e + 1) * P], ident[:])
                last.then_inc(pT_done, 1)
            pe.wait_ge(lo_ready, W_PLP + 1)
            pe.wait_ge(pl_ready, 2)
            wh, wl = w_view(whi, W_PLP % 2, 2), w_view(wlo, W_PLP % 2, 2)
            for n in range(KD):
                if n == 6:
                    norm_sums(3, True)
                if n < 6:
                    pe.wait_ge(h_ready, 3 * KD + n + 3)
                else:
                    pe.wait_ge(e_ready, n - 5)
                for k in range(2):
                    for q, (w, x) in enumerate(((wh, p_h), (wl, p_h), (wh, p_l))):
                        last = mm(ps[:, E_BANK[n], :], w[:, k, n * P:(n + 1) * P], x[:, k, :], start=(k == 0 and q == 0), stop=(k == 1 and q == 2))
                last.then_inc(tiles_done, 1)
            norm_spread(3, True)
            pair(W_PLG, W_PLG % 2, lambda j: pe.wait_ge(e_ready, KD), 4)
            norm_sums(4, True)
            pair(W_PLG + 2, W_PLG % 2, lambda j: pe.wait_ge(gate_ready, j + 1), between=lambda: norm_spread(4, True))
            norm_stats(5, False)
            s = W_IN2 % 2
            for n in range(4):
                need = (2, 4, 2, 4) if n == 2 else (1, 2, 3, 4)

                def step(i, ready):
                    pair(W_IN2 + 8 * n + 2 * i, s, lambda j: pe.wait_ge(p2_free, P2 + 16 * n + 4 * i - 4 + need[j]), ready, 2, (BOTH, BOTH))

                if n == 0:
                    step(0, 5)
                with pe.Fori(1 if n == 0 else 0, 4) as i:
                    if n:
                        pe.wait_ge(p2_free, P2 + 16 * n)
                    step(i, None)
            pe.wait_ge(p2_free, P2 + 64)
            for u in range(4):
                pe.wait_ge(lo_ready, W_IN2 + 32 + u + 1)
                if u >= 2:
                    pe.wait_ge(vev, u - 1)
                slot = (s + u) % 2
                wh, wl = w_view(whi, slot, KD), w_view(wlo, slot, KD)
                for g in range(TT + 1):
                    c0 = 0 if g == 0 else M + (g - 1) * P
                    for k in range(KD):
                        for q, (w, x) in enumerate(((wh, xh), (wl, xh), (wh, xl))):
                            last = mm(ps[:, 3 * (u % 2) + g // 2, g % 2 * UC:(g % 2 + 1) * UC], x[:, k, c0:c0 + P], w[:, k, :],
                                      start=(k == 0 and q == 0), stop=(k == KD - 1 and q == 2))
                last.then_inc(tiles_done, 2)
            pe.wait_ge(vev, 4)
            last_user = {}
            for idx, (lv, n, bank) in enumerate(LEVEL_SEQ):
                pe.wait_ge(lev_up, 1 if lv < 0 else LEVEL_UP[lv - 1, META if n == META else n // HG])
                if lv > 0 and n != META:
                    pe.wait_ge(lev_k, 2 * (lv - 1) + n // HG + 1)
                if bank in last_user:
                    was, at_lv = last_user[bank]
                    if at_lv < 7:
                        pe.wait_ge(lev_sel, was + 1)
                    else:
                        pe.wait_ge(lev_cp, was + 1 - LEVEL_CP0)
                last_user[bank] = (idx, lv)
                xc = lambda i, k=1: slice(M + i * P, M + (i + k) * P)
                if n == META:
                    for m in range(VH):
                        last = mm(ps[0:M, bank, m * M:(m + 1) * M], K[:, m, 0:M], Q[:, m, 0:M], start=True, stop=True)
                elif lv < 7:
                    for i in range(TT):
                        last = mm(ps[:, bank, i * P:(i + 1) * P], K[:, n, xc(i)], Q[:, n, xc(i)], start=True, stop=True)
                elif lv == 7:
                    for i in range(2):
                        last = mm(ps[:, bank, i * P:(i + 1) * P], K[:, n, xc(2 * i)], Q[:, n, xc(2 * i + 1)], start=True, stop=True)
                else:
                    for i in range(2):
                        last = mm(ps[:, bank, i * 2 * P:(i + 1) * 2 * P], K[:, n, xc(i)], Q[:, n, xc(2, 2)], start=True, stop=True)
                last.then_inc(lev_mm, 1)
            pe.wait_ge(lev_up, LEVEL_UP[LEVELS - 1, META])
            pe.wait_ge(lev_cp, 2 * VH)
            pe.wait_ge(lev_sel, LEVEL_CP0)
            def meta_scores(n):
                if n >= 2:
                    pe.wait_ge(amx_cp, n - 1)
                mm(ps[0:M, n % 2, :], K[:, n, 0:M], Q[:, n, M:T], start=True, stop=True).then_inc(amx_mm, 1)

            def head_sums(n):
                pe.wait_ge(hsq, n + 1)
                for i in range(TT + 1):
                    c0 = 0 if i == 0 else M + (i - 1) * P
                    last = mm(ps[:, 6, n * 5 + i:n * 5 + i + 1], K[:, n, c0:c0 + P], ones1[:], start=True, stop=True)
                last.then_inc(hssq, 1)

            meta_scores(0)
            for n in range(VH):
                f = slice(n * P, (n + 1) * P)
                if n + 1 < VH:
                    meta_scores(n + 1)
                if n >= 2:
                    pe.wait_ge(o2_cp, 2 * (n - 1))
                o = ps[:, 2 + n % 2, :]
                for i in range(TT):
                    mm(o[:, i * P:(i + 1) * P], V[:, 1 + i, f], Ad[:, n, i * P:(i + 1) * P], start=(i == 0), stop=False, skip_group_check=True)
                for i in range(2):
                    mm(o[:, (2 * i + 1) * P:(2 * i + 2) * P], V[:, 1 + 2 * i, f], Tod[:, 64 + n * 256 + i * P:64 + n * 256 + (i + 1) * P],
                       start=False, stop=False, skip_group_check=True)
                for i in range(2):
                    mm(o[:, 2 * P:4 * P], V[:, 1 + i, f], Tev[:, 128 + n * 512 + i * 256:128 + n * 512 + (i + 1) * 256],
                       start=False, stop=False, skip_group_check=True)
                pe.wait_ge(amx_cp, n + 1)
                mm(o, V[0:M, 0, f], Amx[:, n % 2, :], start=False, stop=True, skip_group_check=True)
                mm(ps[:, 4 + n % 2, 0:M], V[0:M, 0, f], Am[:, n, :], start=True, stop=True).then_inc(o2_mm, 1)
                if n:
                    head_sums(n - 1)
            head_sums(VH - 1)
            pe.wait_ge(hrstd, 1)
            for n in range(VH):
                if n >= 2:
                    pe.wait_ge(h2_step, 2 * (n - 2) + 1)
                spread(lambda i: rstd[:, n * 5 + i:n * 5 + i + 1], False, 6 if n % 2 == 0 else 2).then_inc(hrb, 1)
            pe.wait_ge(h2_step, 2 * VH)
            square(W_OUT2, 6, h_ready, 5 * KD, 2, (BOTH, BOTH))
            norm_stats(6, False)
            ffn_up(2, 7, W_UP3, conv=True)
            ffn_down(2, W_DN3)
            for i in range(TT):
                for e in range(2):
                    n = 2 * i + e
                    pe.wait_ge(h_ready, 7 * KD)
                    for c in range(4):
                        last = nc.tensor.transpose(ps[:, n, c * P:(c + 1) * P], h[:, 4 * e + c, M + i * P:M + (i + 1) * P], ident[:])
                    last.then_inc(fT, 1)


_IN = ["x", "p", "ffn1_norm", "ffn1_wg", "ffn1_wu", "ffn1_wd", "mix_norm", "w_in", "b_forget", "q_norm_nsa",
       "k_norm_cmp", "k_norm_slc", "k_norm_win", "cmp_pos_k", "cmp_pos_v", "cmp_k_w1", "cmp_k_w2", "cmp_v_w1",
       "cmp_v_w2", "q_norm_fox", "k_norm_fox", "out_norm_nsa", "out_norm_fox", "w_out", "ffn2_norm", "ffn2_wg",
       "ffn2_wu", "ffn2_wd", "ple_gate_norm", "ple_w_gate", "ple_w_proj", "ple_norm", "meta_tokens_2",
       "lb_param_2", "attn_norm_w_2", "w_in_2", "hgrn_norm_w_2", "conv_w_2", "w_out_2", "ffn_norm_w_2", "w_up_2",
       "ffn_conv_w_2", "ffn_conv_b_2", "w_down_2", "final_norm_w_2"]


def constants():
    import numpy as np
    f = np.float32
    r = np.arange(P)
    out = {"k_ident": np.eye(P, dtype=f)}
    out["k_causal"] = np.where(r[None, :] > r[:, None], f(NEG), f(0))
    out["k_headones"] = (r[:, None] // HD == r[None, :] // HD).astype(f)
    rot_dim = HD // 4
    half = rot_dim // 2
    turn = np.zeros((P, P), f)
    cos, sin = np.ones((P, S), f), np.zeros((P, S), f)
    inv = (500000.0 ** (-np.arange(0, rot_dim, 2, dtype=np.float64) / rot_dim)).astype(f)
    ang = (np.arange(S, dtype=f)[None, :] * inv[:, None]).astype(f)
    for b in range(0, P, HD):
        for j in range(half):
            turn[b + half + j, b + j] = -1.0
            turn[b + j, b + half + j] = 1.0
            for d in (j, half + j):
                cos[b + d], sin[b + d] = np.cos(ang[j]), np.sin(ang[j])
    out["k_rot"], out["k_cos"], out["k_sin"] = turn, cos, sin
    t = np.arange(S).reshape(TT, P).T
    n = np.arange(32)
    seen = (n[None, None, :] < NC) & (CS * n[None, None, :] + CB - 1 <= t[:, :, None])
    out["k_cmpneg"] = np.where(seen, f(0), f(NEG)).astype(f)
    out["k_cmprow"] = (t >= CB - 1).astype(f)
    out["k_headsel"] = np.concatenate([np.eye(NH, dtype=f), np.zeros((FL0 - NH, NH), f), np.eye(NH, dtype=f)])
    lev = np.zeros((P, 8, P), f)
    lev[:, 0] = np.eye(P, dtype=f)
    for l in range(7):
        w = 1 << l
        same = r[:, None] // (2 * w) == r[None, :] // (2 * w)
        lev[:, l + 1] = same & (r[:, None] // w % 2 == 0) & (r[None, :] // w % 2 == 1)
    out["k_levels"] = lev
    return out


def kernel(**inputs):
    import numpy as np
    import concourse.bacc as bacc
    from concourse.bass_utils import run_bass_kernel_spmd as run

    nc = bacc.Bacc("TRN2", target_bir_lowering=False, num_devices=1)
    arrays, a = {}, {}
    for name, v in [(n, inputs[n]) for n in _IN] + list(constants().items()):
        v = np.ascontiguousarray(v)
        arrays["in_" + name] = v
        a[name] = nc.dram_tensor("in_" + name, v.shape, mybir.dt.from_np(v.dtype), kind="ExternalInput").ap()
    out = nc.dram_tensor("out", (1, S, D), F32, kind="ExternalOutput").ap()
    build(nc, a, out)
    return run(nc, [arrays], core_ids=[0]).results[0]["out"]
```
